# Optimizing a Trainium2 kernel written in Bass

```python
import math
import jax
import jax.numpy as jnp
from jax import lax
import numpy as np

D_MODEL = 1024
BATCH = 1
SEQ = 256
DEPTH = 1

SSD_HEADS = 8
SSD_HEAD_DIM = 64
SSD_INNER = SSD_HEADS * SSD_HEAD_DIM
SSD_GROUPS = 2
SSD_STATE = 64
SSD_CONV = 4
SSD_CHUNK = 128
CONV_CH = SSD_INNER + 2 * SSD_GROUPS * SSD_STATE
ATT_HEADS = 8
ATT_HEAD_DIM = 64
ATT_INNER = ATT_HEADS * ATT_HEAD_DIM
MOBA_BLOCK = 256
MOBA_TOPK = 3
MOBA_Q_CHUNK = 16
REL_BUCKETS = 32
REL_MAX_DIST = 128
MIX_WIDTH = SSD_INNER + ATT_INNER
IN_COLS = SSD_INNER + CONV_CH + SSD_HEADS + 3 * ATT_INNER
MOE_GROUPS = 4
MOE_EXPERTS_PER_GROUP = 8
MOE_EXPERTS = MOE_GROUPS * MOE_EXPERTS_PER_GROUP
MOE_TOPK = 2
MOE_HIDDEN = 512
MOE_BLOCK_ROWS = 128
EPS = 1e-6

kernel_name = "hymba_ssd_moba_hiermoe"

def rmsnorm(x, g):
    xf = x.astype(jnp.float32)
    y = xf * lax.rsqrt(jnp.mean(xf * xf, axis=-1, keepdims=True) + EPS)
    return (y * g.astype(jnp.float32)).astype(x.dtype)

def t5_bucket(dist):
    dist = jnp.maximum(dist, 0)
    max_exact = REL_BUCKETS // 2
    d = jnp.maximum(dist, max_exact).astype(jnp.float32)
    large = max_exact + (jnp.log(d / max_exact) / math.log(REL_MAX_DIST / max_exact)
                         * (REL_BUCKETS - max_exact)).astype(jnp.int32)
    large = jnp.minimum(large, REL_BUCKETS - 1)
    return jnp.where(dist < max_exact, dist, large)

def causal_dwconv(u, w, b):
    out = lax.conv_general_dilated(
        u, w[:, None, :].astype(u.dtype), window_strides=(1,),
        padding=[(SSD_CONV - 1, 0)], dimension_numbers=('NWC', 'WIO', 'NWC'),
        feature_group_count=u.shape[-1])
    return out + b.astype(u.dtype)

def ssd_mixer(z, xbc, dt_raw, conv_w, conv_b, dt_bias, a_log, d_skip, norm_g):
    f32 = jnp.float32
    bsz, seq, _ = z.shape
    G, E, P, N, L = SSD_GROUPS, SSD_HEADS // SSD_GROUPS, SSD_HEAD_DIM, SSD_STATE, SSD_CHUNK
    nc = seq // L
    xbc = jax.nn.silu(causal_dwconv(xbc, conv_w, conv_b)).astype(f32)
    xs = xbc[..., :SSD_INNER].reshape(bsz, seq, SSD_HEADS, P)
    b_in = xbc[..., SSD_INNER:SSD_INNER + G * N].reshape(bsz, nc, L, G, N)
    c_out = xbc[..., SSD_INNER + G * N:].reshape(bsz, nc, L, G, N)
    dt = jax.nn.softplus(dt_raw.astype(f32) + dt_bias.astype(f32))
    a_dt = dt * (-jnp.exp(a_log.astype(f32)))
    xdt = (xs * dt[..., None]).reshape(bsz, nc, L, G, E, P)
    a_cs = jnp.cumsum(a_dt.reshape(bsz, nc, L, G, E).transpose(0, 3, 4, 1, 2), axis=-1)
    causal = jnp.tril(jnp.ones((L, L), dtype=bool))
    l_mat = jnp.exp(jnp.where(causal, a_cs[..., :, None] - a_cs[..., None, :], -jnp.inf))
    cb = jnp.einsum('bclgn,bcsgn->bcgls', c_out, b_in)
    y_diag = jnp.einsum('bcgls,bgecls,bcsgep->bclgep', cb, l_mat, xdt)
    decay_states = jnp.exp(a_cs[..., -1:] - a_cs)
    states = jnp.einsum('bclgn,bgecl,bclgep->bcgepn', b_in, decay_states, xdt)
    chunk_decay = jnp.exp(a_cs[..., -1])

    def step(h, inp):
        st, dec = inp
        return h * dec[..., None, None] + st, h

    h0 = jnp.zeros((bsz, G, E, P, N), f32)
    _, h_in = lax.scan(step, h0, (jnp.moveaxis(states, 1, 0), jnp.moveaxis(chunk_decay, -1, 0)))
    h_in = jnp.moveaxis(h_in, 0, 1)
    y_off = jnp.einsum('bclgn,bcgepn,bgecl->bclgep', c_out, h_in, jnp.exp(a_cs))
    y = (y_diag + y_off).reshape(bsz, seq, SSD_HEADS, P) + d_skip.astype(f32)[:, None] * xs
    y = y.reshape(bsz, seq, SSD_INNER) * jax.nn.silu(z.astype(f32))
    return rmsnorm(y, norm_g).astype(z.dtype)

def moba_attention(q, k, v, q_g, k_g, rel_bias):
    f32 = jnp.float32
    bsz, seq, _ = q.shape
    H, hd, BS, QC = ATT_HEADS, ATT_HEAD_DIM, MOBA_BLOCK, MOBA_Q_CHUNK
    q = rmsnorm(q.reshape(bsz, seq, H, hd), q_g).transpose(0, 2, 1, 3)
    k = rmsnorm(k.reshape(bsz, seq, H, hd), k_g).transpose(0, 2, 1, 3)
    v = v.reshape(bsz, seq, H, hd).transpose(0, 2, 1, 3)
    s_pad = -(-seq // BS) * BS
    pad = [(0, 0), (0, 0), (0, s_pad - seq), (0, 0)]
    q, k, v = jnp.pad(q, pad), jnp.pad(k, pad), jnp.pad(v, pad)
    nb = s_pad // BS
    topk = min(MOBA_TOPK, nb)
    kb = k.reshape(bsz, H, nb, BS, hd)
    vb = v.reshape(bsz, H, nb, BS, hd)
    kmean = jnp.mean(kb.astype(f32), axis=3)
    gate = jnp.einsum('bhsd,bhnd->bhsn', q.astype(f32), kmean)
    past = jnp.arange(nb)[None, :] < (jnp.arange(s_pad) // BS)[:, None]
    gate = jnp.where(past, gate, -jnp.inf)
    _, sel = lax.top_k(gate, topk)
    scale = ATT_HEAD_DIM ** -0.5
    bi = jnp.arange(bsz)[:, None, None, None]
    hi = jnp.arange(H)[None, :, None, None]

    def chunk(c):
        q0 = c * QC
        qpos = q0 + jnp.arange(QC)
        qc = lax.dynamic_slice_in_dim(q, q0, QC, axis=2)
        selc = lax.dynamic_slice_in_dim(sel, q0, QC, axis=2)
        ksel = kb[bi, hi, selc]
        vsel = vb[bi, hi, selc]
        kpos = selc[..., None] * BS + jnp.arange(BS)
        dist = qpos[:, None, None] - kpos
        valid = jnp.arange(topk)[None, :] < (qpos // BS)[:, None]
        s_sel = jnp.einsum('bhqd,bhqknd->bhqkn', qc, ksel, preferred_element_type=f32) * scale
        s_sel = s_sel + rel_bias[t5_bucket(dist), hi[..., None]].astype(f32)
        s_sel = jnp.where(valid[:, :, None], s_sel, -jnp.inf)
        ob = q0 // BS
        kown = lax.dynamic_index_in_dim(kb, ob, axis=2, keepdims=False)
        vown = lax.dynamic_index_in_dim(vb, ob, axis=2, keepdims=False)
        dist_own = qpos[:, None] - (ob * BS + jnp.arange(BS))[None, :]
        s_own = jnp.einsum('bhqd,bhkd->bhqk', qc, kown, preferred_element_type=f32) * scale
        s_own = s_own + rel_bias[t5_bucket(dist_own)].transpose(2, 0, 1).astype(f32)
        s_own = jnp.where(dist_own >= 0, s_own, -jnp.inf)
        logits = jnp.concatenate([s_sel.reshape(bsz, H, QC, topk * BS), s_own], axis=-1)
        p = jax.nn.softmax(logits, axis=-1)
        p_sel = p[..., :topk * BS].reshape(bsz, H, QC, topk, BS).astype(v.dtype)
        p_own = p[..., topk * BS:].astype(v.dtype)
        return (jnp.einsum('bhqkn,bhqknd->bhqd', p_sel, vsel)
                + jnp.einsum('bhqk,bhkd->bhqd', p_own, vown))

    out = lax.map(chunk, jnp.arange(s_pad // QC))
    out = out.transpose(1, 2, 0, 3, 4).reshape(bsz, H, s_pad, hd)[:, :, :seq]
    return out.transpose(0, 2, 1, 3).reshape(bsz, seq, ATT_INNER)

def hier_moe(xn, w_r1, b_r1, w_r2, b_r2, w_gate, w_up, w_down):
    f32 = jnp.float32
    bsz, seq, d = xn.shape
    T = bsz * seq
    xt = xn.reshape(T, d)
    p1 = jax.nn.softmax(jnp.matmul(xt, w_r1).astype(f32) + b_r1.astype(f32), axis=-1)
    gval, gidx = lax.top_k(p1, 1)
    lg2 = (jnp.matmul(xt, w_r2).astype(f32) + b_r2.astype(f32)).reshape(T, MOE_GROUPS, MOE_EXPERTS_PER_GROUP)
    lg2 = jnp.take_along_axis(lg2, gidx[:, :, None], axis=1)[:, 0]
    ev, eidx = lax.top_k(jax.nn.softmax(lg2, axis=-1), MOE_TOPK)
    gates = gval * (ev / jnp.sum(ev, axis=-1, keepdims=True))
    experts = gidx * MOE_EXPERTS_PER_GROUP + eidx
    M = MOE_BLOCK_ROWS
    A = T * MOE_TOPK
    flat_e = experts.reshape(-1)
    flat_tok = jnp.arange(A) // MOE_TOPK
    flat_gate = gates.reshape(-1)
    order = jnp.argsort(flat_e)
    se, st, sg = flat_e[order], flat_tok[order], flat_gate[order]
    counts = jnp.bincount(flat_e, length=MOE_EXPERTS)
    starts = jnp.cumsum(counts) - counts
    padded = (counts + M - 1) // M * M
    ends = jnp.cumsum(padded)
    pstarts = ends - padded
    dest = pstarts[se] + jnp.arange(A) - starts[se]
    n_blk = -(-A // M) + MOE_EXPERTS
    P = n_blk * M
    slot_tok = jnp.full((P,), T, jnp.int32).at[dest].set(st)
    slot_gate = jnp.zeros((P,), f32).at[dest].set(sg)
    blk_exp = jnp.minimum(jnp.searchsorted(ends, jnp.arange(n_blk) * M, side='right'), MOE_EXPERTS - 1)
    xpad = jnp.concatenate([xt, jnp.zeros((1, d), xt.dtype)], axis=0)
    xb = xpad[slot_tok].reshape(n_blk, M, d)

    def expert_block(args):
        xblk, e = args
        hmid = jax.nn.silu(xblk @ w_gate[e]) * (xblk @ w_up[e])
        return hmid @ w_down[e]

    yb = lax.map(expert_block, (xb, blk_exp)).reshape(P, d)
    out = jnp.zeros((T + 1, d), f32).at[slot_tok].add(yb.astype(f32) * slot_gate[:, None])[:T]
    return out.reshape(bsz, seq, d).astype(xn.dtype)

def setup_inputs(seed: int = 0) -> dict:
    key = jax.random.key(seed)
    ks = jax.random.split(key, 24)
    nrm = jax.random.normal
    D = D_MODEL
    dt = jnp.exp(jax.random.uniform(ks[6], (DEPTH, SSD_HEADS)) * (math.log(0.1) - math.log(0.001)) + math.log(0.001))
    return {
        "x": nrm(ks[0], (BATCH, SEQ, D), jnp.float32),
        "rel_bias": 0.5 * nrm(ks[1], (REL_BUCKETS, ATT_HEADS), jnp.float32),
        "norm1_g": 1.0 + 0.01 * nrm(ks[2], (DEPTH, D), jnp.float32),
        "w_in": nrm(ks[3], (DEPTH, D, IN_COLS), jnp.float32) * D ** -0.5,
        "conv_w": nrm(ks[4], (DEPTH, SSD_CONV, CONV_CH), jnp.float32) * SSD_CONV ** -0.5,
        "conv_b": 0.01 * nrm(ks[5], (DEPTH, CONV_CH), jnp.float32),
        "dt_bias": dt + jnp.log(-jnp.expm1(-dt)),
        "a_log": jnp.log(jax.random.uniform(ks[7], (DEPTH, SSD_HEADS), minval=1.0, maxval=16.0)),
        "d_skip": 1.0 + 0.01 * nrm(ks[8], (DEPTH, SSD_HEADS), jnp.float32),
        "ssd_norm_g": 1.0 + 0.01 * nrm(ks[9], (DEPTH, SSD_INNER), jnp.float32),
        "q_norm_g": 1.0 + 0.01 * nrm(ks[10], (DEPTH, ATT_HEAD_DIM), jnp.float32),
        "k_norm_g": 1.0 + 0.01 * nrm(ks[11], (DEPTH, ATT_HEAD_DIM), jnp.float32),
        "w_out": nrm(ks[12], (DEPTH, MIX_WIDTH, D), jnp.float32) * MIX_WIDTH ** -0.5,
        "norm2_g": 1.0 + 0.01 * nrm(ks[13], (DEPTH, D), jnp.float32),
        "w_r1": nrm(ks[14], (DEPTH, D, MOE_GROUPS), jnp.float32) * D ** -0.5,
        "b_r1": 0.01 * nrm(ks[15], (DEPTH, MOE_GROUPS), jnp.float32),
        "w_r2": nrm(ks[16], (DEPTH, D, MOE_EXPERTS), jnp.float32) * D ** -0.5,
        "b_r2": 0.01 * nrm(ks[17], (DEPTH, MOE_EXPERTS), jnp.float32),
        "w_gate": nrm(ks[18], (DEPTH, MOE_EXPERTS, D, MOE_HIDDEN), jnp.float32) * D ** -0.5,
        "w_up": nrm(ks[19], (DEPTH, MOE_EXPERTS, D, MOE_HIDDEN), jnp.float32) * D ** -0.5,
        "w_down": nrm(ks[20], (DEPTH, MOE_EXPERTS, MOE_HIDDEN, D), jnp.float32) * MOE_HIDDEN ** -0.5,
    }

def reference(x, rel_bias, norm1_g, w_in, conv_w, conv_b, dt_bias, a_log, d_skip, ssd_norm_g,
              q_norm_g, k_norm_g, w_out, norm2_g, w_r1, b_r1, w_r2, b_r2, w_gate, w_up, w_down):
    cuts = [SSD_INNER, SSD_INNER + CONV_CH, SSD_INNER + CONV_CH + SSD_HEADS,
            SSD_INNER + CONV_CH + SSD_HEADS + ATT_INNER,
            SSD_INNER + CONV_CH + SSD_HEADS + 2 * ATT_INNER]
    h = x
    for l in range(DEPTH):
        u = jnp.matmul(rmsnorm(h, norm1_g[l]), w_in[l])
        z, xbc, dt_raw, q, k, v = jnp.split(u, cuts, axis=-1)
        y_ssd = ssd_mixer(z, xbc, dt_raw, conv_w[l], conv_b[l], dt_bias[l], a_log[l],
                          d_skip[l], ssd_norm_g[l])
        y_att = moba_attention(q, k, v, q_norm_g[l], k_norm_g[l], rel_bias)
        h = h + jnp.matmul(jnp.concatenate([y_ssd, y_att], axis=-1), w_out[l])
        h = h + hier_moe(rmsnorm(h, norm2_g[l]), w_r1[l], b_r1[l], w_r2[l], b_r2[l],
                         w_gate[l], w_up[l], w_down[l])
    return h


_drawn_inputs = setup_inputs


def setup_inputs(seed=0):
    import zlib

    import numpy as np

    out = dict(_drawn_inputs(seed))
    spreads = {}
    factors = {'norm1_g': 2.684,
     'conv_b': 3.977,
     'd_skip': 72.305,
     'ssd_norm_g': 3.347,
     'q_norm_g': 8.0,
     'k_norm_g': 8.0,
     'norm2_g': 2.669,
     'b_r1': 64.0,
     'b_r2': 4.449}
    for name, (base, spread) in spreads.items():
        noise = np.random.default_rng([zlib.crc32(name.encode()), seed]).standard_normal(out[name].shape)
        drawn = base * np.exp(spread * noise) if base else spread * noise
        out[name] = jnp.asarray(drawn.astype(out[name].dtype))
    for name, factor in factors.items():
        out[name] = (out[name] * factor).astype(out[name].dtype)
    return out
```

```python
from contextlib import ExitStack

import numpy as np

import concourse.bass as bass
from concourse import mybir

F32 = mybir.dt.float32
I32 = mybir.dt.int32
ALU = mybir.AluOpType
ACT = mybir.ActivationFunctionType
AX = mybir.AxisListType

P = 128
SEQ = 256
TILES = SEQ // P
D = 1024
DC = D // P
HEADS = 8
HD = 64
INNER = HEADS * HD
GROUPS = 2
HPG = HEADS // GROUPS
STATE = 64
TAPS = 4
CONV_CH = INNER + 2 * GROUPS * STATE
CONV_BLOCKS = CONV_CH // P
XS_BLOCKS = INNER // P
B_BLOCK = XS_BLOCKS
C_BLOCK = XS_BLOCKS + 1
IN_COLS = INNER + CONV_CH + HEADS + 3 * INNER
COL_Z = 0
COL_XBC = INNER
COL_Q = INNER + CONV_CH + HEADS
COL_K = COL_Q + INNER
COL_V = COL_K + INNER
XBC_COLS = CONV_CH + HEADS
BUCKETS = 32
MAX_DIST = 128
MOE_GROUPS = 4
PER_GROUP = 8
EXPERTS = MOE_GROUPS * PER_GROUP
ROUTES = MOE_GROUPS + EXPERTS
HID = 512
HC = HID // P
EPS = 1e-6
LOW = -1e30
CAP = 64
ROUNDS = SEQ // CAP
SLOTS = 3
PIECE = DC * HID
HALF = D // 2


def bucket_ranges():
    exact = BUCKETS // 2
    dist = np.arange(SEQ)
    far = exact + (np.log(np.maximum(dist, exact) / exact) / np.log(MAX_DIST / exact)
                   * (BUCKETS - exact)).astype(np.int64)
    bucket = np.where(dist < exact, dist, np.minimum(far, BUCKETS - 1))
    return [(b, int(np.flatnonzero(bucket == b)[0]), int(np.flatnonzero(bucket == b)[-1]))
            for b in range(BUCKETS) if (bucket == b).any()]


def hymba_layer(nc, x, rel_bias, norm1_g, w_in, conv_w, conv_b, dt_bias, a_log, d_skip, ssd_norm_g,
                q_norm_g, k_norm_g, w_out, norm2_g, w_r1, b_r1, w_r2, b_r2, w_gate, w_up, w_down,
                bias_rows, out):
    x_rows = x.rearrange("b (t p) d -> p (b t) d", p=P)
    out_rows = out.rearrange("b (t p) d -> p (b t) d", p=P)
    win_rows = w_in.rearrange("l (p c) n -> p (l c) n", c=DC)
    wout_rows = w_out.rearrange("l (c p) n -> p (l c) n", p=P)
    gate_rows = w_gate.rearrange("l e (p c) n -> (l e) p c n", c=DC)
    up_rows = w_up.rearrange("l e (p c) n -> (l e) p c n", c=DC)
    down_rows = w_down.rearrange("l e (c p) n -> (l e) p c n", p=P)

    ctx = ExitStack()
    with ctx:
        def sb(name, shape, dt=F32):
            return ctx.enter_context(nc.sbuf_tensor(name, shape, dt))

        def sem(name):
            return ctx.enter_context(nc.semaphore(name))

        ring = sb("ring", [P, SLOTS * 3 * PIECE])

        def piece(i, n=1):
            return ring[:, i * PIECE:(i + n) * PIECE]

        wg_sb = [piece(3 * s).rearrange("p (c n) -> p c n", c=DC) for s in range(SLOTS)]
        wu_sb = [piece(3 * s + 1).rearrange("p (c n) -> p c n", c=DC) for s in range(SLOTS)]
        wd_sb = [piece(3 * s + 2).rearrange("p (c n) -> p c n", c=HC) for s in range(SLOTS)]
        wxbc_sb = ring[:, 0:DC * XBC_COLS].rearrange("p (c n) -> p c n", c=DC)
        wq_sb, wk_sb, wv_sb, wz_sb = [piece(i).rearrange("p (c n) -> p c n", c=DC) for i in (2, 3, 4, 5)]
        wout_sb = piece(6, 2).rearrange("p (c n) -> p c n", c=DC)
        raw_at = DC * XBC_COLS
        RAWW = SEQ + TAPS - 1
        raw = ring[:, raw_at:raw_at + CONV_BLOCKS * RAWW].rearrange("p (b t) -> p b t", b=CONV_BLOCKS)
        assert raw_at + CONV_BLOCKS * RAWW <= 2 * PIECE
        last_piece = piece(8)
        bias_tab = last_piece[:, 0:HEADS * SEQ].rearrange("p (h j) -> p h j", h=HEADS)
        z_silu = last_piece[:, 0:TILES * INNER].rearrange("p (t n) -> p t n", t=TILES)
        xdt = last_piece[:, 2048:3072].rearrange("p (t n) -> p t n", t=TILES)
        y_ssd = last_piece[:, 3072:4096].rearrange("p (t n) -> p t n", t=TILES)

        work = sb("work", [P, 5504])
        xn = work[:, 0:2048].rearrange("p (t c q) -> p t c q", t=TILES, c=DC)
        xe_sb = work[:, 2048:2560].rearrange("p (c k) -> p c k", c=DC)
        silu_sb = work[:, 2560:2816].rearrange("p (m k) -> p m k", m=HC)
        hid_sb = work[:, 2816:3072].rearrange("p (m k) -> p m k", m=HC)
        yt_sb = work[:, 3072:3584].rearrange("p (m k) -> p m k", m=HC)
        y_sb = work[:, 3584:4096]
        sel = work[:, 4096:4224].rearrange("p (t k) -> p t k", t=TILES)
        gsel = work[:, 4224:4480].rearrange("p (t k) -> p t k", t=TILES)
        gselT_sb = work[:, 4480:4736].rearrange("p (t k) -> p t k", t=TILES)
        qk_tok = work[:, 0:2048].rearrange("p (w t n) -> p w t n", w=2, t=TILES)
        decay_mat = work[:, 0:2048].rearrange("p (t h l) -> p t h l", t=TILES, h=HEADS)
        prob = work[:, 2048:3584].rearrange("p (k n) -> p k n", k=4)
        a_bcast = work[:, 2048:3072].rearrange("p (h l) -> p h l", h=HEADS)
        probT = work[:, 3584:4352].rearrange("p (k n) -> p k n", k=2)
        v_tok = work[:, 4352:5376].rearrange("p (t n) -> p t n", t=TILES)

        front = sb("front", [P, 5632])
        xT = front[:, 0:2048].rearrange("p (c t) -> p c t", c=DC)
        y_att = front[:, 0:1024].rearrange("p (t n) -> p t n", t=TILES)
        conv = front[:, 2048:3584].rearrange("p (b t) -> p b t", b=CONV_BLOCKS)
        qkT = front[:, 3584:5632].rearrange("p (w b t) -> p w b t", w=2, b=XS_BLOCKS)
        mixT = front[:, 3584:5632].rearrange("p (c t) -> p c t", c=DC)
        x_scaled = front[:, 3584:5632].rearrange("p (t q c) -> p t c q", t=TILES, c=DC)
        squares = front[:, 3584:5632].rearrange("p (w t n) -> p w t n", w=2, t=TILES)
        xnT = front[:, 0:2048].rearrange("p (c t) -> p c t", c=DC)
        y_off = work[:, 2048:2560]

        h_sb = sb("h", [P, TILES, D])
        ident = sb("ident", [P, P])
        upto = sb("upto", [P, P])
        before = sb("before", [P, P])
        ones = sb("ones", [P, P])
        zeros = sb("zeros", [P, P])
        rank_iota = sb("rank_iota", [P, 2 * CAP])
        expert_iota = sb("expert_iota", [P, EXPERTS])
        minus_half = sb("minus_half", [P, 16])
        g1_col = sb("g1_col", [P, DC])
        qg_col = sb("qg_col", [P, 1])
        kg_col = sb("kg_col", [P, 1])
        qkg_col = sb("qkg_col", [P, 1])
        conv_rows = last_piece[0:TAPS + 1, 3072:3072 + CONV_CH]
        conv_cols = sb("conv_cols", [P, CONV_BLOCKS, TAPS + 1])
        rel_rows = sb("rel_rows", [BUCKETS, HEADS])
        relT = sb("relT", [HEADS, BUCKETS])
        bias_line = last_piece[0:HEADS, 2048:2048 + SEQ + P]
        dtb_bc = sb("dtb_bc", [P, HEADS])
        alog_bc = sb("alog_bc", [P, HEADS])
        dskip_bc = sb("dskip_bc", [P, HEADS])
        ssdg_bc = sb("ssdg_bc", [P, INNER])
        g2_bc = sb("g2_bc", [P, D])
        br_bc = sb("br_bc", [P, ROUTES])
        wr1_sb = sb("wr1_sb", [P, DC, MOE_GROUPS])
        wr2_sb = sb("wr2_sb", [P, DC, EXPERTS])
        wr_sb = sb("wr_sb", [P, DC, ROUTES])
        ms1 = sb("ms1", [P, TILES])
        rs1 = sb("rs1", [P, TILES])
        msqk = sb("msqk", [P, 2, TILES * HEADS])
        rsqk = sb("rsqk", [P, 2, TILES * HEADS])
        dt_lin = sb("dt_lin", [P, TILES, HEADS])
        dt_abs = sb("dt_abs", [P, TILES, HEADS])
        dt_exp = sb("dt_exp", [P, TILES, HEADS])
        dt_log = sb("dt_log", [P, TILES, HEADS])
        dt_sb = sb("dt_sb", [P, TILES, HEADS])
        a_exp = sb("a_exp", [P, HEADS])
        a_dt = sb("a_dt", [P, TILES, HEADS])
        a_cs = sb("a_cs", [P, TILES, HEADS])
        decay_arg = sb("decay_arg", [P, HEADS])
        decay_end = sb("decay_end", [P, HEADS])
        decay_in = sb("decay_in", [P, HEADS])
        cb_sb = sb("cb_sb", [P, TILES, GROUPS, P])
        b_tok = sb("b_tok", [P, P])
        state_sb = sb("state_sb", [P, HPG * HD])
        row_max = sb("row_max", [P, HEADS, TILES])
        neg_max = sb("neg_max", [P, HEADS, TILES])
        row_sum = sb("row_sum", [P, HEADS, TILES])
        row_inv = sb("row_inv", [P, HEADS, TILES])
        ms3 = sb("ms3", [P, TILES])
        rs3 = sb("rs3", [P, TILES])
        ms2 = sb("ms2", [P, TILES])
        rs2 = sb("rs2", [P, TILES])
        logit = sb("logit", [P, TILES, ROUTES])
        top = sb("top", [P, 4, TILES])
        low_at = sb("low_at", [P, TILES])
        gexp = sb("gexp", [P, TILES, MOE_GROUPS])
        gsum = sb("gsum", [P, TILES])
        gval = sb("gval", [P, TILES])
        ghot = sb("ghot", [P, TILES, MOE_GROUPS])
        eq4 = sb("eq4", [P, TILES, MOE_GROUPS])
        eq32 = sb("eq32", [P, TILES, EXPERTS])
        masked = sb("masked", [P, TILES, EXPERTS])
        hot1 = sb("hot1", [P, TILES, EXPERTS])
        hot2 = sb("hot2", [P, TILES, EXPERTS])
        share = sb("share", [P, 4, TILES])
        gates = sb("gates", [P, TILES, EXPERTS])
        chosen = sb("chosen", [P, TILES, EXPERTS])
        rank = sb("rank", [P, TILES, EXPERTS])
        most = sb("most", [1, 1])
        most_int = sb("most_int", [1, 1], I32)

        bank = [ctx.enter_context(nc.psum_tensor(f"bank{i}", [P, 512], F32)) for i in range(8)]

        x_in, small_in, late_in = sem("x_in"), sem("small_in"), sem("late_in")
        wxbc_in, wq_in, wk_in, wv_in, wz_in = [sem(n) for n in ("wxbc_in", "wq_in", "wk_in", "wv_in", "wz_in")]
        wout_in, biasline_out, biastab_in, out_done = [sem(n) for n in ("wout_in", "biasline_out", "biastab_in", "out_done")]
        wg_in = [sem(f"wg_in{s}") for s in range(SLOTS)]
        wu_in = [sem(f"wu_in{s}") for s in range(SLOTS)]
        wd_in = [sem(f"wd_in{s}") for s in range(SLOTS)]
        names = """const_base const_ready zero_ready ms1_ready rs1_ready ms1_act xscaled xT_mm xT_ready small_mm small_ready
            relT_ready line_ready xbc_mm raw_ready dt_mm dtlin_ready q_mm k_mm v_mm z_mm squares_ready msqk_ready rsqk_ready
            qk_ready v_ready conv_ready convsilu dtabs_ready dtlog_ready aexp_ready adt_ready acs_mm acs_ready ab_ready
            rowcs_mm decay_lin decay_exp dend_lin dend_exp xs_mm btok_mm xdt_ready btok_ready cb_mm cb_ready mix_ready
            qkT_mm qT_ready kT_ready qkg_ready score_mm score_ready negmax_ready prob_ready probT_mm probT_ready pv_mm
            zsilu_ready yatt_ready ydiag_mm xdec_ready state_mm state_ready yoff_mm ms3_ready rs3_ready yssd_ready
            mixT_mm mixT_ready wout_mm h_ready ms2_ready ms2_act rs2_ready xn_ready xnT_mm xnT_ready wr_ready logit_mm
            gexp_in gexp_ready share_in share_ready chosen_ready rank_mm most_ready
            sel_ready gsel_ready xe_mm xe_ready gate_mm gu_mm silu_ready hid_ready yt_mm yt_ready yh_mm yh_ready
            st_mm st_ready scat_mm moe_done result_ready dve_step act_step o_rank
            o_turn o_w o_sel o_xe o_xesb o_gu o_silu o_hid o_yt o_ytsb o_yh o_yhsb o_st o_stsb o_scat""".split()
        S = {n: sem(n) for n in names}

        block = ctx.enter_context(nc.Block())

        def bc(ap, shape):
            return ap.to_broadcast(shape)

        def flat(ap):
            return ap

        @block.sync
        def _(sp):
            sp.dma_start(h_sb[:, :, :], x_rows).then_inc(x_in, 16)
            sp.dma_start(wxbc_sb, win_rows[:, :, COL_XBC:COL_XBC + XBC_COLS]).then_inc(wxbc_in, 16)
            sp.dma_start(wq_sb, win_rows[:, :, COL_Q:COL_Q + INNER]).then_inc(wq_in, 16)
            sp.dma_start(wk_sb, win_rows[:, :, COL_K:COL_K + INNER]).then_inc(wk_in, 16)
            sp.dma_start(wv_sb, win_rows[:, :, COL_V:COL_V + INNER]).then_inc(wv_in, 16)
            sp.dma_start(wz_sb, win_rows[:, :, COL_Z:COL_Z + INNER]).then_inc(wz_in, 16)
            sp.dma_start(wout_sb, wout_rows).then_inc(wout_in, 16)

            sp.wait_ge(S["line_ready"], len(bucket_ranges()))
            sp.dma_start(bias_rows.rearrange("p h i -> h p i"), bias_line.unsqueeze(1).to_broadcast([HEADS, P, SEQ + P])
                         ).then_inc(biasline_out, 16)
            sp.wait_ge(biasline_out, 16)
            sp.dma_start(bias_tab, bass.AP(bias_rows.tensor, P - 1,
                                           [[HEADS * (SEQ + P) - 1, P], [SEQ + P, HEADS], [1, SEQ]])
                         ).then_inc(biastab_in, 16)

            sp.wait_ge(S["dt_mm"], 1)
            sp.dma_start(wg_sb[0], gate_rows[0]).then_inc(wg_in[0], 16)
            sp.wait_ge(S["conv_ready"], CONV_BLOCKS)
            sp.dma_start(wu_sb[0], up_rows[0]).then_inc(wu_in[0], 16)
            sp.wait_ge(S["q_mm"], TILES)
            sp.dma_start(wd_sb[0], down_rows[0]).then_inc(wd_in[0], 16)
            sp.wait_ge(S["k_mm"], TILES)
            sp.dma_start(wg_sb[1], gate_rows[1]).then_inc(wg_in[1], 16)
            sp.wait_ge(S["v_mm"], TILES)
            sp.dma_start(wu_sb[1], up_rows[1]).then_inc(wu_in[1], 16)
            sp.wait_ge(S["z_mm"], 1)
            sp.dma_start(wd_sb[1], down_rows[1]).then_inc(wd_in[1], 16)
            sp.wait_ge(S["wout_mm"], TILES * 2)
            sp.dma_start(wg_sb[2], gate_rows[2]).then_inc(wg_in[2], 16)
            sp.dma_start(wu_sb[2], up_rows[2]).then_inc(wu_in[2], 16)
            sp.wait_ge(S["yssd_ready"], TILES)
            sp.dma_start(wd_sb[2], down_rows[2]).then_inc(wd_in[2], 16)

            def refill(e, s):
                sp.wait_ge(S["gate_mm"], e + 1)
                sp.dma_start(wg_sb[s], gate_rows[e + SLOTS]).then_inc(wg_in[s], 16)
                sp.wait_ge(S["gu_mm"], e + 1)
                sp.dma_start(wu_sb[s], up_rows[e + SLOTS]).then_inc(wu_in[s], 16)
                sp.wait_ge(S["yt_mm"], e + 1)
                sp.dma_start(wd_sb[s], down_rows[e + SLOTS]).then_inc(wd_in[s], 16)

            full = (EXPERTS - SLOTS) // SLOTS
            with sp.Fori(0, full) as i:
                for s in range(SLOTS):
                    refill(i * SLOTS + s, s)
            for e in range(full * SLOTS, EXPERTS - SLOTS):
                refill(e, e % SLOTS)

            sp.wait_ge(S["most_ready"], 1)
            most_tokens = sp.value_load(most_int[0:1, 0:1], min_val=0, max_val=SEQ)
            with sp.If(most_tokens > CAP):
                with sp.Fori(0, ROUNDS - 1) as r:
                    with sp.Fori(0, EXPERTS) as e:
                        sp.wait_ge(S["o_turn"], r * EXPERTS + e + 1)
                        sp.dma_start(wg_sb[0], gate_rows[e]).then_inc(S["o_w"], 16)
                        sp.dma_start(wu_sb[0], up_rows[e]).then_inc(S["o_w"], 16)
                        sp.dma_start(wd_sb[0], down_rows[e]).then_inc(S["o_w"], 16)
            sp.nop()

            for t in range(TILES):
                for n in range(2):
                    sp.wait_ge(S["result_ready"], t * 2 + n + 1)
                    sp.dma_start(out_rows[:, t, n * HALF:(n + 1) * HALF],
                                 h_sb[:, t, n * HALF:(n + 1) * HALF]).then_inc(out_done, 16)
            sp.wait_ge(out_done, 16 * TILES * 2)

        @block.gpsimd
        def _(pool):
            pool.memset(ident[:, :], 0.0).then_inc(S["const_base"], 1)
            pool.memset(ones[:, :], 1.0).then_inc(S["const_base"], 1)
            pool.memset(zeros[:, :], 0.0).then_inc(S["const_base"], 1)
            pool.memset(minus_half[:, :], -0.5).then_inc(S["const_base"], 1)
            pool.memset(bias_line[:, :], LOW).then_inc(S["const_base"], 1)
            pool.iota(rank_iota[:, :], [[0, 2], [1, CAP]], base=0, channel_multiplier=0,
                      allow_small_or_imprecise_dtypes=True).then_inc(S["const_base"], 1)
            pool.iota(expert_iota[:, :], [[1, EXPERTS]], base=0, channel_multiplier=0,
                      allow_small_or_imprecise_dtypes=True).then_inc(S["const_base"], 1)
            pool.wait_ge(S["const_base"], 7)
            pool.affine_select(out=ident[:, :], in_=ident[:, :], compare_op=ALU.not_equal, fill=1.0, base=0,
                               pattern=[[-1, P]], channel_multiplier=1).then_inc(S["const_ready"], 1)
            pool.affine_select(out=upto[:, :], in_=ones[:, :], compare_op=ALU.is_ge, fill=0.0, base=0,
                               pattern=[[1, P]], channel_multiplier=-1).then_inc(S["const_ready"], 1)
            pool.affine_select(out=before[:, :], in_=ones[:, :], compare_op=ALU.is_ge, fill=0.0, base=-1,
                               pattern=[[1, P]], channel_multiplier=-1).then_inc(S["const_ready"], 1)

            def rsqrt(dst, src, n, wait, count, done):
                pool.wait_ge(wait, count)
                pool.tensor_tensor(dst, src, minus_half[:, 0:n], ALU.pow).then_inc(done, 1)

            rsqrt(rs1[:, :], ms1[:, :], TILES, S["ms1_ready"], 1, S["rs1_ready"])
            pool.wait_ge(S["relT_ready"], 1)
            for b, near, far in bucket_ranges():
                last = pool.tensor_copy(bias_line[:, SEQ - 1 - far:SEQ - near],
                                        bc(relT[:, b:b + 1], [HEADS, far - near + 1]))
                last.then_inc(S["line_ready"], 1)
            rsqrt(rsqk[:, 0, :], msqk[:, 0, :], TILES * HEADS, S["msqk_ready"], 1, S["rsqk_ready"])
            rsqrt(rsqk[:, 1, :], msqk[:, 1, :], TILES * HEADS, S["msqk_ready"], 2, S["rsqk_ready"])
            for t in range(TILES):
                rsqrt(rs3[:, t:t + 1], ms3[:, t:t + 1], 1, S["ms3_ready"], t + 1, S["rs3_ready"])
            for t in range(TILES):
                rsqrt(rs2[:, t:t + 1], ms2[:, t:t + 1], 1, S["ms2_ready"], t + 1, S["rs2_ready"])

        @block.tensor
        def _(pe):
            conv_ps = bank[4][:, 0:CONV_BLOCKS * 8].rearrange("p (b k) -> p b k", b=CONV_BLOCKS)
            pe.wait_ge(S["const_ready"], 3)
            pe.wait_ge(small_in, 16 * 11)
            for b in range(CONV_BLOCKS):
                pe.transpose(conv_ps[:, b, 0:TAPS + 1], conv_rows[:, b * P:(b + 1) * P], ident[0:TAPS + 1, 0:TAPS + 1])
            pe.transpose(bank[4][0:HEADS, 64:64 + BUCKETS], rel_rows[:, :], ident[0:BUCKETS, 0:BUCKETS]
                         ).then_inc(S["small_mm"], 1)
            for t in range(TILES):
                pe.wait_ge(S["xscaled"], t + 1)
                for c in range(DC):
                    mm = pe.transpose(bank[c // 2][:, (c % 2) * SEQ + t * P:(c % 2) * SEQ + (t + 1) * P],
                                      x_scaled[:, t, c, :], ident[:, :])
            mm.then_inc(S["xT_mm"], 1)

            pe.wait_ge(S["xT_ready"], DC // 2)
            pe.wait_ge(wxbc_in, 16)
            for b in range(CONV_BLOCKS):
                for c in range(DC):
                    mm = pe.matmul(bank[5 + b // 2][:, (b % 2) * SEQ:(b % 2 + 1) * SEQ],
                                   wxbc_sb[:, c, b * P:(b + 1) * P], xT[:, c, :], start=(c == 0), stop=(c == DC - 1))
                if b % 2:
                    mm.then_inc(S["xbc_mm"], 1)
            pe.wait_ge(S["small_ready"], 1)
            for t in range(TILES):
                for c in range(DC):
                    mm = pe.matmul(bank[4][:, t * HEADS:(t + 1) * HEADS], xT[:, c, t * P:(t + 1) * P],
                                   wxbc_sb[:, c, CONV_CH:XBC_COLS], start=(c == 0), stop=(c == DC - 1))
            mm.then_inc(S["dt_mm"], 1)

            def project(dst, w, t, done):
                for c in range(DC):
                    mm = pe.matmul(dst[:, :], xT[:, c, t * P:(t + 1) * P], w[:, c, :], start=(c == 0), stop=(c == DC - 1))
                mm.then_inc(done, 1)

            pe.wait_ge(wq_in, 16)
            for t in range(TILES):
                project(bank[t], wq_sb, t, S["q_mm"])
            pe.wait_ge(wk_in, 16)
            for t in range(TILES):
                project(bank[2 + t], wk_sb, t, S["k_mm"])
            pe.wait_ge(S["adt_ready"], 1)
            pe.matmul(bank[4][:, 0:TILES * HEADS], upto[:, :], a_dt[:, :, :].rearrange("p t h -> p (t h)"),
                      start=True, stop=True).then_inc(S["acs_mm"], 1)
            pe.wait_ge(wv_in, 16)
            for t in range(TILES):
                pe.wait_ge(S["raw_ready"], t + 1)
                project(bank[5 + t], wv_sb, t, S["v_mm"])

            for t in range(TILES):
                if t == 0:
                    pe.wait_ge(S["raw_ready"], 3)
                    pe.wait_ge(S["convsilu"], 3)
                else:
                    pe.wait_ge(S["v_ready"], 1)
                for b in range(XS_BLOCKS):
                    mm = pe.transpose((bank[7] if t == 0 else bank[5])[:, b * P:(b + 1) * P],
                                      conv[:, b, t * P:(t + 1) * P], ident[:, :])
                mm.then_inc(S["xs_mm"], 1)
            pe.wait_ge(S["acs_ready"], 1)
            pe.transpose(bank[4][:, P:2 * P], conv[:, B_BLOCK, 0:P], ident[:, :])
            pe.wait_ge(S["v_ready"], 2)
            for t in range(TILES):
                for g in range(GROUPS):
                    rows = slice(g * STATE, (g + 1) * STATE)
                    mm = pe.matmul(bank[6 - 2 * g][:, (GROUPS + t) * P:(GROUPS + t + 1) * P],
                                   conv[rows, B_BLOCK, t * P:(t + 1) * P], conv[rows, C_BLOCK, t * P:(t + 1) * P],
                                   start=True, stop=True)
            mm.then_inc(S["cb_mm"], 1)
            pe.wait_ge(S["qk_ready"], 2 * TILES)
            for t in range(TILES):
                pe.wait_ge(S["ab_ready"], t + 1)
                for h in range(HEADS):
                    mm = pe.matmul(bank[2 * t + h // 4][:, (h % 4) * P:(h % 4 + 1) * P], a_bcast[:, h, :], upto[:, :],
                                   start=True, stop=True)
                mm.then_inc(S["rowcs_mm"], 1)
            for w in range(2):
                if w == 0:
                    pe.wait_ge(S["btok_ready"], 1)
                    pe.wait_ge(S["cb_ready"], GROUPS)
                    pe.wait_ge(S["xdt_ready"], TILES * 2)
                for b in range(XS_BLOCKS):
                    for t in range(TILES):
                        at = (b % 2) * SEQ + t * P
                        mm = pe.transpose(bank[4 + 2 * w + b // 2][:, at:at + P], qk_tok[:, w, t, b * P:(b + 1) * P],
                                          ident[:, :])
                mm.then_inc(S["qkT_mm"], 1)

            def scores(h):
                b, rows, dst = h // 2, slice((h % 2) * HD, (h % 2 + 1) * HD), bank[4 + h % 2]
                pe.wait_ge(S["qT_ready"], 2)
                pe.wait_ge(S["kT_ready"], 2)
                if h >= 2:
                    pe.wait_ge(S["score_ready"], h - 1)
                pe.matmul(dst[:, 0:SEQ], qkT[rows, 0, b, P:SEQ], qkT[rows, 1, b, :], start=True, stop=True)
                pe.matmul(dst[:, SEQ:SEQ + P], qkT[rows, 0, b, 0:P], qkT[rows, 1, b, 0:P],
                          start=True, stop=True).then_inc(S["score_mm"], 1)

            def turn_probs(h):
                pe.wait_ge(S["prob_ready"], h + 1)
                if h >= 2:
                    pe.wait_ge(S["probT_ready"], h - 1)
                for j in range(3):
                    mm = pe.transpose(bank[6 + h % 2][:, j * P:(j + 1) * P], prob[:, h % 4, j * P:(j + 1) * P], ident[:, :])
                mm.then_inc(S["probT_mm"], 1)

            def weigh_values(h):
                pe.wait_ge(S["probT_ready"], h + 1)
                cols = slice(h * HD, (h + 1) * HD)
                pT = probT[:, h % 2, :]
                pe.matmul(bank[2][:, cols], pT[:, 2 * P:3 * P], v_tok[:, 0, cols], start=True, stop=True)
                pe.matmul(bank[3][:, cols], pT[:, 0:P], v_tok[:, 0, cols], start=True, stop=False)
                pe.matmul(bank[3][:, cols], pT[:, P:2 * P], v_tok[:, 1, cols], start=False, stop=True
                          ).then_inc(S["pv_mm"], 1)

            pe.wait_ge(wz_in, 16)
            pe.wait_ge(S["decay_lin"], TILES * HEADS)
            pe.wait_ge(S["dend_lin"], 1)
            scores(0)
            scores(1)
            for h in range(HEADS):
                for k in (2 * h, 2 * h + 1):
                    t, c = k // DC, k % DC
                    mm = pe.matmul(bank[t][:, :], xT[:, c, t * P:(t + 1) * P], wz_sb[:, c, :],
                                   start=(c == 0), stop=(c == DC - 1))
                if h == HEADS - 1:
                    mm.then_inc(S["z_mm"], 1)
                if h + 2 < HEADS:
                    scores(h + 2)
                turn_probs(h)
                if h >= 1:
                    weigh_values(h - 1)
            weigh_values(HEADS - 1)

            pe.wait_ge(S["mix_ready"], 2 * TILES)
            pe.wait_ge(S["score_ready"], HEADS)
            for t in range(TILES):
                for h in range(HEADS):
                    cols = slice(h * HD, (h + 1) * HD)
                    mm = pe.matmul(bank[4 + t][:, cols], decay_mat[:, t, h, :], xdt[:, t, cols], start=True, stop=True)
                if t == 0:
                    mm.then_inc(S["ydiag_mm"], 1)
                    pe.wait_ge(S["xdec_ready"], 1)
                    pe.wait_ge(S["probT_ready"], HEADS)
                    pe.matmul(bank[6][:, :], b_tok[:, :], xdt[:, 0, :], start=True, stop=True).then_inc(S["state_mm"], 1)
                else:
                    mm.then_inc(S["ydiag_mm"], 1)
            pe.wait_ge(S["state_ready"], GROUPS)
            for g in range(GROUPS):
                rows = slice(g * STATE, (g + 1) * STATE)
                mm = pe.matmul(bank[7 - g][:, g * HPG * HD:(g + 1) * HPG * HD], conv[rows, C_BLOCK, P:SEQ],
                               state_sb[rows, :], start=True, stop=True)
            mm.then_inc(S["yoff_mm"], 1)

            for src, base, dst, ready in ((y_att, XS_BLOCKS, 2, S["yatt_ready"]), (y_ssd, 0, 6, S["yssd_ready"])):
                for t in range(TILES):
                    pe.wait_ge(ready, TILES if base else t + 1)
                    if not base and t == 0:
                        pe.wait_ge(S["state_ready"], GROUPS)
                    for b in range(XS_BLOCKS):
                        mm = pe.transpose(bank[dst + t][:, b * P:(b + 1) * P], src[:, t, b * P:(b + 1) * P], ident[:, :])
                    mm.then_inc(S["mixT_mm"], 1)

            pe.wait_ge(wout_in, 16)
            pe.wait_ge(S["zsilu_ready"], TILES)
            pe.wait_ge(S["mixT_ready"], TILES)
            order = list(range(XS_BLOCKS, DC)) + list(range(XS_BLOCKS))
            for t in range(TILES):
                for k, c in enumerate(order):
                    if k == XS_BLOCKS:
                        pe.wait_ge(S["mixT_ready"], TILES + t + 1)
                    for n in range(2):
                        mm = pe.matmul(bank[(0, 1, 4, 5)[2 * t + n]][:, :], mixT[:, c, t * P:(t + 1) * P],
                                       wout_sb[:, c, n * HALF:(n + 1) * HALF], start=(k == 0), stop=(k == DC - 1))
                        if k == DC - 1:
                            mm.then_inc(S["wout_mm"], 1)
            pe.wait_ge(S["mixT_ready"], 2 * TILES)
            for t in range(TILES):
                pe.wait_ge(S["xn_ready"], t + 1)
                for c in range(DC):
                    at = (c % 2) * SEQ + t * P
                    mm = pe.transpose(bank[(2, 3, 6, 7)[c // 2]][:, at:at + P], xn[:, t, c, :], ident[:, :])
            mm.then_inc(S["xnT_mm"], 1)
            pe.wait_ge(S["wr_ready"], 2)
            pe.wait_ge(S["xnT_ready"], DC // 2)
            pe.wait_ge(S["h_ready"], 2 * TILES)
            for t in range(TILES):
                for c in range(DC):
                    mm = pe.matmul(bank[0][:, t * ROUTES:(t + 1) * ROUTES], xnT[:, c, t * P:(t + 1) * P], wr_sb[:, c, :],
                                   start=(c == 0), stop=(c == DC - 1))
            mm.then_inc(S["logit_mm"], 1)
            pe.wait_ge(S["chosen_ready"], 1)
            pe.matmul(bank[1][:, 0:EXPERTS], before[:, :], chosen[:, 0, :], start=True, stop=True)
            pe.matmul(bank[1][:, EXPERTS:2 * EXPERTS], ones[:, :], chosen[:, 0, :], start=True, stop=False)
            pe.matmul(bank[1][:, EXPERTS:2 * EXPERTS], before[:, :], chosen[:, 1, :], start=False, stop=True)
            pe.matmul(bank[1][:, 2 * EXPERTS:3 * EXPERTS], ones[:, :], chosen[:, 0, :], start=True, stop=False)
            pe.matmul(bank[1][:, 2 * EXPERTS:3 * EXPERTS], ones[:, :], chosen[:, 1, :], start=False, stop=True
                      ).then_inc(S["rank_mm"], 1)
            total = [bank[4 + i] for i in range(4)]
            for i in range(4):
                for j in range(4):
                    pe.matmul(total[i][:, j * P:(j + 1) * P], zeros[0:32, :], zeros[0:32, :],
                              start=(j == 0), stop=False, skip_group_check=True)

            xe_ps = bank[0][:, 0:DC * CAP].rearrange("p (c k) -> p c k", c=DC)
            gate_ps = bank[1][:, 0:HC * CAP].rearrange("p (m k) -> p m k", m=HC)
            up_ps = bank[3][:, 0:HC * CAP].rearrange("p (m k) -> p m k", m=HC)
            yt_ps = bank[2][:, :].rearrange("p (m n k) -> p m n k", m=HC, n=2)

            def gather():
                for c in range(DC):
                    for t in range(TILES):
                        mm = pe.matmul(xe_ps[:, c, :], xn[:, t, c, :], sel[:, t, :], start=(t == 0), stop=(t == TILES - 1))
                return mm

            def hidden(dst, w, blocks):
                for m in blocks:
                    for c in range(DC):
                        mm = pe.matmul(dst[:, m, :], w[:, c, m * P:(m + 1) * P], xe_sb[:, c, :],
                                       start=(c == 0), stop=(c == DC - 1))
                return mm

            def down(w):
                for m in range(DC):
                    for c in range(HC):
                        mm = pe.matmul(yt_ps[:, m % HC, m // HC, :], w[:, c, m * P:(m + 1) * P], hid_sb[:, c, :],
                                       start=(c == 0), stop=(c == HC - 1))
                return mm

            def turn_rows():
                for m in range(HC):
                    mm = pe.transpose(bank[1][:, m * P:(m + 1) * P], yt_sb[:, m, :], ident[:, :])
                return mm

            def turn_selection():
                for t in range(TILES):
                    mm = pe.transpose(bank[3][:, t * P:(t + 1) * P], gsel[:, t, :], ident[:, :])
                return mm

            def scatter():
                for t in range(TILES):
                    for n in range(2):
                        rows = slice(n * CAP, (n + 1) * CAP)
                        mm = pe.matmul(total[2 * t + n][:, :], gselT_sb[rows, t, :], y_sb[rows, :],
                                       start=False, stop=False, skip_group_check=True)
                return mm

            def expert(e, s, turn, first, second, last):
                pe.wait_ge(S["xe_ready"], e + 1)
                pe.wait_ge(wg_in[s], 16 * (turn + 1))
                if not first:
                    pe.wait_ge(S["hid_ready"], e)
                if not first and not second:
                    pe.wait_ge(S["yh_ready"], e - 1)
                hidden(gate_ps, wg_sb[s], range(HC)).then_inc(S["gate_mm"], 1)
                pe.wait_ge(wu_in[s], 16 * (turn + 1))
                if not first and not second:
                    pe.wait_ge(S["st_ready"], e - 1)
                hidden(up_ps, wu_sb[s], range(HC)).then_inc(S["gu_mm"], 1)
                if not first:
                    pe.wait_ge(S["yt_ready"], e)
                    pe.wait_ge(S["silu_ready"], e + 1)
                    turn_rows().then_inc(S["yh_mm"], 1)
                if not last:
                    pe.wait_ge(S["sel_ready"], e + 2)
                    gather().then_inc(S["xe_mm"], 1)
                if not first:
                    pe.wait_ge(S["gsel_ready"], e)
                    pe.wait_ge(S["hid_ready"], e + 1)
                    turn_selection().then_inc(S["st_mm"], 1)
                pe.wait_ge(S["hid_ready"], e + 1)
                pe.wait_ge(wd_in[s], 16 * (turn + 1))
                if not first:
                    pe.wait_ge(S["yt_ready"], e)
                down(wd_sb[s]).then_inc(S["yt_mm"], 1)
                if not first:
                    pe.wait_ge(S["yh_ready"], e)
                    pe.wait_ge(S["st_ready"], e)
                    scatter().then_inc(S["scat_mm"], 1)

            pe.wait_ge(S["most_ready"], 1)
            most_tokens = pe.value_load(most_int[0:1, 0:1], min_val=0, max_val=SEQ)
            pe.wait_ge(S["sel_ready"], 1)
            gather().then_inc(S["xe_mm"], 1)
            for e in range(SLOTS):
                expert(e, e, 0, e == 0, e == 1, False)
            with pe.Fori(1, EXPERTS // SLOTS) as i:
                for s in range(SLOTS):
                    expert(i * SLOTS + s, s, i, False, False, False)
            for e in range(EXPERTS // SLOTS * SLOTS, EXPERTS):
                expert(e, e % SLOTS, e // SLOTS, False, False, e == EXPERTS - 1)
            pe.wait_ge(S["yt_ready"], EXPERTS)
            turn_rows().then_inc(S["yh_mm"], 1)
            pe.wait_ge(S["yh_ready"], EXPERTS)
            pe.wait_ge(S["gsel_ready"], EXPERTS)
            turn_selection().then_inc(S["st_mm"], 1)
            pe.wait_ge(S["st_ready"], EXPERTS)
            scatter().then_inc(S["scat_mm"], 1)

            with pe.If(most_tokens > CAP):
                with pe.Fori(0, ROUNDS - 1) as r:
                    with pe.Fori(0, EXPERTS) as e:
                        n = r * EXPERTS + e
                        pe.wait_ge(S["o_sel"], n + 1)
                        gather().then_inc(S["o_xe"], 1)
                        pe.wait_ge(S["o_xesb"], n + 1)
                        pe.wait_ge(S["o_w"], (n + 1) * 48)
                        hidden(gate_ps, wg_sb[0], range(HC))
                        hidden(up_ps, wu_sb[0], range(HC)).then_inc(S["o_gu"], 1)
                        pe.wait_ge(S["o_hid"], n + 1)
                        down(wd_sb[0]).then_inc(S["o_yt"], 1)
                        pe.wait_ge(S["o_ytsb"], n + 1)
                        turn_rows().then_inc(S["o_yh"], 1)
                        pe.wait_ge(S["o_yhsb"], n + 1)
                        turn_selection().then_inc(S["o_st"], 1)
                        pe.wait_ge(S["o_stsb"], n + 1)
                        scatter().then_inc(S["o_scat"], 1)
            pe.matmul(bank[0][:, 0:P], zeros[0:32, :], zeros[0:32, :], start=True, stop=True).then_inc(S["moe_done"], 1)

        @block.scalar
        def _(act):
            steps = [0]

            def link(ins):
                steps[0] += 1
                ins.then_inc(S["act_step"], 1)
                act.wait_ge(S["act_step"], steps[0])

            def row(v):
                return v.rearrange("l n -> (l n)").partition_broadcast(P)

            for dst, src in ((conv_rows[0:TAPS, :], conv_w.rearrange("l k n -> (l k) n")),
                             (conv_rows[TAPS:TAPS + 1, :], conv_b), (rel_rows[:, :], rel_bias),
                             (g1_col[:, :], norm1_g.rearrange("l (p c) -> p (l c)", c=DC)),
                             (qg_col[0:HD, :], q_norm_g.rearrange("l n -> n l")),
                             (qg_col[HD:P, :], q_norm_g.rearrange("l n -> n l")),
                             (kg_col[0:HD, :], k_norm_g.rearrange("l n -> n l")),
                             (kg_col[HD:P, :], k_norm_g.rearrange("l n -> n l")),
                             (dtb_bc[:, :], row(dt_bias)), (alog_bc[:, :], row(a_log)), (dskip_bc[:, :], row(d_skip))):
                act.dma_start(dst, src).then_inc(small_in, 16)
            for dst, src in ((ssdg_bc[:, :], row(ssd_norm_g)), (g2_bc[:, :], row(norm2_g)),
                             (br_bc[:, 0:MOE_GROUPS], row(b_r1)), (br_bc[:, MOE_GROUPS:ROUTES], row(b_r2)),
                             (wr1_sb[:, :, :], w_r1.rearrange("l (p c) n -> p (l c) n", c=DC)),
                             (wr2_sb[:, :, :], w_r2.rearrange("l (p c) n -> p (l c) n", c=DC))):
                act.dma_start(dst, src).then_inc(late_in, 16)

            act.wait_ge(x_in, 16)
            act.activation(conv[:, 0:4, :].rearrange("p b t -> p (b t)"), h_sb[:, 1, :], ACT.Square,
                           accum_out=ms1[:, 1:2]).then_inc(S["ms1_act"], 1)
            act.wait_ge(S["zero_ready"], 1)
            for i in range(3):
                act.wait_ge(S["xbc_mm"], i + 1)
                act.copy(raw[:, 2 * i:2 * i + 2, TAPS - 1:RAWW], bank[5 + i][:, :].rearrange("p (b t) -> p b t", b=2)
                         ).then_inc(S["raw_ready"], 1)
            act.wait_ge(S["dtabs_ready"], 1)
            act.activation(dt_exp[:, :, :], dt_abs[:, :, :], ACT.Exp, scale=-1.0)
            act.wait_ge(small_in, 16 * 11)
            link(act.activation(a_exp[:, :], alog_bc[:, :], ACT.Exp))
            act.activation(dt_log[:, :, :], dt_exp[:, :, :], ACT.Ln, bias=ones[:, 0:1]).then_inc(S["dtlog_ready"], 1)
            for w, done in ((0, S["q_mm"]), (1, S["k_mm"])):
                for t in range(TILES):
                    act.wait_ge(done, t + 1)
                    act.activation(squares[:, w, t, :], bank[2 * w + t][:, :], ACT.Square).then_inc(S["squares_ready"], 1)
            for i in range(3):
                act.wait_ge(S["conv_ready"], 2 * i + 2)
                act.activation(conv[:, 2 * i:2 * i + 2, :], conv[:, 2 * i:2 * i + 2, :], ACT.Silu).then_inc(S["convsilu"], 1)
            for t in range(TILES):
                act.wait_ge(S["v_mm"], t + 1)
                act.copy(v_tok[:, t, :], bank[5 + t][:, :]).then_inc(S["v_ready"], 1)
            for t in range(TILES):
                act.wait_ge(S["adt_ready"], 1)
                if t:
                    act.wait_ge(S["rowcs_mm"], t)
                act.copy(a_bcast, bc(a_dt[:, t, :].unsqueeze(2), [P, HEADS, P])).then_inc(S["ab_ready"], 1)
            act.wait_ge(S["acs_ready"], 1)
            act.activation(decay_in[:, :], a_cs[:, 1, :], ACT.Exp)
            act.wait_ge(S["dend_lin"], 1)
            act.activation(decay_end[:, :], decay_arg[:, :], ACT.Exp).then_inc(S["dend_exp"], 1)
            for t in range(TILES):
                for g in range(GROUPS):
                    act.wait_ge(S["decay_lin"], t * HEADS + (g + 1) * HPG)
                    block4 = decay_mat[:, t, g * HPG:(g + 1) * HPG, :]
                    act.activation(block4, block4, ACT.Exp).then_inc(S["decay_exp"], 1)
            def numerators(h):
                act.wait_ge(S["negmax_ready"], h + 1)
                act.activation(prob[:, h % 4, 0:SEQ], prob[:, h % 4, 0:SEQ], ACT.Exp, bias=neg_max[:, h, 1:2],
                               accum_out=row_sum[:, h, 1:2])
                act.activation(prob[:, h % 4, SEQ:SEQ + P], prob[:, h % 4, SEQ:SEQ + P], ACT.Exp, bias=neg_max[:, h, 0:1],
                               accum_out=row_sum[:, h, 0:1]).then_inc(S["prob_ready"], 1)

            def keep_turned(h):
                act.wait_ge(S["probT_mm"], h + 1)
                if h >= 2:
                    act.wait_ge(S["pv_mm"], h - 1)
                act.copy(probT[:, h % 2, :], bank[6 + h % 2][:, 0:3 * P]).then_inc(S["probT_ready"], 1)

            for h in range(HEADS + 1):
                if h < HEADS:
                    numerators(h)
                if h >= 1:
                    keep_turned(h - 1)
            act.wait_ge(S["z_mm"], 1)
            act.wait_ge(S["score_ready"], HEADS)
            for t in range(TILES):
                act.activation(z_silu[:, t, :], bank[t][:, :], ACT.Silu).then_inc(S["zsilu_ready"], 1)
            for i in range(2 * TILES):
                t = i % TILES
                act.wait_ge(S["mixT_mm"], i + 1)
                blocks = slice(XS_BLOCKS, DC) if i < TILES else slice(0, XS_BLOCKS)
                act.copy(mixT[:, blocks, t * P:(t + 1) * P],
                         bank[(2 if i < TILES else 6) + t][:, :].rearrange("p (b t) -> p b t", b=XS_BLOCKS)
                         ).then_inc(S["mixT_ready"], 1)
            for t in range(TILES):
                act.wait_ge(S["h_ready"], 2 * t + 2)
                act.activation(work[:, 3584:4608], h_sb[:, t, :], ACT.Square, accum_out=ms2[:, t:t + 1]
                               ).then_inc(S["ms2_act"], 1)
            act.wait_ge(S["xnT_mm"], 1)
            for i in (0, 1):
                act.copy(xnT[:, 2 * i:2 * i + 2, :], bank[(2, 3)[i]][:, :].rearrange("p (c t) -> p c t", c=2)
                         ).then_inc(S["xnT_ready"], 1)
            act.wait_ge(S["gexp_in"], 1)
            act.activation(gexp[:, :, :], gexp[:, :, :], ACT.Exp).then_inc(S["gexp_ready"], 1)
            act.wait_ge(S["share_in"], 1)
            act.activation(share[:, 0, :], share[:, 0, :], ACT.Exp).then_inc(S["share_ready"], 1)

            gate_ps = bank[1][:, 0:HC * CAP].rearrange("p (m k) -> p m k", m=HC)
            xe_ps = bank[0][:, 0:DC * CAP].rearrange("p (c k) -> p c k", c=DC)
            act.wait_ge(S["most_ready"], 1)
            most_tokens = act.value_load(most_int[0:1, 0:1], min_val=0, max_val=SEQ)
            act.wait_ge(S["xe_mm"], 1)
            act.copy(xe_sb, xe_ps).then_inc(S["xe_ready"], 1)

            def expert(e, first, last):
                act.wait_ge(S["gate_mm"], e + 1)
                if not first:
                    act.wait_ge(S["hid_ready"], e)
                act.activation(silu_sb, gate_ps, ACT.Silu).then_inc(S["silu_ready"], 1)
                if not last:
                    act.wait_ge(S["xe_mm"], e + 2)
                    act.wait_ge(S["gu_mm"], e + 1)
                    act.copy(xe_sb, xe_ps).then_inc(S["xe_ready"], 1)

            expert(0, True, False)
            with act.Fori(1, EXPERTS - 1) as e:
                expert(e, False, False)
            expert(EXPERTS - 1, False, True)

            with act.If(most_tokens > CAP):
                with act.Fori(0, (ROUNDS - 1) * EXPERTS) as n:
                    act.wait_ge(S["o_xe"], n + 1)
                    act.copy(xe_sb, xe_ps).then_inc(S["o_xesb"], 1)
                    act.wait_ge(S["o_gu"], n + 1)
                    act.activation(silu_sb, gate_ps, ACT.Silu).then_inc(S["o_silu"], 1)
            act.nop()

        @block.vector
        def _(dve):
            steps = [0]

            def link(ins):
                steps[0] += 1
                ins.then_inc(S["dve_step"], 1)
                dve.wait_ge(S["dve_step"], steps[0])

            def mean(ap, n):
                return dve.tensor_scalar(ap, ap, 1.0 / n, EPS, ALU.mult, ALU.add)

            dve.memset(raw[:, :, 0:TAPS - 1], 0.0).then_inc(S["zero_ready"], 1)
            dve.wait_ge(x_in, 16)
            link(dve.tensor_tensor_reduce(xT[:, 0:4, :].rearrange("p c t -> p (c t)"), h_sb[:, 0, :], h_sb[:, 0, :], 1.0, 0.0,
                                          ALU.mult, ALU.add, ms1[:, 0:1]))
            dve.wait_ge(S["ms1_act"], 1)
            mean(ms1[:, :], D).then_inc(S["ms1_ready"], 1)
            dve.wait_ge(S["small_mm"], 1)
            dve.tensor_copy(relT[:, :], bank[4][0:HEADS, 64:64 + BUCKETS]).then_inc(S["relT_ready"], 1)
            dve.tensor_copy(conv_cols[:, :, :], bank[4][:, 0:CONV_BLOCKS * 8].rearrange("p (b k) -> p b k", b=CONV_BLOCKS)
                            [:, :, 0:TAPS + 1]).then_inc(S["small_ready"], 1)
            dve.wait_ge(S["rs1_ready"], 1)
            for t in range(TILES):
                dve.tensor_scalar(front[:, 3584 + t * D:3584 + (t + 1) * D], h_sb[:, t, :], rs1[:, t:t + 1], None, ALU.mult
                                  ).then_inc(S["xscaled"], 1)
            dve.tensor_tensor(qkg_col[:, :], qg_col[:, :], kg_col[:, :], ALU.mult).then_inc(S["qkg_ready"], 1)
            dve.wait_ge(S["xT_mm"], 1)
            for i in range(DC // 2):
                dve.tensor_tensor(xT[:, 2 * i:2 * i + 2, :], bank[i][:, :].rearrange("p (c t) -> p c t", c=2),
                                  bc(g1_col[:, 2 * i:2 * i + 2].unsqueeze(2), [P, 2, SEQ]), ALU.mult
                                  ).then_inc(S["xT_ready"], 1)
            dve.wait_ge(S["small_ready"], 1)
            def convolve(b):
                if b % 2 == 0:
                    dve.wait_ge(S["raw_ready"], b // 2 + 1)
                link(dve.tensor_scalar(conv[:, b, :], raw[:, b, 0:SEQ], conv_cols[:, b, 0:1], conv_cols[:, b, TAPS:TAPS + 1],
                                       ALU.mult, ALU.add))
                for k in range(1, TAPS):
                    ins = dve.scalar_tensor_tensor(conv[:, b, :], raw[:, b, k:k + SEQ], conv_cols[:, b, k:k + 1], conv[:, b, :],
                                                   ALU.mult, ALU.add)
                    if k < TAPS - 1:
                        link(ins)
                    else:
                        ins.then_inc(S["conv_ready"], 1)

            for b in range(CONV_BLOCKS):
                convolve(b)
            dve.wait_ge(S["dt_mm"], 1)
            link(dve.tensor_tensor(dt_lin[:, :, :], bank[4][:, 0:TILES * HEADS].rearrange("p (t h) -> p t h", t=TILES),
                                   bc(dtb_bc[:, :].unsqueeze(1), [P, TILES, HEADS]), ALU.add))
            dve.scalar_tensor_tensor(dt_abs[:, :, :], dt_lin[:, :, :], -1.0, dt_lin[:, :, :], ALU.mult, ALU.max
                                     ).then_inc(S["dtabs_ready"], 1)
            dve.wait_ge(S["dtlog_ready"], 1)
            link(dve.scalar_tensor_tensor(dt_sb[:, :, :], dt_lin[:, :, :], 0.0, dt_log[:, :, :], ALU.max, ALU.add))
            dve.scalar_tensor_tensor(a_dt[:, :, :], dt_sb[:, :, :], -1.0, bc(a_exp[:, :].unsqueeze(1), [P, TILES, HEADS]),
                                     ALU.mult, ALU.mult).then_inc(S["adt_ready"], 1)
            for w in range(2):
                for t in range(TILES):
                    dve.wait_ge(S["squares_ready"], 2 * w + t + 1)
                    ins = dve.tensor_reduce(msqk[:, w, t * HEADS:(t + 1) * HEADS],
                                            squares[:, w, t, :].rearrange("p (h d) -> p h d", h=HEADS), AX.X, ALU.add)
                    link(ins)
                mean(msqk[:, w, :], HD).then_inc(S["msqk_ready"], 1)
                if w == 0:
                    dve.wait_ge(S["acs_mm"], 1)
                    dve.tensor_copy(a_cs[:, :, :], bank[4][:, 0:TILES * HEADS].rearrange("p (t h) -> p t h", t=TILES)
                                    ).then_inc(S["acs_ready"], 1)
            for w in range(2):
                dve.wait_ge(S["rsqk_ready"], w + 1)
                for t in range(TILES):
                    dve.tensor_tensor(qk_tok[:, w, t, :].rearrange("p (h d) -> p h d", h=HEADS),
                                      bank[2 * w + t][:, :].rearrange("p (h d) -> p h d", h=HEADS),
                                      bc(rsqk[:, w, t * HEADS:(t + 1) * HEADS].unsqueeze(2), [P, HEADS, HD]), ALU.mult
                                      ).then_inc(S["qk_ready"], 1)
            dve.wait_ge(biasline_out, 16)
            for t in range(TILES):
                dve.wait_ge(S["xs_mm"], t + 1)
                xs_ps = (bank[7] if t == 0 else bank[5])[:, :].rearrange("p (h d) -> p h d", h=HEADS)
                for dst, by in ((xdt, dt_sb[:, t, :]), (y_ssd, dskip_bc[:, :])):
                    dve.tensor_tensor(dst[:, t, :].rearrange("p (h d) -> p h d", h=HEADS), xs_ps,
                                      bc(by.unsqueeze(2), [P, HEADS, HD]), ALU.mult).then_inc(S["xdt_ready"], 1)
            dve.wait_ge(S["cb_mm"], 1)
            dve.tensor_copy(b_tok[:, :], bank[4][:, P:2 * P]).then_inc(S["btok_ready"], 1)
            for g in range(GROUPS):
                dve.tensor_tensor(cb_sb[:, :, g, :], bank[6 - 2 * g][:, 2 * P:].rearrange("p (t l) -> p t l", t=TILES),
                                  bc(upto[:, :].unsqueeze(1), [P, TILES, P]), ALU.mult).then_inc(S["cb_ready"], 1)
            dve.wait_ge(S["qkg_ready"], 1)
            dve.wait_ge(S["qkT_mm"], 1)
            for i in range(2):
                dve.tensor_scalar(qkT[:, 0, 2 * i:2 * i + 2, :], bank[4 + i][:, :].rearrange("p (b t) -> p b t", b=2),
                                  qkg_col[:, 0:1], HD ** -0.5, ALU.mult, ALU.mult).then_inc(S["qT_ready"], 1)
            dve.wait_ge(S["qkT_mm"], 2)
            for i in range(2):
                dve.tensor_copy(qkT[:, 1, 2 * i:2 * i + 2, :], bank[6 + i][:, :].rearrange("p (b t) -> p b t", b=2)
                                ).then_inc(S["kT_ready"], 1)
            for t in range(TILES):
                dve.wait_ge(S["rowcs_mm"], t + 1)
                for h in range(HEADS):
                    dve.tensor_scalar(decay_mat[:, t, h, :], bank[2 * t + h // 4][:, (h % 4) * P:(h % 4 + 1) * P],
                                      a_cs[:, t, h:h + 1], 0.0, ALU.subtract, ALU.min).then_inc(S["decay_lin"], 1)
                if t == 0:
                    for g in range(GROUPS):
                        ins = dve.tensor_tensor(decay_arg[:, g * HPG:(g + 1) * HPG],
                                                bank[g][:, :].rearrange("p (h l) -> p h l", h=HPG)[:, :, P - 1],
                                                a_cs[:, 0, g * HPG:(g + 1) * HPG], ALU.subtract)
                        if g:
                            ins.then_inc(S["dend_lin"], 1)

            def bias_and_max(h):
                dve.wait_ge(S["score_mm"], h + 1)
                if h == 0:
                    dve.wait_ge(biastab_in, 16)
                if h >= 4:
                    dve.wait_ge(S["probT_mm"], h - 3)
                dve.tensor_tensor_reduce(prob[:, h % 4, 0:SEQ], bank[4 + h % 2][:, 0:SEQ], bias_tab[:, h, :], 1.0, LOW,
                                         ALU.add, ALU.max, row_max[:, h, 1:2])
                link(dve.tensor_tensor_reduce(prob[:, h % 4, SEQ:SEQ + P], bank[4 + h % 2][:, SEQ:SEQ + P],
                                              bias_tab[:, h, P:SEQ], 1.0, LOW, ALU.add, ALU.max, row_max[:, h, 0:1]))
                dve.tensor_scalar(neg_max[:, h, :], row_max[:, h, :], -1.0, None, ALU.mult).then_inc(S["negmax_ready"], 1)
                dve.nop().then_inc(S["score_ready"], 1)

            def mix(t, g):
                dve.wait_ge(S["decay_exp"], t * GROUPS + g + 1)
                block4 = decay_mat[:, t, g * HPG:(g + 1) * HPG, :]
                dve.tensor_tensor(block4, block4, bc(cb_sb[:, t, g, :].unsqueeze(1), [P, HPG, P]), ALU.mult
                                  ).then_inc(S["mix_ready"], 1)

            for h in range(HEADS):
                bias_and_max(h)
                if h % 2 == 1:
                    mix((h // 2) // GROUPS, (h // 2) % GROUPS)
            dve.wait_ge(S["prob_ready"], HEADS)
            link(dve.reciprocal(row_inv[:, :, :], row_sum[:, :, :]))
            dve.wait_ge(S["pv_mm"], HEADS)
            dve.wait_ge(S["z_mm"], 1)
            for t in range(TILES):
                dve.tensor_tensor(y_att[:, t, :].rearrange("p (h d) -> p h d", h=HEADS),
                                  bank[2 + t][:, :].rearrange("p (h d) -> p h d", h=HEADS),
                                  bc(row_inv[:, :, t].unsqueeze(2), [P, HEADS, HD]), ALU.mult).then_inc(S["yatt_ready"], 1)
            dve.wait_ge(S["ydiag_mm"], 1)
            link(dve.tensor_tensor(y_ssd[:, 0, :], bank[4][:, :], y_ssd[:, 0, :], ALU.add))
            dve.wait_ge(S["dend_exp"], 1)
            dve.tensor_tensor(xdt[:, 0, :].rearrange("p (h d) -> p h d", h=HEADS),
                              xdt[:, 0, :].rearrange("p (h d) -> p h d", h=HEADS),
                              bc(decay_end[:, :].unsqueeze(2), [P, HEADS, HD]), ALU.mult).then_inc(S["xdec_ready"], 1)

            def gated(t):
                dve.wait_ge(S["zsilu_ready"], t + 1)
                link(dve.tensor_tensor(y_ssd[:, t, :], y_ssd[:, t, :], z_silu[:, t, :], ALU.mult))
                link(dve.tensor_tensor_reduce(work[:, 2560:3072], y_ssd[:, t, :], y_ssd[:, t, :], 1.0, 0.0, ALU.mult, ALU.add,
                                              ms3[:, t:t + 1]))
                mean(ms3[:, t:t + 1], INNER).then_inc(S["ms3_ready"], 1)

            def normed(t):
                dve.wait_ge(late_in, 16 * 6)
                dve.wait_ge(S["rs3_ready"], t + 1)
                dve.scalar_tensor_tensor(y_ssd[:, t, :], y_ssd[:, t, :], rs3[:, t:t + 1], ssdg_bc[:, :], ALU.mult, ALU.mult
                                         ).then_inc(S["yssd_ready"], 1)

            dve.wait_ge(S["state_mm"], 1)
            for g in range(GROUPS):
                rows = slice(g * STATE, (g + 1) * STATE)
                dve.tensor_copy(state_sb[rows, :], bank[6][rows, g * HPG * HD:(g + 1) * HPG * HD]
                                ).then_inc(S["state_ready"], 1)
            gated(0)
            dve.wait_ge(S["ydiag_mm"], 2)
            dve.tensor_tensor(y_ssd[:, 1, :], bank[5][:, :], y_ssd[:, 1, :], ALU.add)
            dve.wait_ge(S["yoff_mm"], 1)
            for g in range(GROUPS):
                cols, hs = slice(g * HPG * HD, (g + 1) * HPG * HD), slice(g * HPG, (g + 1) * HPG)
                link(dve.tensor_tensor(y_off[:, cols].rearrange("p (h d) -> p h d", h=HPG),
                                       bank[7 - g][:, cols].rearrange("p (h d) -> p h d", h=HPG),
                                       bc(decay_in[:, hs].unsqueeze(2), [P, HPG, HD]), ALU.mult))
            link(dve.tensor_tensor(y_ssd[:, 1, :], y_ssd[:, 1, :], y_off, ALU.add))
            normed(0)
            gated(1)
            normed(1)
            dve.tensor_copy(wr_sb[:, :, 0:MOE_GROUPS], wr1_sb[:, :, :]).then_inc(S["wr_ready"], 1)
            dve.tensor_copy(wr_sb[:, :, MOE_GROUPS:ROUTES], wr2_sb[:, :, :]).then_inc(S["wr_ready"], 1)
            for t in range(TILES):
                for n in range(2):
                    dve.wait_ge(S["wout_mm"], 2 * t + n + 1)
                    cols = slice(n * HALF, (n + 1) * HALF)
                    dve.tensor_tensor(h_sb[:, t, cols], bank[(0, 1, 4, 5)[2 * t + n]][:, :], h_sb[:, t, cols], ALU.add
                                      ).then_inc(S["h_ready"], 1)
                dve.wait_ge(S["ms2_act"], t + 1)
                mean(ms2[:, t:t + 1], D).then_inc(S["ms2_ready"], 1)
                dve.wait_ge(S["rs2_ready"], t + 1)
                dve.scalar_tensor_tensor(xn[:, t, :, :].rearrange("p c q -> p q c"),
                                         h_sb[:, t, :].rearrange("p (q c) -> p q c", c=DC), rs2[:, t:t + 1],
                                         g2_bc[:, :].rearrange("p (q c) -> p q c", c=DC), ALU.mult, ALU.mult
                                         ).then_inc(S["xn_ready"], 1)
            dve.wait_ge(S["xnT_mm"], 1)
            for i in (2, 3):
                dve.tensor_copy(xnT[:, 2 * i:2 * i + 2, :], bank[(2, 3, 6, 7)[i]][:, :].rearrange("p (c t) -> p c t", c=2)
                                ).then_inc(S["xnT_ready"], 1)

            dve.wait_ge(S["logit_mm"], 1)
            link(dve.tensor_tensor(logit[:, :, :], bank[0][:, 0:TILES * ROUTES].rearrange("p (t n) -> p t n", t=TILES),
                                   bc(br_bc[:, :].unsqueeze(1), [P, TILES, ROUTES]), ALU.add))
            l1, l2 = logit[:, :, 0:MOE_GROUPS], logit[:, :, MOE_GROUPS:ROUTES]

            def first_highest(hot, eq, values, high, n):
                link(dve.tensor_reduce(high, values, AX.X, ALU.max))
                link(dve.tensor_tensor(eq, values, bc(high.unsqueeze(2), [P, TILES, n]), ALU.is_equal))
                link(dve.scalar_tensor_tensor(eq, eq, -float(P), bc(expert_iota[:, 0:n].unsqueeze(1), [P, TILES, n]),
                                              ALU.mult, ALU.add))
                link(dve.tensor_reduce(low_at[:, :], eq, AX.X, ALU.min))
                link(dve.tensor_tensor(hot, eq, bc(low_at[:, :].unsqueeze(2), [P, TILES, n]), ALU.is_equal))

            first_highest(ghot[:, :, :], eq4[:, :, :], l1, top[:, 0, :], MOE_GROUPS)
            dve.tensor_tensor(gexp[:, :, :], l1, bc(top[:, 0, :].unsqueeze(2), [P, TILES, MOE_GROUPS]), ALU.subtract
                              ).then_inc(S["gexp_in"], 1)
            link(dve.tensor_scalar(ghot[:, :, :], ghot[:, :, :], -LOW, LOW, ALU.mult, ALU.add))
            link(dve.tensor_tensor(masked[:, :, :].rearrange("p t (g k) -> p t g k", g=MOE_GROUPS),
                                   l2.rearrange("p t (g k) -> p t g k", g=MOE_GROUPS),
                                   bc(ghot[:, :, :].unsqueeze(3), [P, TILES, MOE_GROUPS, PER_GROUP]), ALU.add))
            first_highest(hot1[:, :, :], eq32[:, :, :], masked[:, :, :], top[:, 1, :], EXPERTS)
            link(dve.scalar_tensor_tensor(masked[:, :, :], hot1[:, :, :], 2 * LOW, masked[:, :, :], ALU.mult, ALU.add))
            first_highest(hot2[:, :, :], eq32[:, :, :], masked[:, :, :], top[:, 2, :], EXPERTS)
            dve.tensor_tensor(share[:, 0, :], top[:, 2, :], top[:, 1, :], ALU.subtract).then_inc(S["share_in"], 1)
            dve.tensor_tensor(chosen[:, :, :], hot1[:, :, :], hot2[:, :, :], ALU.add).then_inc(S["chosen_ready"], 1)
            dve.wait_ge(S["gexp_ready"], 1)
            link(dve.tensor_reduce(gsum[:, :], gexp[:, :, :], AX.X, ALU.add))
            dve.wait_ge(S["share_ready"], 1)
            link(dve.scalar_tensor_tensor(share[:, 1, :], share[:, 0, :], 1.0, gsum[:, :], ALU.add, ALU.mult))
            link(dve.reciprocal(share[:, 2, :], share[:, 1, :]))
            link(dve.tensor_tensor(share[:, 3, :], share[:, 2, :], share[:, 0, :], ALU.mult))
            link(dve.tensor_tensor(hot1[:, :, :], hot1[:, :, :], bc(share[:, 2, :].unsqueeze(2), [P, TILES, EXPERTS]), ALU.mult))
            link(dve.tensor_tensor(hot2[:, :, :], hot2[:, :, :], bc(share[:, 3, :].unsqueeze(2), [P, TILES, EXPERTS]), ALU.mult))
            link(dve.tensor_tensor(gates[:, :, :], hot1[:, :, :], hot2[:, :, :], ALU.add))
            dve.wait_ge(S["rank_mm"], 1)
            rank_ps = bank[1][:, 0:TILES * EXPERTS].rearrange("p (t n) -> p t n", t=TILES)
            link(dve.scalar_tensor_tensor(rank[:, :, :], rank_ps, 1.0, chosen[:, :, :], ALU.add, ALU.mult))
            link(dve.tensor_scalar(rank[:, :, :], rank[:, :, :], 1.0, None, ALU.subtract))
            link(dve.tensor_reduce(most[0:1, :], bank[1][0:1, 2 * EXPERTS:3 * EXPERTS], AX.X, ALU.max))
            dve.tensor_copy(most_int[0:1, :], most[0:1, :]).then_inc(S["most_ready"], 1)
            dve.wait_ge(S["most_ready"], 1)

            def select(e, done):
                for t in range(TILES):
                    ins = dve.tensor_scalar(sel[:, t, :], rank_iota[:, 0:CAP], rank[:, t, bass.ds(e, 1)], None, ALU.is_equal)
                ins.then_inc(done, 1)

            def select_gated(e, done):
                for t in range(TILES):
                    ins = dve.tensor_scalar(gsel[:, t, :], rank_iota[:, :], rank[:, t, bass.ds(e, 1)],
                                            gates[:, t, bass.ds(e, 1)], ALU.is_equal, ALU.mult)
                ins.then_inc(done, 1)

            yt_ps = bank[2][:, :].rearrange("p (m k) -> p m k", m=HC)
            up_ps = bank[3][:, 0:HC * CAP].rearrange("p (m k) -> p m k", m=HC)

            def keep_rows(done):
                dve.tensor_copy(y_sb, bank[1][:, :]).then_inc(done, 1)

            def keep_selection(done):
                dve.tensor_copy(gselT_sb, bank[3][:, 0:TILES * P].rearrange("p (t k) -> p t k", t=TILES)
                                ).then_inc(done, 1)

            def previous(e, second):
                dve.wait_ge(S["yh_mm"], e)
                if not second:
                    dve.wait_ge(S["scat_mm"], e - 1)
                keep_rows(S["yh_ready"])
                dve.wait_ge(S["st_mm"], e)
                keep_selection(S["st_ready"])

            def expert(e, first, second, last, before_last):
                dve.wait_ge(S["gu_mm"], e + 1)
                dve.wait_ge(S["silu_ready"], e + 1)
                if not first:
                    dve.wait_ge(S["yt_mm"], e)
                dve.tensor_tensor(hid_sb, up_ps, silu_sb, ALU.mult).then_inc(S["hid_ready"], 1)
                if not first:
                    previous(e, second)
                select_gated(e, S["gsel_ready"])
                if not (last or before_last):
                    dve.wait_ge(S["xe_mm"], e + 2)
                    select(e + 2, S["sel_ready"])
                if not first:
                    dve.wait_ge(S["yh_mm"], e)
                dve.wait_ge(S["yt_mm"], e + 1)
                dve.tensor_copy(yt_sb, yt_ps).then_inc(S["yt_ready"], 1)

            select(0, S["sel_ready"])
            dve.wait_ge(S["xe_mm"], 1)
            select(1, S["sel_ready"])
            expert(0, True, False, False, False)
            expert(1, False, True, False, False)
            with dve.Fori(2, EXPERTS - 2) as e:
                expert(e, False, False, False, False)
            expert(EXPERTS - 2, False, False, False, True)
            expert(EXPERTS - 1, False, False, True, False)
            previous(EXPERTS, False)

            most_tokens = dve.value_load(most_int[0:1, 0:1], min_val=0, max_val=SEQ)
            with dve.If(most_tokens > CAP):
                dve.wait_ge(S["scat_mm"], EXPERTS)
                dve.nop().then_inc(S["o_turn"], 1)
                with dve.Fori(0, ROUNDS - 1) as r:
                    dve.tensor_scalar(rank[:, :, :], rank[:, :, :], float(CAP), None, ALU.subtract).then_inc(S["o_rank"], 1)
                    with dve.Fori(0, EXPERTS) as e:
                        n = r * EXPERTS + e
                        dve.wait_ge(S["o_rank"], r + 1)
                        for t in range(TILES):
                            dve.tensor_scalar(gsel[:, t, :], rank_iota[:, :], rank[:, t, bass.ds(e, 1)],
                                              gates[:, t, bass.ds(e, 1)], ALU.is_equal, ALU.mult)
                        select(e, S["o_sel"])
                        dve.wait_ge(S["o_gu"], n + 1)
                        dve.wait_ge(S["o_silu"], n + 1)
                        dve.tensor_tensor(hid_sb, up_ps, silu_sb, ALU.mult).then_inc(S["o_hid"], 1)
                        dve.wait_ge(S["o_yt"], n + 1)
                        dve.tensor_copy(yt_sb, yt_ps).then_inc(S["o_ytsb"], 1)
                        dve.wait_ge(S["o_yh"], n + 1)
                        keep_rows(S["o_yhsb"])
                        dve.wait_ge(S["o_st"], n + 1)
                        keep_selection(S["o_stsb"])
                        dve.wait_ge(S["o_scat"], n + 1)
                        dve.nop().then_inc(S["o_turn"], 1)
            dve.nop()

            dve.wait_ge(S["moe_done"], 1)
            for t in range(TILES):
                for n in range(2):
                    cols = slice(n * HALF, (n + 1) * HALF)
                    dve.tensor_tensor(h_sb[:, t, cols], bank[4 + 2 * t + n][:, :], h_sb[:, t, cols], ALU.add
                                      ).then_inc(S["result_ready"], 1)


_INS = ["x", "rel_bias", "norm1_g", "w_in", "conv_w", "conv_b", "dt_bias", "a_log", "d_skip", "ssd_norm_g",
        "q_norm_g", "k_norm_g", "w_out", "norm2_g", "w_r1", "b_r1", "w_r2", "b_r2", "w_gate", "w_up", "w_down"]


def kernel(**inputs):
    import numpy as _np
    import concourse.bacc as _bacc
    from concourse import mybir as _mybir
    from concourse.bass_utils import run_bass_kernel_spmd as _run

    nc = _bacc.Bacc("TRN2", target_bir_lowering=False, num_devices=1, dynamic_dma_scratch_size=1024)
    arrays, args = {}, []
    for name in _INS:
        a = _np.ascontiguousarray(inputs[name])
        arrays[f"in_{name}_dram"] = a
        args.append(nc.dram_tensor(f"in_{name}_dram", a.shape, _mybir.dt.from_np(a.dtype), kind="ExternalInput").ap())
    args.append(nc.dram_tensor("bias_rows", (P, HEADS, SEQ + P), F32, kind="Internal").ap())
    args.append(nc.dram_tensor("out_0_dram", (1, SEQ, D), F32, kind="ExternalOutput").ap())
    hymba_layer(nc, *args)
    r = _run(nc, [arrays], core_ids=[0])
    return r.results[0]["out_0_dram"]
```

```python
from contextlib import ExitStack

import numpy as np

import concourse.bass as bass
from concourse import mybir

F32 = mybir.dt.float32
F32R = mybir.dt.float32r
BF16 = mybir.dt.bfloat16
I32 = mybir.dt.int32
ALU = mybir.AluOpType
ACT = mybir.ActivationFunctionType
AX = mybir.AxisListType

P = 128
SEQ = 256
TILES = SEQ // P
D = 1024
DC = D // P
HEADS = 8
HD = 64
INNER = HEADS * HD
GROUPS = 2
HPG = HEADS // GROUPS
STATE = 64
TAPS = 4
CONV_CH = INNER + 2 * GROUPS * STATE
CONV_BLOCKS = CONV_CH // P
XS_BLOCKS = INNER // P
B_BLOCK = XS_BLOCKS
C_BLOCK = XS_BLOCKS + 1
IN_COLS = INNER + CONV_CH + HEADS + 3 * INNER
COL_Z = 0
COL_XBC = INNER
COL_Q = INNER + CONV_CH + HEADS
COL_K = COL_Q + INNER
COL_V = COL_K + INNER
XBC_COLS = CONV_CH + HEADS
BUCKETS = 32
MAX_DIST = 128
MOE_GROUPS = 4
PER_GROUP = 8
EXPERTS = MOE_GROUPS * PER_GROUP
ROUTES = MOE_GROUPS + EXPERTS
HID = 512
HC = HID // P
EPS = 1e-6
LOW = -1e30
CAP = 64
ROUNDS = SEQ // CAP
SLOTS = 3
UNIT = 2
UNITS = 2 * (DC // UNIT)
BODY = 2 * SLOTS
PEELED = EXPERTS % BODY
assert 2 * CAP == P and PEELED == 2
PIECE = DC * HID
HALF = D // 2


def bucket_ranges():
    exact = BUCKETS // 2
    dist = np.arange(SEQ)
    far = exact + (np.log(np.maximum(dist, exact) / exact) / np.log(MAX_DIST / exact)
                   * (BUCKETS - exact)).astype(np.int64)
    bucket = np.where(dist < exact, dist, np.minimum(far, BUCKETS - 1))
    return [(b, int(np.flatnonzero(bucket == b)[0]), int(np.flatnonzero(bucket == b)[-1]))
            for b in range(BUCKETS) if (bucket == b).any()]


def hymba_layer(nc, x, rel_bias, norm1_g, w_in, conv_w, conv_b, dt_bias, a_log, d_skip, ssd_norm_g,
                q_norm_g, k_norm_g, w_out, norm2_g, w_r1, b_r1, w_r2, b_r2, w_gate, w_up, w_down,
                bias_rows, out):
    x_rows = x.rearrange("b (t p) d -> p (b t) d", p=P)
    out_rows = out.rearrange("b (t p) d -> p (b t) d", p=P)
    win_rows = w_in.rearrange("l (p c) n -> p (l c) n", c=DC)
    wout_rows = w_out.rearrange("l (c p) n -> p (l c) n", p=P)
    gate_rows = w_gate.rearrange("l e (p c) n -> (l e) p c n", c=DC)
    up_rows = w_up.rearrange("l e (p c) n -> (l e) p c n", c=DC)
    down_rows = w_down.rearrange("l e (c p) n -> (l e) p c n", p=P)

    ctx = ExitStack()
    with ctx:
        def sb(name, shape, dt=F32):
            return ctx.enter_context(nc.sbuf_tensor(name, shape, dt))

        def sem(name):
            return ctx.enter_context(nc.semaphore(name))

        ring = sb("ring", [P, SLOTS * 3 * PIECE])

        def piece(i, n=1):
            return ring[:, i * PIECE:(i + n) * PIECE]

        wg_sb = [piece(3 * s).rearrange("p (c n) -> p c n", c=DC) for s in range(SLOTS)]
        wu_sb = [piece(3 * s + 1).rearrange("p (c n) -> p c n", c=DC) for s in range(SLOTS)]
        wd_sb = [piece(3 * s + 2).rearrange("p (c n) -> p c n", c=HC) for s in range(SLOTS)]
        wxbc_sb = ring[:, 0:DC * XBC_COLS].rearrange("p (c n) -> p c n", c=DC)
        wq_sb, wk_sb, wv_sb, wz_sb = [piece(i).rearrange("p (c n) -> p c n", c=DC) for i in (2, 3, 4, 5)]
        wout_sb = piece(6, 2).rearrange("p (c n) -> p c n", c=DC)
        raw_at = DC * XBC_COLS
        RAWW = SEQ + TAPS - 1
        raw = ring[:, raw_at:raw_at + CONV_BLOCKS * RAWW].rearrange("p (b t) -> p b t", b=CONV_BLOCKS)
        assert raw_at + CONV_BLOCKS * RAWW <= 2 * PIECE
        last_piece = piece(8)
        bias_tab = last_piece[:, 0:HEADS * SEQ].rearrange("p (h j) -> p h j", h=HEADS)
        z_silu = last_piece[:, 0:TILES * INNER].rearrange("p (t n) -> p t n", t=TILES)
        xdt = last_piece[:, 2048:3072].rearrange("p (t n) -> p t n", t=TILES)
        y_ssd = last_piece[:, 3072:4096].rearrange("p (t n) -> p t n", t=TILES)

        work = sb("work", [P, 5504])
        xn = work[:, 0:2048].rearrange("p (t c q) -> p t c q", t=TILES, c=DC)
        xn_parts = [work[:, 2048 + 1024 * k:3072 + 1024 * k].bitcast(BF16).rearrange("p (t c q) -> p t c q", t=TILES, c=DC)
                    for k in range(3)]
        low_sb = work[0:CAP, 0:512]
        silu_sb = work[0:CAP, 512:1024]
        hid_sb = work[0:CAP, 1024:1536]
        hidT_sb = work[:, 1536:1792].rearrange("p (m k) -> p m k", m=HC)
        gselT_sb = work[:, 1792:2048].rearrange("p (t k) -> p t k", t=TILES)
        gsel = work[:, 5120:5376].rearrange("p (t w k) -> p t w k", t=TILES, w=2)
        sel = work[:, 5376:5440].bitcast(BF16).rearrange("p (t k) -> p t k", t=TILES)
        qk_tok = work[:, 0:2048].rearrange("p (w t n) -> p w t n", w=2, t=TILES)
        decay_mat = work[:, 0:2048].rearrange("p (t h l) -> p t h l", t=TILES, h=HEADS)
        prob = work[:, 2048:3584].rearrange("p (k n) -> p k n", k=4)
        a_bcast = work[:, 2048:3072].rearrange("p (h l) -> p h l", h=HEADS)
        probT = work[:, 3584:4352].rearrange("p (k n) -> p k n", k=2)
        v_tok = work[:, 4352:5376].rearrange("p (t n) -> p t n", t=TILES)

        with nc.sbuf_tensor("front", [P, 6144], F32) as front:
            pass
        xe_split = sb("xe_split", [P, 2, DC, P], F32R)
        w_split = sb("w_split", [P, 2, 2, UNIT, HID], F32R)
        xT = front[:, 0:2048].rearrange("p (c t) -> p c t", c=DC)
        y_att = front[:, 0:1024].rearrange("p (t n) -> p t n", t=TILES)
        conv = front[:, 2048:3584].rearrange("p (b t) -> p b t", b=CONV_BLOCKS)
        qkT = front[:, 3584:5632].rearrange("p (w b t) -> p w b t", w=2, b=XS_BLOCKS)
        mixT = front[:, 3584:5632].rearrange("p (c t) -> p c t", c=DC)
        x_scaled = front[:, 3584:5632].rearrange("p (t q c) -> p t c q", t=TILES, c=DC)
        squares = front[:, 3584:5632].rearrange("p (w t n) -> p w t n", w=2, t=TILES)
        xnT = front[:, 0:2048].rearrange("p (c t) -> p c t", c=DC)
        y_off = work[:, 2048:2560]

        h_sb = sb("h", [P, TILES, D])
        ident = sb("ident", [P, P])
        upto = sb("upto", [P, P])
        before = sb("before", [P, P])
        ones = sb("ones", [P, P])
        zeros = sb("zeros", [P, P])
        rank_iota = sb("rank_iota", [P, 2 * CAP])
        expert_iota = sb("expert_iota", [P, EXPERTS])
        minus_half = sb("minus_half", [P, 16])
        g1_col = sb("g1_col", [P, DC])
        qg_col = sb("qg_col", [P, 1])
        kg_col = sb("kg_col", [P, 1])
        qkg_col = sb("qkg_col", [P, 1])
        conv_rows = last_piece[0:TAPS + 1, 3072:3072 + CONV_CH]
        conv_cols = sb("conv_cols", [P, CONV_BLOCKS, TAPS + 1])
        rel_rows = sb("rel_rows", [BUCKETS, HEADS])
        relT = sb("relT", [HEADS, BUCKETS])
        bias_line = last_piece[0:HEADS, 2048:2048 + SEQ + P]
        dtb_bc = sb("dtb_bc", [P, HEADS])
        alog_bc = sb("alog_bc", [P, HEADS])
        dskip_bc = sb("dskip_bc", [P, HEADS])
        ssdg_bc = sb("ssdg_bc", [P, INNER])
        g2_bc = sb("g2_bc", [P, D])
        y_sb = g2_bc
        br_bc = sb("br_bc", [P, ROUTES])
        wr1_sb = sb("wr1_sb", [P, DC, MOE_GROUPS])
        wr2_sb = sb("wr2_sb", [P, DC, EXPERTS])
        wr_sb = sb("wr_sb", [P, DC, ROUTES])
        ms1 = sb("ms1", [P, TILES])
        rs1 = sb("rs1", [P, TILES])
        msqk = sb("msqk", [P, 2, TILES * HEADS])
        rsqk = sb("rsqk", [P, 2, TILES * HEADS])
        dt_lin = sb("dt_lin", [P, TILES, HEADS])
        dt_abs = sb("dt_abs", [P, TILES, HEADS])
        dt_exp = sb("dt_exp", [P, TILES, HEADS])
        dt_log = sb("dt_log", [P, TILES, HEADS])
        dt_sb = sb("dt_sb", [P, TILES, HEADS])
        a_exp = sb("a_exp", [P, HEADS])
        a_dt = sb("a_dt", [P, TILES, HEADS])
        a_cs = sb("a_cs", [P, TILES, HEADS])
        decay_arg = sb("decay_arg", [P, HEADS])
        decay_end = sb("decay_end", [P, HEADS])
        decay_in = sb("decay_in", [P, HEADS])
        cb_sb = sb("cb_sb", [P, TILES, GROUPS, P])
        b_tok = sb("b_tok", [P, P])
        state_sb = sb("state_sb", [P, HPG * HD])
        row_max = sb("row_max", [P, HEADS, TILES])
        neg_max = sb("neg_max", [P, HEADS, TILES])
        row_sum = sb("row_sum", [P, HEADS, TILES])
        row_inv = sb("row_inv", [P, HEADS, TILES])
        ms3 = sb("ms3", [P, TILES])
        rs3 = sb("rs3", [P, TILES])
        ms2 = sb("ms2", [P, TILES])
        rs2 = sb("rs2", [P, TILES])
        logit = sb("logit", [P, TILES, ROUTES])
        top = sb("top", [P, 4, TILES])
        low_at = sb("low_at", [P, TILES])
        gexp = sb("gexp", [P, TILES, MOE_GROUPS])
        gsum = sb("gsum", [P, TILES])
        gval = sb("gval", [P, TILES])
        ghot = sb("ghot", [P, TILES, MOE_GROUPS])
        eq4 = sb("eq4", [P, TILES, MOE_GROUPS])
        eq32 = sb("eq32", [P, TILES, EXPERTS])
        masked = sb("masked", [P, TILES, EXPERTS])
        hot1 = sb("hot1", [P, TILES, EXPERTS])
        hot2 = sb("hot2", [P, TILES, EXPERTS])
        share = sb("share", [P, 4, TILES])
        gates = sb("gates", [P, TILES, EXPERTS])
        chosen = sb("chosen", [P, TILES, EXPERTS])
        rank = sb("rank", [P, TILES, EXPERTS + 2])
        most = sb("most", [1, 1])
        most_int = sb("most_int", [1, 1], I32)

        bank = [ctx.enter_context(nc.psum_tensor(f"bank{i}", [P, 512], F32)) for i in range(8)]

        x_in, small_in, late_in = sem("x_in"), sem("small_in"), sem("late_in")
        wxbc_in, wq_in, wk_in, wv_in, wz_in = [sem(n) for n in ("wxbc_in", "wq_in", "wk_in", "wv_in", "wz_in")]
        wout_in, biasline_out, biastab_in, out_done = [sem(n) for n in ("wout_in", "biasline_out", "biastab_in", "out_done")]
        wg_in = [sem(f"wg_in{s}") for s in range(SLOTS)]
        wu_in = [sem(f"wu_in{s}") for s in range(SLOTS)]
        wd_in = [sem(f"wd_in{s}") for s in range(SLOTS)]
        names = """const_base const_ready zero_ready ms1_ready rs1_ready ms1_act xscaled xT_mm xT_ready small_mm
            small_ready relT_ready line_ready xbc_mm raw_ready dt_mm q_mm k_mm v_mm z_mm squares_ready
            msqk_ready rsqk_ready qk_ready v_ready conv_ready convsilu dtabs_ready dtlog_ready adt_ready acs_mm
            acs_ready ab_ready rowcs_mm decay_lin decay_exp dend_lin dend_exp xs_mm xdt_ready btok_ready cb_mm
            cb_ready mix_ready qkT_mm qT_ready kT_ready qkg_ready score_mm score_ready negmax_ready prob_ready
            probT_mm probT_ready pv_mm zsilu_ready yatt_ready ydiag_mm xdec_ready state_mm state_ready yoff_mm
            ms3_ready rs3_ready yssd_ready mixT_mm mixT_ready wout_mm h_ready ms2_ready ms2_act rs2_ready
            xn_ready xnT_mm xnT_ready wr_ready logit_mm gexp_in gexp_ready share_in share_ready chosen_ready
            rank_mm most_ready split0 split1 split2 split3 split4 sel_ready gsel_ready xe_mm xh_ready xe_ready
            whi_ready wlo_ready unit_mm glow_ready gsum_ready silu_ready ulow_ready hid_ready hidT_mm hidT_ready
            y0_mm y_mm y0_ready y1_ready st_mm st_ready scat_mm moe_done result_ready dve_step act_step o_rank
            o_turn o_w o_sel o_xe o_xh o_xs usum_ready o_st o_stsb o_scat""".split()
        S = {n: sem(n) for n in names}

        block = ctx.enter_context(nc.Block())

        def bc(ap, shape):
            return ap.to_broadcast(shape)

        def flat(ap):
            return ap

        @block.sync
        def _(sp):
            sp.dma_start(h_sb[:, :, :], x_rows).then_inc(x_in, 16)
            sp.dma_start(wxbc_sb, win_rows[:, :, COL_XBC:COL_XBC + XBC_COLS]).then_inc(wxbc_in, 16)
            sp.dma_start(wq_sb, win_rows[:, :, COL_Q:COL_Q + INNER]).then_inc(wq_in, 16)
            sp.dma_start(wk_sb, win_rows[:, :, COL_K:COL_K + INNER]).then_inc(wk_in, 16)
            sp.dma_start(wv_sb, win_rows[:, :, COL_V:COL_V + INNER]).then_inc(wv_in, 16)
            sp.dma_start(wz_sb, win_rows[:, :, COL_Z:COL_Z + INNER]).then_inc(wz_in, 16)
            sp.dma_start(wout_sb, wout_rows).then_inc(wout_in, 16)

            sp.wait_ge(S["line_ready"], len(bucket_ranges()))
            sp.dma_start(bias_rows.rearrange("p h i -> h p i"), bias_line.unsqueeze(1).to_broadcast([HEADS, P, SEQ + P])
                         ).then_inc(biasline_out, 16)
            sp.wait_ge(biasline_out, 16)
            sp.dma_start(bias_tab, bass.AP(bias_rows.tensor, P - 1,
                                           [[HEADS * (SEQ + P) - 1, P], [SEQ + P, HEADS], [1, SEQ]])
                         ).then_inc(biastab_in, 16)

            sp.wait_ge(S["dt_mm"], 1)
            sp.dma_start(wg_sb[0], gate_rows[0]).then_inc(wg_in[0], 16)
            sp.wait_ge(S["conv_ready"], CONV_BLOCKS)
            sp.dma_start(wu_sb[0], up_rows[0]).then_inc(wu_in[0], 16)
            sp.wait_ge(S["q_mm"], TILES)
            sp.dma_start(wd_sb[0], down_rows[0]).then_inc(wd_in[0], 16)
            sp.wait_ge(S["k_mm"], TILES)
            sp.dma_start(wg_sb[1], gate_rows[1]).then_inc(wg_in[1], 16)
            sp.wait_ge(S["v_mm"], TILES)
            sp.dma_start(wu_sb[1], up_rows[1]).then_inc(wu_in[1], 16)
            sp.wait_ge(S["z_mm"], 1)
            sp.dma_start(wd_sb[1], down_rows[1]).then_inc(wd_in[1], 16)
            sp.wait_ge(S["wout_mm"], TILES * 2)
            sp.dma_start(wg_sb[2], gate_rows[2]).then_inc(wg_in[2], 16)
            sp.dma_start(wu_sb[2], up_rows[2]).then_inc(wu_in[2], 16)
            sp.wait_ge(S["yssd_ready"], TILES)
            sp.dma_start(wd_sb[2], down_rows[2]).then_inc(wd_in[2], 16)

            def refill(e, s):
                sp.wait_ge(S["wlo_ready"], e * UNITS + UNITS // 2)
                sp.dma_start(wg_sb[s], gate_rows[e + SLOTS]).then_inc(wg_in[s], 16)
                sp.wait_ge(S["wlo_ready"], e * UNITS + UNITS)
                sp.dma_start(wu_sb[s], up_rows[e + SLOTS]).then_inc(wu_in[s], 16)
                sp.wait_ge(S["y_mm"], e + 1)
                sp.dma_start(wd_sb[s], down_rows[e + SLOTS]).then_inc(wd_in[s], 16)

            full = (EXPERTS - SLOTS) // SLOTS
            with sp.Fori(0, full) as i:
                for s in range(SLOTS):
                    refill(i * SLOTS + s, s)
            for e in range(full * SLOTS, EXPERTS - SLOTS):
                refill(e, e % SLOTS)

            sp.wait_ge(S["most_ready"], 1)
            most_tokens = sp.value_load(most_int[0:1, 0:1], min_val=0, max_val=SEQ)
            with sp.If(most_tokens > CAP):
                with sp.Fori(0, ROUNDS - 1) as r:
                    with sp.Fori(0, EXPERTS) as e:
                        sp.wait_ge(S["o_turn"], r * EXPERTS + e + 1)
                        sp.dma_start(wg_sb[0], gate_rows[e]).then_inc(S["o_w"], 16)
                        sp.dma_start(wu_sb[0], up_rows[e]).then_inc(S["o_w"], 16)
                        sp.dma_start(wd_sb[0], down_rows[e]).then_inc(S["o_w"], 16)
            sp.nop()

            for t in range(TILES):
                for n in range(2):
                    sp.wait_ge(S["result_ready"], t * 2 + n + 1)
                    sp.dma_start(out_rows[:, t, n * HALF:(n + 1) * HALF],
                                 h_sb[:, t, n * HALF:(n + 1) * HALF]).then_inc(out_done, 16)
            sp.wait_ge(out_done, 16 * TILES * 2)

        @block.gpsimd
        def _(pool):
            pool.memset(ident[:, :], 0.0).then_inc(S["const_base"], 1)
            pool.memset(ones[:, :], 1.0).then_inc(S["const_base"], 1)
            pool.memset(zeros[:, :], 0.0).then_inc(S["const_base"], 1)
            pool.memset(minus_half[:, :], -0.5).then_inc(S["const_base"], 1)
            pool.memset(bias_line[:, :], LOW).then_inc(S["const_base"], 1)
            pool.iota(rank_iota[:, :], [[0, 2], [1, CAP]], base=0, channel_multiplier=0,
                      allow_small_or_imprecise_dtypes=True).then_inc(S["const_base"], 1)
            pool.iota(expert_iota[:, :], [[1, EXPERTS]], base=0, channel_multiplier=0,
                      allow_small_or_imprecise_dtypes=True).then_inc(S["const_base"], 1)
            pool.wait_ge(S["const_base"], 7)
            pool.affine_select(out=ident[:, :], in_=ident[:, :], compare_op=ALU.not_equal, fill=1.0, base=0,
                               pattern=[[-1, P]], channel_multiplier=1).then_inc(S["const_ready"], 1)
            pool.affine_select(out=upto[:, :], in_=ones[:, :], compare_op=ALU.is_ge, fill=0.0, base=0,
                               pattern=[[1, P]], channel_multiplier=-1).then_inc(S["const_ready"], 1)
            pool.affine_select(out=before[:, :], in_=ones[:, :], compare_op=ALU.is_ge, fill=0.0, base=-1,
                               pattern=[[1, P]], channel_multiplier=-1).then_inc(S["const_ready"], 1)

            def rsqrt(dst, src, n, wait, count, done):
                pool.wait_ge(wait, count)
                pool.tensor_tensor(dst, src, minus_half[:, 0:n], ALU.pow).then_inc(done, 1)

            rsqrt(rs1[:, :], ms1[:, :], TILES, S["ms1_ready"], 1, S["rs1_ready"])
            pool.wait_ge(S["relT_ready"], 1)
            for b, near, far in bucket_ranges():
                last = pool.tensor_copy(bias_line[:, SEQ - 1 - far:SEQ - near],
                                        bc(relT[:, b:b + 1], [HEADS, far - near + 1]))
                last.then_inc(S["line_ready"], 1)
            rsqrt(rsqk[:, 0, :], msqk[:, 0, :], TILES * HEADS, S["msqk_ready"], 1, S["rsqk_ready"])
            rsqrt(rsqk[:, 1, :], msqk[:, 1, :], TILES * HEADS, S["msqk_ready"], 2, S["rsqk_ready"])
            for t in range(TILES):
                rsqrt(rs3[:, t:t + 1], ms3[:, t:t + 1], 1, S["ms3_ready"], t + 1, S["rs3_ready"])
            for t in range(TILES):
                rsqrt(rs2[:, t:t + 1], ms2[:, t:t + 1], 1, S["ms2_ready"], t + 1, S["rs2_ready"])
            pool.wait_ge(S["xnT_mm"], 1)
            for k in range(2):
                pool.wait_ge(S[f"split{2 * k}"], 1)
                pool.tensor_tensor(work[:, 0:2048], work[:, 0:2048],
                                   work[:, 2048 + 1024 * k:3072 + 1024 * k].bitcast(BF16), ALU.subtract
                                   ).then_inc(S[f"split{2 * k + 1}"], 1)

        @block.tensor
        def _(pe):
            conv_ps = bank[4][:, 0:CONV_BLOCKS * 8].rearrange("p (b k) -> p b k", b=CONV_BLOCKS)
            pe.wait_ge(S["const_ready"], 3)
            pe.wait_ge(small_in, 16 * 11)
            for b in range(CONV_BLOCKS):
                pe.transpose(conv_ps[:, b, 0:TAPS + 1], conv_rows[:, b * P:(b + 1) * P], ident[0:TAPS + 1, 0:TAPS + 1])
            pe.transpose(bank[4][0:HEADS, 64:64 + BUCKETS], rel_rows[:, :], ident[0:BUCKETS, 0:BUCKETS]
                         ).then_inc(S["small_mm"], 1)
            for t in range(TILES):
                pe.wait_ge(S["xscaled"], t + 1)
                for c in range(DC):
                    mm = pe.transpose(bank[c // 2][:, (c % 2) * SEQ + t * P:(c % 2) * SEQ + (t + 1) * P],
                                      x_scaled[:, t, c, :], ident[:, :])
            mm.then_inc(S["xT_mm"], 1)

            pe.wait_ge(S["xT_ready"], DC // 2)
            pe.wait_ge(wxbc_in, 16)
            for b in range(CONV_BLOCKS):
                for c in range(DC):
                    mm = pe.matmul(bank[5 + b // 2][:, (b % 2) * SEQ:(b % 2 + 1) * SEQ],
                                   wxbc_sb[:, c, b * P:(b + 1) * P], xT[:, c, :], start=(c == 0), stop=(c == DC - 1))
                if b % 2:
                    mm.then_inc(S["xbc_mm"], 1)
            pe.wait_ge(S["small_ready"], 1)
            for t in range(TILES):
                for c in range(DC):
                    mm = pe.matmul(bank[4][:, t * HEADS:(t + 1) * HEADS], xT[:, c, t * P:(t + 1) * P],
                                   wxbc_sb[:, c, CONV_CH:XBC_COLS], start=(c == 0), stop=(c == DC - 1))
            mm.then_inc(S["dt_mm"], 1)

            def project(dst, w, t, done):
                for c in range(DC):
                    mm = pe.matmul(dst[:, :], xT[:, c, t * P:(t + 1) * P], w[:, c, :], start=(c == 0), stop=(c == DC - 1))
                mm.then_inc(done, 1)

            pe.wait_ge(wq_in, 16)
            for t in range(TILES):
                project(bank[t], wq_sb, t, S["q_mm"])
            pe.wait_ge(wk_in, 16)
            for t in range(TILES):
                project(bank[2 + t], wk_sb, t, S["k_mm"])
            pe.wait_ge(S["adt_ready"], 1)
            pe.matmul(bank[4][:, 0:TILES * HEADS], upto[:, :], a_dt[:, :, :].rearrange("p t h -> p (t h)"),
                      start=True, stop=True).then_inc(S["acs_mm"], 1)
            pe.wait_ge(wv_in, 16)
            for t in range(TILES):
                pe.wait_ge(S["raw_ready"], t + 1)
                project(bank[5 + t], wv_sb, t, S["v_mm"])

            for t in range(TILES):
                if t == 0:
                    pe.wait_ge(S["raw_ready"], 3)
                    pe.wait_ge(S["convsilu"], 3)
                else:
                    pe.wait_ge(S["v_ready"], 1)
                for b in range(XS_BLOCKS):
                    mm = pe.transpose((bank[7] if t == 0 else bank[5])[:, b * P:(b + 1) * P],
                                      conv[:, b, t * P:(t + 1) * P], ident[:, :])
                mm.then_inc(S["xs_mm"], 1)
            pe.wait_ge(S["acs_ready"], 1)
            pe.transpose(bank[4][:, P:2 * P], conv[:, B_BLOCK, 0:P], ident[:, :])
            pe.wait_ge(S["v_ready"], 2)
            for t in range(TILES):
                for g in range(GROUPS):
                    rows = slice(g * STATE, (g + 1) * STATE)
                    mm = pe.matmul(bank[6 - 2 * g][:, (GROUPS + t) * P:(GROUPS + t + 1) * P],
                                   conv[rows, B_BLOCK, t * P:(t + 1) * P], conv[rows, C_BLOCK, t * P:(t + 1) * P],
                                   start=True, stop=True)
            mm.then_inc(S["cb_mm"], 1)
            pe.wait_ge(S["qk_ready"], 2 * TILES)
            for t in range(TILES):
                pe.wait_ge(S["ab_ready"], t + 1)
                for h in range(HEADS):
                    mm = pe.matmul(bank[2 * t + h // 4][:, (h % 4) * P:(h % 4 + 1) * P], a_bcast[:, h, :], upto[:, :],
                                   start=True, stop=True)
                mm.then_inc(S["rowcs_mm"], 1)
            for w in range(2):
                if w == 0:
                    pe.wait_ge(S["btok_ready"], 1)
                    pe.wait_ge(S["cb_ready"], GROUPS)
                    pe.wait_ge(S["xdt_ready"], TILES * 2)
                for b in range(XS_BLOCKS):
                    for t in range(TILES):
                        at = (b % 2) * SEQ + t * P
                        mm = pe.transpose(bank[4 + 2 * w + b // 2][:, at:at + P], qk_tok[:, w, t, b * P:(b + 1) * P],
                                          ident[:, :])
                mm.then_inc(S["qkT_mm"], 1)

            def scores(h):
                b, rows, dst = h // 2, slice((h % 2) * HD, (h % 2 + 1) * HD), bank[4 + h % 2]
                pe.wait_ge(S["qT_ready"], 2)
                pe.wait_ge(S["kT_ready"], 2)
                if h >= 2:
                    pe.wait_ge(S["score_ready"], h - 1)
                pe.matmul(dst[:, 0:SEQ], qkT[rows, 0, b, P:SEQ], qkT[rows, 1, b, :], start=True, stop=True)
                pe.matmul(dst[:, SEQ:SEQ + P], qkT[rows, 0, b, 0:P], qkT[rows, 1, b, 0:P],
                          start=True, stop=True).then_inc(S["score_mm"], 1)

            def turn_probs(h):
                pe.wait_ge(S["prob_ready"], h + 1)
                if h >= 2:
                    pe.wait_ge(S["probT_ready"], h - 1)
                for j in range(3):
                    mm = pe.transpose(bank[6 + h % 2][:, j * P:(j + 1) * P], prob[:, h % 4, j * P:(j + 1) * P], ident[:, :])
                mm.then_inc(S["probT_mm"], 1)

            def weigh_values(h):
                pe.wait_ge(S["probT_ready"], h + 1)
                cols = slice(h * HD, (h + 1) * HD)
                pT = probT[:, h % 2, :]
                pe.matmul(bank[2][:, cols], pT[:, 2 * P:3 * P], v_tok[:, 0, cols], start=True, stop=True)
                pe.matmul(bank[3][:, cols], pT[:, 0:P], v_tok[:, 0, cols], start=True, stop=False)
                pe.matmul(bank[3][:, cols], pT[:, P:2 * P], v_tok[:, 1, cols], start=False, stop=True
                          ).then_inc(S["pv_mm"], 1)

            pe.wait_ge(wz_in, 16)
            pe.wait_ge(S["decay_lin"], TILES * HEADS)
            pe.wait_ge(S["dend_lin"], 1)
            scores(0)
            scores(1)
            for h in range(HEADS):
                for k in (2 * h, 2 * h + 1):
                    t, c = k // DC, k % DC
                    mm = pe.matmul(bank[t][:, :], xT[:, c, t * P:(t + 1) * P], wz_sb[:, c, :],
                                   start=(c == 0), stop=(c == DC - 1))
                if h == HEADS - 1:
                    mm.then_inc(S["z_mm"], 1)
                if h + 2 < HEADS:
                    scores(h + 2)
                turn_probs(h)
                if h >= 1:
                    weigh_values(h - 1)
            weigh_values(HEADS - 1)

            pe.wait_ge(S["mix_ready"], 2 * TILES)
            pe.wait_ge(S["score_ready"], HEADS)
            for t in range(TILES):
                for h in range(HEADS):
                    cols = slice(h * HD, (h + 1) * HD)
                    mm = pe.matmul(bank[4 + t][:, cols], decay_mat[:, t, h, :], xdt[:, t, cols], start=True, stop=True)
                if t == 0:
                    mm.then_inc(S["ydiag_mm"], 1)
                    pe.wait_ge(S["xdec_ready"], 1)
                    pe.wait_ge(S["probT_ready"], HEADS)
                    pe.matmul(bank[6][:, :], b_tok[:, :], xdt[:, 0, :], start=True, stop=True).then_inc(S["state_mm"], 1)
                else:
                    mm.then_inc(S["ydiag_mm"], 1)
            pe.wait_ge(S["state_ready"], GROUPS)
            for g in range(GROUPS):
                rows = slice(g * STATE, (g + 1) * STATE)
                mm = pe.matmul(bank[7 - g][:, g * HPG * HD:(g + 1) * HPG * HD], conv[rows, C_BLOCK, P:SEQ],
                               state_sb[rows, :], start=True, stop=True)
            mm.then_inc(S["yoff_mm"], 1)

            for src, base, dst, ready in ((y_att, XS_BLOCKS, 2, S["yatt_ready"]), (y_ssd, 0, 6, S["yssd_ready"])):
                for t in range(TILES):
                    pe.wait_ge(ready, TILES if base else t + 1)
                    if not base and t == 0:
                        pe.wait_ge(S["state_ready"], GROUPS)
                    for b in range(XS_BLOCKS):
                        mm = pe.transpose(bank[dst + t][:, b * P:(b + 1) * P], src[:, t, b * P:(b + 1) * P], ident[:, :])
                    mm.then_inc(S["mixT_mm"], 1)

            pe.wait_ge(wout_in, 16)
            pe.wait_ge(S["zsilu_ready"], TILES)
            pe.wait_ge(S["mixT_ready"], TILES)
            order = list(range(XS_BLOCKS, DC)) + list(range(XS_BLOCKS))
            for t in range(TILES):
                for k, c in enumerate(order):
                    if k == XS_BLOCKS:
                        pe.wait_ge(S["mixT_ready"], TILES + t + 1)
                    for n in range(2):
                        mm = pe.matmul(bank[(0, 1, 4, 5)[2 * t + n]][:, :], mixT[:, c, t * P:(t + 1) * P],
                                       wout_sb[:, c, n * HALF:(n + 1) * HALF], start=(k == 0), stop=(k == DC - 1))
                        if k == DC - 1:
                            mm.then_inc(S["wout_mm"], 1)
            pe.wait_ge(S["mixT_ready"], 2 * TILES)
            for t in range(TILES):
                pe.wait_ge(S["xn_ready"], t + 1)
                for c in range(DC):
                    at = (c % 2) * SEQ + t * P
                    mm = pe.transpose(bank[(2, 3, 6, 7)[c // 2]][:, at:at + P], xn[:, t, c, :], ident[:, :])
            mm.then_inc(S["xnT_mm"], 1)
            pe.wait_ge(S["wr_ready"], 2)
            pe.wait_ge(S["xnT_ready"], DC // 2)
            pe.wait_ge(S["h_ready"], 2 * TILES)
            for t in range(TILES):
                for c in range(DC):
                    mm = pe.matmul(bank[0][:, t * ROUTES:(t + 1) * ROUTES], xnT[:, c, t * P:(t + 1) * P], wr_sb[:, c, :],
                                   start=(c == 0), stop=(c == DC - 1))
            mm.then_inc(S["logit_mm"], 1)
            pe.wait_ge(S["chosen_ready"], 1)
            pe.matmul(bank[1][:, 0:EXPERTS], before[:, :], chosen[:, 0, :], start=True, stop=True)
            pe.matmul(bank[1][:, EXPERTS:2 * EXPERTS], ones[:, :], chosen[:, 0, :], start=True, stop=False)
            pe.matmul(bank[1][:, EXPERTS:2 * EXPERTS], before[:, :], chosen[:, 1, :], start=False, stop=True)
            pe.matmul(bank[1][:, 2 * EXPERTS:3 * EXPERTS], ones[:, :], chosen[:, 0, :], start=True, stop=False)
            pe.matmul(bank[1][:, 2 * EXPERTS:3 * EXPERTS], ones[:, :], chosen[:, 1, :], start=False, stop=True
                      ).then_inc(S["rank_mm"], 1)
            total = [bank[4 + i] for i in range(4)]
            for i in range(4):
                for j in range(4):
                    pe.matmul(total[i][:, j * P:(j + 1) * P], zeros[0:32, :], zeros[0:32, :],
                              start=(j == 0), stop=False, skip_group_check=True)

            xe_ps = bank[0][:, :].rearrange("p (c k) -> p c k", c=DC)

            def gather():
                for c in range(DC):
                    for k in range(3):
                        for t in range(TILES):
                            mm = pe.matmul(xe_ps[:, c, :], xn_parts[k][:, t, c, :], sel[:, t, :],
                                           start=(k == 0 and t == 0), stop=(k == 2 and t == TILES - 1))
                return mm

            def unit(u, parity, before_last=None):
                for j in range(UNIT):
                    c = (u * UNIT + j) % DC
                    for part in range(2):
                        if before_last is not None and j == UNIT - 1 and part == 1:
                            pe.wait_ge(*before_last)
                        mm = pe.matmul(bank[u // (UNITS // 2)][:, :], xe_split[:, parity, c, :], w_split[:, u % 2, part, j, :],
                                       start=(c == 0 and part == 0), stop=(c == DC - 1 and part == 1))
                return mm

            def turn_hidden():
                for m in range(HC):
                    mm = pe.transpose(bank[1][:, m * CAP:(m + 1) * CAP], hid_sb[:, m * P:(m + 1) * P], ident[0:CAP, 0:CAP])
                return mm

            def down(k, w, parity):
                n, c = k // HC, k % HC
                return pe.matmul(bank[2 + n][parity * CAP:(parity + 1) * CAP, :], hidT_sb[:, c, :],
                                 w[:, c, n * HALF:(n + 1) * HALF], start=(c == 0), stop=(c == HC - 1))

            def turn_selection():
                for t in range(TILES):
                    mm = pe.transpose(bank[2][:, t * P:(t + 1) * P], gsel[:, t, :, :].rearrange("p w k -> p (w k)"), ident[:, :])
                return mm

            def scatter():
                for t in range(TILES):
                    for n in range(2):
                        mm = pe.matmul(total[2 * t + n][:, :], gselT_sb[:, t, :], y_sb[:, n * HALF:(n + 1) * HALF],
                                       start=False, stop=False, skip_group_check=True)
                return mm

            def downs(e, s, turn, parity, ks, e_first=False, st_turns=None):
                for k in ks:
                    if k == 0:
                        pe.wait_ge(wd_in[s], 16 * (turn + 1))
                        if st_turns is not None:
                            pe.wait_ge(S["st_ready"], st_turns)
                        if not e_first:
                            pe.wait_ge(S["y0_ready"], e)
                        pe.wait_ge(S["hidT_ready"], e + 1)
                    if k == HC and not e_first:
                        pe.wait_ge(S["y1_ready"], e)
                    mm = down(k, wd_sb[s], parity)
                    if k == HC - 1:
                        mm.then_inc(S["y0_mm"], 1)
                mm.then_inc(S["y_mm"], 1) if ks[-1] == 2 * HC - 1 else None

            def expert(e, s, turn, parity, first, second, pair):
                before_s = (s - 1) % SLOTS
                before_turn = turn if s else turn - 1
                for u in range(UNITS):
                    if u == 0:
                        pe.wait_ge(S["xe_ready"], e + 1)
                    if u == UNITS // 2 and not first:
                        pe.wait_ge(S["hidT_ready"], e)
                    pe.wait_ge(S["wlo_ready"], e * UNITS + (u + 1))
                    hidden = (S["hid_ready"], e) if u == 1 and not first else None
                    unit(u, parity, hidden).then_inc(S["unit_mm"], 1)
                    if u == 1 and not first:
                        turn_hidden().then_inc(S["hidT_mm"], 1)
                        if parity and not second:
                            pe.wait_ge(S["y1_ready"], e - 1)
                            pe.wait_ge(S["y0_ready"], e - 1)
                            pe.wait_ge(S["st_ready"], pair)
                            scatter().then_inc(S["scat_mm"], 1)
                    if u == UNITS - 2:
                        pe.wait_ge(S["sel_ready"], e + 2)
                        pe.wait_ge(S["gsum_ready"], e + 1)
                        gather().then_inc(S["xe_mm"], 1)
                    if u >= 2 and not first:
                        downs(e - 1, before_s, before_turn, 1 - parity, [u - 2], e_first=second,
                              st_turns=None if (not parity or second) else pair)
                if not first:
                    downs(e - 1, before_s, before_turn, 1 - parity, [UNITS - 2, UNITS - 1])
                    if not parity:
                        pe.wait_ge(S["gsel_ready"], pair)
                        pe.wait_ge(S["y0_ready"], e)
                        turn_selection().then_inc(S["st_mm"], 1)

            pe.wait_ge(S["most_ready"], 1)
            most_tokens = pe.value_load(most_int[0:1, 0:1], min_val=0, max_val=SEQ)
            pe.wait_ge(S["split4"], 1)
            pe.wait_ge(S["sel_ready"], 1)
            gather().then_inc(S["xe_mm"], 1)
            for e in range(PEELED):
                expert(e, e, 0, e, e == 0, e == 1, 0)
            with pe.Fori(0, EXPERTS // BODY) as i:
                for j in range(BODY):
                    k = PEELED + j
                    expert(i * BODY + k, k % SLOTS, i * 2 + k // SLOTS, k % 2, False, False, i * SLOTS + k // 2)
            last = EXPERTS - 1
            pe.wait_ge(S["hid_ready"], last + 1)
            turn_hidden().then_inc(S["hidT_mm"], 1)
            downs(last, last % SLOTS, last // SLOTS, 1, list(range(2 * HC)))
            pe.wait_ge(S["gsel_ready"], EXPERTS // 2)
            pe.wait_ge(S["y0_ready"], EXPERTS)
            turn_selection().then_inc(S["st_mm"], 1)
            pe.wait_ge(S["y1_ready"], EXPERTS)
            pe.wait_ge(S["st_ready"], EXPERTS // 2)
            scatter().then_inc(S["scat_mm"], 1)

            with pe.If(most_tokens > CAP):
                with pe.Fori(0, ROUNDS - 1) as r:
                    with pe.Fori(0, EXPERTS) as e:
                        n = r * EXPERTS + e
                        m = n + EXPERTS
                        pe.wait_ge(S["o_sel"], n + 1)
                        gather().then_inc(S["o_xe"], 1)
                        pe.wait_ge(S["o_xs"], n + 1)
                        for u in range(UNITS):
                            pe.wait_ge(S["wlo_ready"], m * UNITS + (u + 1))
                            unit(u, 0).then_inc(S["unit_mm"], 1)
                        pe.wait_ge(S["hid_ready"], m + 1)
                        pe.matmul(bank[0][:, 0:P], zeros[0:32, :], zeros[0:32, :], start=True, stop=True)
                        turn_hidden().then_inc(S["hidT_mm"], 1)
                        pe.wait_ge(S["hidT_ready"], m + 1)
                        for k in range(2 * HC):
                            mm = down(k, wd_sb[0], 0)
                        mm.then_inc(S["y_mm"], 1)
                        pe.wait_ge(S["y0_ready"], m + 1)
                        turn_selection().then_inc(S["o_st"], 1)
                        pe.wait_ge(S["o_stsb"], n + 1)
                        pe.wait_ge(S["y1_ready"], m + 1)
                        scatter().then_inc(S["o_scat"], 1)
            pe.matmul(bank[0][:, 0:P], zeros[0:32, :], zeros[0:32, :], start=True, stop=True).then_inc(S["moe_done"], 1)

        @block.scalar
        def _(act):
            steps = [0]

            def link(ins):
                steps[0] += 1
                ins.then_inc(S["act_step"], 1)
                act.wait_ge(S["act_step"], steps[0])

            def row(v):
                return v.rearrange("l n -> (l n)").partition_broadcast(P)

            for dst, src in ((conv_rows[0:TAPS, :], conv_w.rearrange("l k n -> (l k) n")),
                             (conv_rows[TAPS:TAPS + 1, :], conv_b), (rel_rows[:, :], rel_bias),
                             (g1_col[:, :], norm1_g.rearrange("l (p c) -> p (l c)", c=DC)),
                             (qg_col[0:HD, :], q_norm_g.rearrange("l n -> n l")),
                             (qg_col[HD:P, :], q_norm_g.rearrange("l n -> n l")),
                             (kg_col[0:HD, :], k_norm_g.rearrange("l n -> n l")),
                             (kg_col[HD:P, :], k_norm_g.rearrange("l n -> n l")),
                             (dtb_bc[:, :], row(dt_bias)), (alog_bc[:, :], row(a_log)), (dskip_bc[:, :], row(d_skip))):
                act.dma_start(dst, src).then_inc(small_in, 16)
            for dst, src in ((ssdg_bc[:, :], row(ssd_norm_g)), (g2_bc[:, :], row(norm2_g)),
                             (br_bc[:, 0:MOE_GROUPS], row(b_r1)), (br_bc[:, MOE_GROUPS:ROUTES], row(b_r2)),
                             (wr1_sb[:, :, :], w_r1.rearrange("l (p c) n -> p (l c) n", c=DC)),
                             (wr2_sb[:, :, :], w_r2.rearrange("l (p c) n -> p (l c) n", c=DC))):
                act.dma_start(dst, src).then_inc(late_in, 16)

            act.wait_ge(x_in, 16)
            act.activation(conv[:, 0:4, :].rearrange("p b t -> p (b t)"), h_sb[:, 1, :], ACT.Square,
                           accum_out=ms1[:, 1:2]).then_inc(S["ms1_act"], 1)
            act.wait_ge(S["zero_ready"], 1)
            for i in range(3):
                act.wait_ge(S["xbc_mm"], i + 1)
                act.copy(raw[:, 2 * i:2 * i + 2, TAPS - 1:RAWW], bank[5 + i][:, :].rearrange("p (b t) -> p b t", b=2)
                         ).then_inc(S["raw_ready"], 1)
            act.wait_ge(S["dtabs_ready"], 1)
            act.activation(dt_exp[:, :, :], dt_abs[:, :, :], ACT.Exp, scale=-1.0)
            act.wait_ge(small_in, 16 * 11)
            link(act.activation(a_exp[:, :], alog_bc[:, :], ACT.Exp))
            act.activation(dt_log[:, :, :], dt_exp[:, :, :], ACT.Ln, bias=ones[:, 0:1]).then_inc(S["dtlog_ready"], 1)
            for w, done in ((0, S["q_mm"]), (1, S["k_mm"])):
                for t in range(TILES):
                    act.wait_ge(done, t + 1)
                    act.activation(squares[:, w, t, :], bank[2 * w + t][:, :], ACT.Square).then_inc(S["squares_ready"], 1)
            for i in range(3):
                act.wait_ge(S["conv_ready"], 2 * i + 2)
                act.activation(conv[:, 2 * i:2 * i + 2, :], conv[:, 2 * i:2 * i + 2, :], ACT.Silu).then_inc(S["convsilu"], 1)
            for t in range(TILES):
                act.wait_ge(S["v_mm"], t + 1)
                act.copy(v_tok[:, t, :], bank[5 + t][:, :]).then_inc(S["v_ready"], 1)
            for t in range(TILES):
                act.wait_ge(S["adt_ready"], 1)
                if t:
                    act.wait_ge(S["rowcs_mm"], t)
                act.copy(a_bcast, bc(a_dt[:, t, :].unsqueeze(2), [P, HEADS, P])).then_inc(S["ab_ready"], 1)
            act.wait_ge(S["acs_ready"], 1)
            act.activation(decay_in[:, :], a_cs[:, 1, :], ACT.Exp)
            act.wait_ge(S["dend_lin"], 1)
            act.activation(decay_end[:, :], decay_arg[:, :], ACT.Exp).then_inc(S["dend_exp"], 1)
            for t in range(TILES):
                for g in range(GROUPS):
                    act.wait_ge(S["decay_lin"], t * HEADS + (g + 1) * HPG)
                    block4 = decay_mat[:, t, g * HPG:(g + 1) * HPG, :]
                    act.activation(block4, block4, ACT.Exp).then_inc(S["decay_exp"], 1)
            def numerators(h):
                act.wait_ge(S["negmax_ready"], h + 1)
                act.activation(prob[:, h % 4, 0:SEQ], prob[:, h % 4, 0:SEQ], ACT.Exp, bias=neg_max[:, h, 1:2],
                               accum_out=row_sum[:, h, 1:2])
                act.activation(prob[:, h % 4, SEQ:SEQ + P], prob[:, h % 4, SEQ:SEQ + P], ACT.Exp, bias=neg_max[:, h, 0:1],
                               accum_out=row_sum[:, h, 0:1]).then_inc(S["prob_ready"], 1)

            def keep_turned(h):
                act.wait_ge(S["probT_mm"], h + 1)
                if h >= 2:
                    act.wait_ge(S["pv_mm"], h - 1)
                act.copy(probT[:, h % 2, :], bank[6 + h % 2][:, 0:3 * P]).then_inc(S["probT_ready"], 1)

            for h in range(HEADS + 1):
                if h < HEADS:
                    numerators(h)
                if h >= 1:
                    keep_turned(h - 1)
            act.wait_ge(S["z_mm"], 1)
            act.wait_ge(S["score_ready"], HEADS)
            for t in range(TILES):
                act.activation(z_silu[:, t, :], bank[t][:, :], ACT.Silu).then_inc(S["zsilu_ready"], 1)
            for i in range(2 * TILES):
                t = i % TILES
                act.wait_ge(S["mixT_mm"], i + 1)
                blocks = slice(XS_BLOCKS, DC) if i < TILES else slice(0, XS_BLOCKS)
                act.copy(mixT[:, blocks, t * P:(t + 1) * P],
                         bank[(2 if i < TILES else 6) + t][:, :].rearrange("p (b t) -> p b t", b=XS_BLOCKS)
                         ).then_inc(S["mixT_ready"], 1)
            for t in range(TILES):
                act.wait_ge(S["h_ready"], 2 * t + 2)
                act.activation(work[:, 4096:5120], h_sb[:, t, :], ACT.Square, accum_out=ms2[:, t:t + 1]
                               ).then_inc(S["ms2_act"], 1)
            act.wait_ge(S["xnT_mm"], 1)
            for i in (0, 1):
                act.copy(xnT[:, 2 * i:2 * i + 2, :], bank[(2, 3)[i]][:, :].rearrange("p (c t) -> p c t", c=2)
                         ).then_inc(S["xnT_ready"], 1)
            act.wait_ge(S["xn_ready"], TILES)
            for k in range(3):
                if k:
                    act.wait_ge(S[f"split{2 * k - 1}"], 1)
                act.copy(work[:, 2048 + 1024 * k:3072 + 1024 * k].bitcast(BF16), work[:, 0:2048]
                         ).then_inc(S[f"split{2 * k}"], 1)
            act.wait_ge(S["gexp_in"], 1)
            act.activation(gexp[:, :, :], gexp[:, :, :], ACT.Exp).then_inc(S["gexp_ready"], 1)
            act.wait_ge(S["share_in"], 1)
            act.activation(share[:, 0, :], share[:, 0, :], ACT.Exp).then_inc(S["share_ready"], 1)

            xe_ps = bank[0][:, :].rearrange("p (c k) -> p c k", c=DC)

            def high_part(u, s):
                w = (wg_sb, wu_sb)[u // (UNITS // 2)][s]
                c = (u * UNIT) % DC
                return act.copy(w_split[:, u % 2, 0, :, :], w[:, c:c + UNIT, :])

            def high_weights(e, s, turn, u, first=False):
                if u % (UNITS // 2) == 0:
                    act.wait_ge((wg_in, wu_in)[u // (UNITS // 2)][s], 16 * (turn + 1))
                if not (first and u < 2):
                    act.wait_ge(S["unit_mm"], e * UNITS + (u - 1))
                high_part(u, s).then_inc(S["whi_ready"], 1)

            def high_tokens(e, parity):
                act.wait_ge(S["xe_mm"], e + 1)
                act.copy(xe_split[:, parity, :, 0:CAP], xe_ps).then_inc(S["xh_ready"], 1)

            def low_rows(src):
                return act.copy(low_sb, bank[src][CAP:P, :])

            def keep_hidden():
                return act.copy(hidT_sb, bank[1][:, 0:HC * CAP].rearrange("p (m k) -> p m k", m=HC))

            def keep_y0(e, parity):
                act.wait_ge(S["y0_mm"], e + 1)
                rows = slice(parity * CAP, (parity + 1) * CAP)
                act.copy(y_sb[rows, 0:HALF], bank[2][rows, :]).then_inc(S["y0_ready"], 1)

            def up_low(e):
                act.wait_ge(S["unit_mm"], e * UNITS + UNITS)
                act.wait_ge(S["gsum_ready"], e + 1)
                low_rows(1).then_inc(S["ulow_ready"], 1)

            def turned(e, first):
                act.wait_ge(S["hidT_mm"], e + 1)
                if not first:
                    act.wait_ge(S["y_mm"], e)
                keep_hidden().then_inc(S["hidT_ready"], 1)

            def expert(e, s, turn, parity, first, second):
                for u in range(UNITS):
                    high_weights(e, s, turn, u, first)
                    if u == 0 and not first:
                        up_low(e - 1)
                    if u == 2 and not first:
                        turned(e - 1, second)
                    if u == 5:
                        act.wait_ge(S["unit_mm"], e * UNITS + UNITS // 2)
                        if not first:
                            act.wait_ge(S["hid_ready"], e)
                        low_rows(0).then_inc(S["glow_ready"], 1)
                        act.wait_ge(S["gsum_ready"], e + 1)
                        act.activation(silu_sb, silu_sb, ACT.Silu).then_inc(S["silu_ready"], 1)
                    if u == 6 and not first:
                        keep_y0(e - 1, 1 - parity)
                high_tokens(e + 1, 1 - parity)

            act.wait_ge(S["most_ready"], 1)
            most_tokens = act.value_load(most_int[0:1, 0:1], min_val=0, max_val=SEQ)
            act.wait_ge(S["logit_mm"], 1)
            high_tokens(0, 0)
            expert(0, 0, 0, 0, True, False)
            expert(1, 1, 0, 1, False, True)
            with act.Fori(0, EXPERTS // BODY) as i:
                for j in range(BODY):
                    k = PEELED + j
                    expert(i * BODY + k, k % SLOTS, i * 2 + k // SLOTS, k % 2, False, False)
            up_low(EXPERTS - 1)
            turned(EXPERTS - 1, False)
            keep_y0(EXPERTS - 1, 1)

            with act.If(most_tokens > CAP):
                with act.Fori(0, (ROUNDS - 1) * EXPERTS) as n:
                    m = n + EXPERTS
                    act.wait_ge(S["o_xe"], n + 1)
                    act.copy(xe_split[:, 0, :, 0:CAP], xe_ps).then_inc(S["o_xh"], 1)
                    act.wait_ge(S["o_w"], (n + 1) * 48)
                    for u in range(UNITS):
                        if u >= 2:
                            act.wait_ge(S["unit_mm"], m * UNITS + (u - 1))
                        high_part(u, 0).then_inc(S["whi_ready"], 1)
                        if u == 5:
                            act.wait_ge(S["unit_mm"], m * UNITS + UNITS // 2)
                            low_rows(0).then_inc(S["glow_ready"], 1)
                            act.wait_ge(S["gsum_ready"], m + 1)
                            act.activation(silu_sb, silu_sb, ACT.Silu).then_inc(S["silu_ready"], 1)
                    act.wait_ge(S["unit_mm"], m * UNITS + UNITS)
                    low_rows(1).then_inc(S["ulow_ready"], 1)
                    act.wait_ge(S["hidT_mm"], m + 1)
                    keep_hidden().then_inc(S["hidT_ready"], 1)
                    act.wait_ge(S["y_mm"], m + 1)
                    act.copy(y_sb[0:CAP, 0:HALF], bank[2][0:CAP, :]).then_inc(S["y0_ready"], 1)
            act.nop()

        @block.vector
        def _(dve):
            steps = [0]

            def link(ins):
                steps[0] += 1
                ins.then_inc(S["dve_step"], 1)
                dve.wait_ge(S["dve_step"], steps[0])

            def mean(ap, n):
                return dve.tensor_scalar(ap, ap, 1.0 / n, EPS, ALU.mult, ALU.add)

            dve.memset(raw[:, :, 0:TAPS - 1], 0.0).then_inc(S["zero_ready"], 1)
            dve.wait_ge(x_in, 16)
            link(dve.tensor_tensor_reduce(xT[:, 0:4, :].rearrange("p c t -> p (c t)"), h_sb[:, 0, :], h_sb[:, 0, :], 1.0, 0.0,
                                          ALU.mult, ALU.add, ms1[:, 0:1]))
            dve.wait_ge(S["ms1_act"], 1)
            mean(ms1[:, :], D).then_inc(S["ms1_ready"], 1)
            dve.wait_ge(S["small_mm"], 1)
            dve.tensor_copy(relT[:, :], bank[4][0:HEADS, 64:64 + BUCKETS]).then_inc(S["relT_ready"], 1)
            dve.tensor_copy(conv_cols[:, :, :], bank[4][:, 0:CONV_BLOCKS * 8].rearrange("p (b k) -> p b k", b=CONV_BLOCKS)
                            [:, :, 0:TAPS + 1]).then_inc(S["small_ready"], 1)
            dve.wait_ge(S["rs1_ready"], 1)
            for t in range(TILES):
                dve.tensor_scalar(front[:, 3584 + t * D:3584 + (t + 1) * D], h_sb[:, t, :], rs1[:, t:t + 1], None, ALU.mult
                                  ).then_inc(S["xscaled"], 1)
            dve.tensor_tensor(qkg_col[:, :], qg_col[:, :], kg_col[:, :], ALU.mult).then_inc(S["qkg_ready"], 1)
            dve.wait_ge(S["xT_mm"], 1)
            for i in range(DC // 2):
                dve.tensor_tensor(xT[:, 2 * i:2 * i + 2, :], bank[i][:, :].rearrange("p (c t) -> p c t", c=2),
                                  bc(g1_col[:, 2 * i:2 * i + 2].unsqueeze(2), [P, 2, SEQ]), ALU.mult
                                  ).then_inc(S["xT_ready"], 1)
            dve.wait_ge(S["small_ready"], 1)
            def convolve(b):
                if b % 2 == 0:
                    dve.wait_ge(S["raw_ready"], b // 2 + 1)
                link(dve.tensor_scalar(conv[:, b, :], raw[:, b, 0:SEQ], conv_cols[:, b, 0:1], conv_cols[:, b, TAPS:TAPS + 1],
                                       ALU.mult, ALU.add))
                for k in range(1, TAPS):
                    ins = dve.scalar_tensor_tensor(conv[:, b, :], raw[:, b, k:k + SEQ], conv_cols[:, b, k:k + 1], conv[:, b, :],
                                                   ALU.mult, ALU.add)
                    if k < TAPS - 1:
                        link(ins)
                    else:
                        ins.then_inc(S["conv_ready"], 1)

            for b in range(CONV_BLOCKS):
                convolve(b)
            dve.wait_ge(S["dt_mm"], 1)
            link(dve.tensor_tensor(dt_lin[:, :, :], bank[4][:, 0:TILES * HEADS].rearrange("p (t h) -> p t h", t=TILES),
                                   bc(dtb_bc[:, :].unsqueeze(1), [P, TILES, HEADS]), ALU.add))
            dve.scalar_tensor_tensor(dt_abs[:, :, :], dt_lin[:, :, :], -1.0, dt_lin[:, :, :], ALU.mult, ALU.max
                                     ).then_inc(S["dtabs_ready"], 1)
            dve.wait_ge(S["dtlog_ready"], 1)
            link(dve.scalar_tensor_tensor(dt_sb[:, :, :], dt_lin[:, :, :], 0.0, dt_log[:, :, :], ALU.max, ALU.add))
            dve.scalar_tensor_tensor(a_dt[:, :, :], dt_sb[:, :, :], -1.0, bc(a_exp[:, :].unsqueeze(1), [P, TILES, HEADS]),
                                     ALU.mult, ALU.mult).then_inc(S["adt_ready"], 1)
            for w in range(2):
                for t in range(TILES):
                    dve.wait_ge(S["squares_ready"], 2 * w + t + 1)
                    ins = dve.tensor_reduce(msqk[:, w, t * HEADS:(t + 1) * HEADS],
                                            squares[:, w, t, :].rearrange("p (h d) -> p h d", h=HEADS), AX.X, ALU.add)
                    link(ins)
                mean(msqk[:, w, :], HD).then_inc(S["msqk_ready"], 1)
                if w == 0:
                    dve.wait_ge(S["acs_mm"], 1)
                    dve.tensor_copy(a_cs[:, :, :], bank[4][:, 0:TILES * HEADS].rearrange("p (t h) -> p t h", t=TILES)
                                    ).then_inc(S["acs_ready"], 1)
            for w in range(2):
                dve.wait_ge(S["rsqk_ready"], w + 1)
                for t in range(TILES):
                    dve.tensor_tensor(qk_tok[:, w, t, :].rearrange("p (h d) -> p h d", h=HEADS),
                                      bank[2 * w + t][:, :].rearrange("p (h d) -> p h d", h=HEADS),
                                      bc(rsqk[:, w, t * HEADS:(t + 1) * HEADS].unsqueeze(2), [P, HEADS, HD]), ALU.mult
                                      ).then_inc(S["qk_ready"], 1)
            dve.wait_ge(biasline_out, 16)
            for t in range(TILES):
                dve.wait_ge(S["xs_mm"], t + 1)
                xs_ps = (bank[7] if t == 0 else bank[5])[:, :].rearrange("p (h d) -> p h d", h=HEADS)
                for dst, by in ((xdt, dt_sb[:, t, :]), (y_ssd, dskip_bc[:, :])):
                    dve.tensor_tensor(dst[:, t, :].rearrange("p (h d) -> p h d", h=HEADS), xs_ps,
                                      bc(by.unsqueeze(2), [P, HEADS, HD]), ALU.mult).then_inc(S["xdt_ready"], 1)
            dve.wait_ge(S["cb_mm"], 1)
            dve.tensor_copy(b_tok[:, :], bank[4][:, P:2 * P]).then_inc(S["btok_ready"], 1)
            for g in range(GROUPS):
                dve.tensor_tensor(cb_sb[:, :, g, :], bank[6 - 2 * g][:, 2 * P:].rearrange("p (t l) -> p t l", t=TILES),
                                  bc(upto[:, :].unsqueeze(1), [P, TILES, P]), ALU.mult).then_inc(S["cb_ready"], 1)
            dve.wait_ge(S["qkg_ready"], 1)
            dve.wait_ge(S["qkT_mm"], 1)
            for i in range(2):
                dve.tensor_scalar(qkT[:, 0, 2 * i:2 * i + 2, :], bank[4 + i][:, :].rearrange("p (b t) -> p b t", b=2),
                                  qkg_col[:, 0:1], HD ** -0.5, ALU.mult, ALU.mult).then_inc(S["qT_ready"], 1)
            dve.wait_ge(S["qkT_mm"], 2)
            for i in range(2):
                dve.tensor_copy(qkT[:, 1, 2 * i:2 * i + 2, :], bank[6 + i][:, :].rearrange("p (b t) -> p b t", b=2)
                                ).then_inc(S["kT_ready"], 1)
            for t in range(TILES):
                dve.wait_ge(S["rowcs_mm"], t + 1)
                for h in range(HEADS):
                    dve.tensor_scalar(decay_mat[:, t, h, :], bank[2 * t + h // 4][:, (h % 4) * P:(h % 4 + 1) * P],
                                      a_cs[:, t, h:h + 1], 0.0, ALU.subtract, ALU.min).then_inc(S["decay_lin"], 1)
                if t == 0:
                    for g in range(GROUPS):
                        ins = dve.tensor_tensor(decay_arg[:, g * HPG:(g + 1) * HPG],
                                                bank[g][:, :].rearrange("p (h l) -> p h l", h=HPG)[:, :, P - 1],
                                                a_cs[:, 0, g * HPG:(g + 1) * HPG], ALU.subtract)
                        if g:
                            ins.then_inc(S["dend_lin"], 1)

            def bias_and_max(h):
                dve.wait_ge(S["score_mm"], h + 1)
                if h == 0:
                    dve.wait_ge(biastab_in, 16)
                if h >= 4:
                    dve.wait_ge(S["probT_mm"], h - 3)
                dve.tensor_tensor_reduce(prob[:, h % 4, 0:SEQ], bank[4 + h % 2][:, 0:SEQ], bias_tab[:, h, :], 1.0, LOW,
                                         ALU.add, ALU.max, row_max[:, h, 1:2])
                link(dve.tensor_tensor_reduce(prob[:, h % 4, SEQ:SEQ + P], bank[4 + h % 2][:, SEQ:SEQ + P],
                                              bias_tab[:, h, P:SEQ], 1.0, LOW, ALU.add, ALU.max, row_max[:, h, 0:1]))
                dve.tensor_scalar(neg_max[:, h, :], row_max[:, h, :], -1.0, None, ALU.mult).then_inc(S["negmax_ready"], 1)
                dve.nop().then_inc(S["score_ready"], 1)

            def mix(t, g):
                dve.wait_ge(S["decay_exp"], t * GROUPS + g + 1)
                block4 = decay_mat[:, t, g * HPG:(g + 1) * HPG, :]
                dve.tensor_tensor(block4, block4, bc(cb_sb[:, t, g, :].unsqueeze(1), [P, HPG, P]), ALU.mult
                                  ).then_inc(S["mix_ready"], 1)

            for h in range(HEADS):
                bias_and_max(h)
                if h % 2 == 1:
                    mix((h // 2) // GROUPS, (h // 2) % GROUPS)
            dve.wait_ge(S["prob_ready"], HEADS)
            link(dve.reciprocal(row_inv[:, :, :], row_sum[:, :, :]))
            dve.wait_ge(S["pv_mm"], HEADS)
            dve.wait_ge(S["z_mm"], 1)
            for t in range(TILES):
                dve.tensor_tensor(y_att[:, t, :].rearrange("p (h d) -> p h d", h=HEADS),
                                  bank[2 + t][:, :].rearrange("p (h d) -> p h d", h=HEADS),
                                  bc(row_inv[:, :, t].unsqueeze(2), [P, HEADS, HD]), ALU.mult).then_inc(S["yatt_ready"], 1)
            dve.wait_ge(S["ydiag_mm"], 1)
            link(dve.tensor_tensor(y_ssd[:, 0, :], bank[4][:, :], y_ssd[:, 0, :], ALU.add))
            dve.wait_ge(S["dend_exp"], 1)
            dve.tensor_tensor(xdt[:, 0, :].rearrange("p (h d) -> p h d", h=HEADS),
                              xdt[:, 0, :].rearrange("p (h d) -> p h d", h=HEADS),
                              bc(decay_end[:, :].unsqueeze(2), [P, HEADS, HD]), ALU.mult).then_inc(S["xdec_ready"], 1)

            def gated(t):
                dve.wait_ge(S["zsilu_ready"], t + 1)
                link(dve.tensor_tensor(y_ssd[:, t, :], y_ssd[:, t, :], z_silu[:, t, :], ALU.mult))
                link(dve.tensor_tensor_reduce(work[:, 2560:3072], y_ssd[:, t, :], y_ssd[:, t, :], 1.0, 0.0, ALU.mult, ALU.add,
                                              ms3[:, t:t + 1]))
                mean(ms3[:, t:t + 1], INNER).then_inc(S["ms3_ready"], 1)

            def normed(t):
                dve.wait_ge(late_in, 16 * 6)
                dve.wait_ge(S["rs3_ready"], t + 1)
                dve.scalar_tensor_tensor(y_ssd[:, t, :], y_ssd[:, t, :], rs3[:, t:t + 1], ssdg_bc[:, :], ALU.mult, ALU.mult
                                         ).then_inc(S["yssd_ready"], 1)

            dve.wait_ge(S["state_mm"], 1)
            for g in range(GROUPS):
                rows = slice(g * STATE, (g + 1) * STATE)
                dve.tensor_copy(state_sb[rows, :], bank[6][rows, g * HPG * HD:(g + 1) * HPG * HD]
                                ).then_inc(S["state_ready"], 1)
            gated(0)
            dve.wait_ge(S["ydiag_mm"], 2)
            dve.tensor_tensor(y_ssd[:, 1, :], bank[5][:, :], y_ssd[:, 1, :], ALU.add)
            dve.wait_ge(S["yoff_mm"], 1)
            for g in range(GROUPS):
                cols, hs = slice(g * HPG * HD, (g + 1) * HPG * HD), slice(g * HPG, (g + 1) * HPG)
                link(dve.tensor_tensor(y_off[:, cols].rearrange("p (h d) -> p h d", h=HPG),
                                       bank[7 - g][:, cols].rearrange("p (h d) -> p h d", h=HPG),
                                       bc(decay_in[:, hs].unsqueeze(2), [P, HPG, HD]), ALU.mult))
            link(dve.tensor_tensor(y_ssd[:, 1, :], y_ssd[:, 1, :], y_off, ALU.add))
            normed(0)
            gated(1)
            normed(1)
            dve.tensor_copy(wr_sb[:, :, 0:MOE_GROUPS], wr1_sb[:, :, :]).then_inc(S["wr_ready"], 1)
            dve.tensor_copy(wr_sb[:, :, MOE_GROUPS:ROUTES], wr2_sb[:, :, :]).then_inc(S["wr_ready"], 1)
            for t in range(TILES):
                for n in range(2):
                    dve.wait_ge(S["wout_mm"], 2 * t + n + 1)
                    cols = slice(n * HALF, (n + 1) * HALF)
                    dve.tensor_tensor(h_sb[:, t, cols], bank[(0, 1, 4, 5)[2 * t + n]][:, :], h_sb[:, t, cols], ALU.add
                                      ).then_inc(S["h_ready"], 1)
                dve.wait_ge(S["ms2_act"], t + 1)
                mean(ms2[:, t:t + 1], D).then_inc(S["ms2_ready"], 1)
                dve.wait_ge(S["rs2_ready"], t + 1)
                dve.scalar_tensor_tensor(xn[:, t, :, :].rearrange("p c q -> p q c"),
                                         h_sb[:, t, :].rearrange("p (q c) -> p q c", c=DC), rs2[:, t:t + 1],
                                         g2_bc[:, :].rearrange("p (q c) -> p q c", c=DC), ALU.mult, ALU.mult
                                         ).then_inc(S["xn_ready"], 1)
            dve.wait_ge(S["xnT_mm"], 1)
            for i in (2, 3):
                dve.tensor_copy(xnT[:, 2 * i:2 * i + 2, :], bank[(2, 3, 6, 7)[i]][:, :].rearrange("p (c t) -> p c t", c=2)
                                ).then_inc(S["xnT_ready"], 1)

            dve.wait_ge(S["logit_mm"], 1)
            link(dve.tensor_tensor(logit[:, :, :], bank[0][:, 0:TILES * ROUTES].rearrange("p (t n) -> p t n", t=TILES),
                                   bc(br_bc[:, :].unsqueeze(1), [P, TILES, ROUTES]), ALU.add))
            l1, l2 = logit[:, :, 0:MOE_GROUPS], logit[:, :, MOE_GROUPS:ROUTES]

            def first_highest(hot, eq, values, high, n):
                link(dve.tensor_reduce(high, values, AX.X, ALU.max))
                link(dve.tensor_tensor(eq, values, bc(high.unsqueeze(2), [P, TILES, n]), ALU.is_equal))
                link(dve.scalar_tensor_tensor(eq, eq, -float(P), bc(expert_iota[:, 0:n].unsqueeze(1), [P, TILES, n]),
                                              ALU.mult, ALU.add))
                link(dve.tensor_reduce(low_at[:, :], eq, AX.X, ALU.min))
                link(dve.tensor_tensor(hot, eq, bc(low_at[:, :].unsqueeze(2), [P, TILES, n]), ALU.is_equal))

            first_highest(ghot[:, :, :], eq4[:, :, :], l1, top[:, 0, :], MOE_GROUPS)
            dve.tensor_tensor(gexp[:, :, :], l1, bc(top[:, 0, :].unsqueeze(2), [P, TILES, MOE_GROUPS]), ALU.subtract
                              ).then_inc(S["gexp_in"], 1)
            link(dve.tensor_scalar(ghot[:, :, :], ghot[:, :, :], -LOW, LOW, ALU.mult, ALU.add))
            link(dve.tensor_tensor(masked[:, :, :].rearrange("p t (g k) -> p t g k", g=MOE_GROUPS),
                                   l2.rearrange("p t (g k) -> p t g k", g=MOE_GROUPS),
                                   bc(ghot[:, :, :].unsqueeze(3), [P, TILES, MOE_GROUPS, PER_GROUP]), ALU.add))
            first_highest(hot1[:, :, :], eq32[:, :, :], masked[:, :, :], top[:, 1, :], EXPERTS)
            link(dve.scalar_tensor_tensor(masked[:, :, :], hot1[:, :, :], 2 * LOW, masked[:, :, :], ALU.mult, ALU.add))
            first_highest(hot2[:, :, :], eq32[:, :, :], masked[:, :, :], top[:, 2, :], EXPERTS)
            dve.tensor_tensor(share[:, 0, :], top[:, 2, :], top[:, 1, :], ALU.subtract).then_inc(S["share_in"], 1)
            dve.tensor_tensor(chosen[:, :, :], hot1[:, :, :], hot2[:, :, :], ALU.add).then_inc(S["chosen_ready"], 1)
            dve.wait_ge(S["gexp_ready"], 1)
            link(dve.tensor_reduce(gsum[:, :], gexp[:, :, :], AX.X, ALU.add))
            dve.wait_ge(S["share_ready"], 1)
            link(dve.scalar_tensor_tensor(share[:, 1, :], share[:, 0, :], 1.0, gsum[:, :], ALU.add, ALU.mult))
            link(dve.reciprocal(share[:, 2, :], share[:, 1, :]))
            link(dve.tensor_tensor(share[:, 3, :], share[:, 2, :], share[:, 0, :], ALU.mult))
            link(dve.tensor_tensor(hot1[:, :, :], hot1[:, :, :], bc(share[:, 2, :].unsqueeze(2), [P, TILES, EXPERTS]), ALU.mult))
            link(dve.tensor_tensor(hot2[:, :, :], hot2[:, :, :], bc(share[:, 3, :].unsqueeze(2), [P, TILES, EXPERTS]), ALU.mult))
            link(dve.tensor_tensor(gates[:, :, :], hot1[:, :, :], hot2[:, :, :], ALU.add))
            dve.wait_ge(S["rank_mm"], 1)
            rank_ps = bank[1][:, 0:TILES * EXPERTS].rearrange("p (t n) -> p t n", t=TILES)
            link(dve.memset(rank[:, :, :], 0.0))
            link(dve.scalar_tensor_tensor(rank[:, :, 0:EXPERTS], rank_ps, 1.0, chosen[:, :, :], ALU.add, ALU.mult))
            link(dve.tensor_scalar(rank[:, :, :], rank[:, :, :], 1.0, None, ALU.subtract))
            link(dve.tensor_reduce(most[0:1, :], bank[1][0:1, 2 * EXPERTS:3 * EXPERTS], AX.X, ALU.max))
            dve.tensor_copy(most_int[0:1, :], most[0:1, :]).then_inc(S["most_ready"], 1)
            dve.wait_ge(S["most_ready"], 1)

            def select(e, done):
                for t in range(TILES):
                    ins = dve.tensor_scalar(sel[:, t, :], rank_iota[:, 0:CAP], rank[:, t, bass.ds(e, 1)], None, ALU.is_equal)
                ins.then_inc(done, 1)

            def select_gated(e, parity):
                for t in range(TILES):
                    ins = dve.tensor_scalar(gsel[:, t, parity, :], rank_iota[:, 0:CAP], rank[:, t, bass.ds(e, 1)],
                                            gates[:, t, bass.ds(e, 1)], ALU.is_equal, ALU.mult)
                return ins

            def low_part(u, s):
                w = (wg_sb, wu_sb)[u // (UNITS // 2)][s]
                c = (u * UNIT) % DC
                return dve.tensor_tensor(w_split[:, u % 2, 1, :, :], w[:, c:c + UNIT, :],
                                         w_split[:, u % 2, 0, :, :].bitcast(F32), ALU.subtract)

            xe_ps = bank[0][:, :].rearrange("p (c k) -> p c k", c=DC)

            def low_tokens(parity):
                return dve.tensor_tensor(xe_split[:, parity, :, CAP:P], xe_ps,
                                         xe_split[:, parity, :, 0:CAP].bitcast(F32), ALU.subtract)

            def gate_sum():
                return dve.tensor_tensor(silu_sb, bank[0][0:CAP, :], low_sb, ALU.add)

            def up_sum(steps_sem, done):
                dve.tensor_tensor(hid_sb, bank[1][0:CAP, :], low_sb, ALU.add).then_inc(steps_sem[0], 1)
                dve.wait_ge(*steps_sem)
                dve.tensor_tensor(hid_sb, hid_sb, silu_sb, ALU.mult).then_inc(done, 1)

            def keep_y1(e, parity):
                dve.wait_ge(S["y_mm"], e + 1)
                rows = slice(parity * CAP, (parity + 1) * CAP)
                dve.tensor_copy(y_sb[rows, HALF:D], bank[3][rows, :]).then_inc(S["y1_ready"], 1)

            def keep_selection():
                return dve.tensor_copy(gselT_sb, bank[2][:, 0:TILES * P].rearrange("p (t k) -> p t k", t=TILES))

            def low_weights(e, s, u):
                dve.wait_ge(S["whi_ready"], e * UNITS + (u + 1))
                low_part(u, s).then_inc(S["wlo_ready"], 1)

            def hidden(e, first):
                dve.wait_ge(S["ulow_ready"], e + 1)
                dve.wait_ge(S["silu_ready"], e + 1)
                if not first:
                    dve.wait_ge(S["hidT_mm"], e)
                up_sum((S["usum_ready"], e + 1), S["hid_ready"])

            def expert(e, s, parity, first, second, pair):
                for u in range(UNITS):
                    low_weights(e, s, u)
                    if u == 0 and not first:
                        if not second:
                            keep_y1(e - 2, parity)
                        if parity and not second:
                            dve.wait_ge(S["st_mm"], pair)
                            keep_selection().then_inc(S["st_ready"], 1)
                        hidden(e - 1, second)
                    if u == 3:
                        if parity:
                            select_gated(e - 1, 0)
                            select_gated(e, 1).then_inc(S["gsel_ready"], 1)
                    if u == 5:
                        dve.wait_ge(S["glow_ready"], e + 1)
                        gate_sum().then_inc(S["gsum_ready"], 1)
                dve.wait_ge(S["xh_ready"], e + 2)
                low_tokens(1 - parity).then_inc(S["xe_ready"], 1)
                select(e + 2, S["sel_ready"])

            select(0, S["sel_ready"])
            dve.wait_ge(S["xh_ready"], 1)
            low_tokens(0).then_inc(S["xe_ready"], 1)
            select(1, S["sel_ready"])
            expert(0, 0, 0, True, False, 0)
            expert(1, 1, 1, False, True, 0)
            with dve.Fori(0, EXPERTS // BODY) as i:
                for j in range(BODY):
                    k = PEELED + j
                    expert(i * BODY + k, k % SLOTS, k % 2, False, False, i * SLOTS + k // 2)
            keep_y1(EXPERTS - 2, 0)
            hidden(EXPERTS - 1, False)
            keep_y1(EXPERTS - 1, 1)
            dve.wait_ge(S["st_mm"], EXPERTS // 2)
            keep_selection().then_inc(S["st_ready"], 1)

            most_tokens = dve.value_load(most_int[0:1, 0:1], min_val=0, max_val=SEQ)
            with dve.If(most_tokens > CAP):
                dve.wait_ge(S["scat_mm"], EXPERTS // 2)
                dve.memset(y_sb[CAP:P, :], 0.0)
                for t in range(TILES):
                    dve.memset(gsel[:, t, 1, :], 0.0)
                dve.nop().then_inc(S["o_turn"], 1)
                with dve.Fori(0, ROUNDS - 1) as r:
                    dve.tensor_scalar(rank[:, :, :], rank[:, :, :], float(CAP), None, ALU.subtract).then_inc(S["o_rank"], 1)
                    with dve.Fori(0, EXPERTS) as e:
                        n = r * EXPERTS + e
                        m = n + EXPERTS
                        dve.wait_ge(S["o_rank"], r + 1)
                        select_gated(e, 0)
                        select(e, S["o_sel"])
                        dve.wait_ge(S["o_xh"], n + 1)
                        low_tokens(0).then_inc(S["o_xs"], 1)
                        for u in range(UNITS):
                            dve.wait_ge(S["whi_ready"], m * UNITS + (u + 1))
                            low_part(u, 0).then_inc(S["wlo_ready"], 1)
                            if u == 5:
                                dve.wait_ge(S["glow_ready"], m + 1)
                                gate_sum().then_inc(S["gsum_ready"], 1)
                        dve.wait_ge(S["ulow_ready"], m + 1)
                        dve.wait_ge(S["silu_ready"], m + 1)
                        up_sum((S["usum_ready"], m + 1), S["hid_ready"])
                        dve.wait_ge(S["y_mm"], m + 1)
                        dve.tensor_copy(y_sb[0:CAP, HALF:D], bank[3][0:CAP, :]).then_inc(S["y1_ready"], 1)
                        dve.wait_ge(S["o_st"], n + 1)
                        keep_selection().then_inc(S["o_stsb"], 1)
                        dve.wait_ge(S["o_scat"], n + 1)
                        dve.nop().then_inc(S["o_turn"], 1)
            dve.nop()

            dve.wait_ge(S["moe_done"], 1)
            for t in range(TILES):
                for n in range(2):
                    cols = slice(n * HALF, (n + 1) * HALF)
                    dve.tensor_tensor(h_sb[:, t, cols], bank[4 + 2 * t + n][:, :], h_sb[:, t, cols], ALU.add
                                      ).then_inc(S["result_ready"], 1)


_INS = ["x", "rel_bias", "norm1_g", "w_in", "conv_w", "conv_b", "dt_bias", "a_log", "d_skip", "ssd_norm_g",
        "q_norm_g", "k_norm_g", "w_out", "norm2_g", "w_r1", "b_r1", "w_r2", "b_r2", "w_gate", "w_up", "w_down"]


def kernel(**inputs):
    import numpy as _np
    import concourse.bacc as _bacc
    from concourse import mybir as _mybir
    from concourse.bass_utils import run_bass_kernel_spmd as _run

    nc = _bacc.Bacc("TRN2", target_bir_lowering=False, num_devices=1, dynamic_dma_scratch_size=1024)
    arrays, args = {}, []
    for name in _INS:
        a = _np.ascontiguousarray(inputs[name])
        arrays[f"in_{name}_dram"] = a
        args.append(nc.dram_tensor(f"in_{name}_dram", a.shape, _mybir.dt.from_np(a.dtype), kind="ExternalInput").ap())
    args.append(nc.dram_tensor("bias_rows", (P, HEADS, SEQ + P), F32, kind="Internal").ap())
    args.append(nc.dram_tensor("out_0_dram", (1, SEQ, D), F32, kind="ExternalOutput").ap())
    hymba_layer(nc, *args)
    r = _run(nc, [arrays], core_ids=[0])
    return r.results[0]["out_0_dram"]
```

```python
from contextlib import ExitStack

import numpy as np

import concourse.bass as bass
from concourse import mybir

F32 = mybir.dt.float32
F32R = mybir.dt.float32r
BF16 = mybir.dt.bfloat16
I32 = mybir.dt.int32
ALU = mybir.AluOpType
ACT = mybir.ActivationFunctionType
AX = mybir.AxisListType

P = 128
SEQ = 256
TILES = SEQ // P
D = 1024
DC = D // P
HEADS = 8
HD = 64
INNER = HEADS * HD
GROUPS = 2
HPG = HEADS // GROUPS
STATE = 64
TAPS = 4
CONV_CH = INNER + 2 * GROUPS * STATE
CONV_BLOCKS = CONV_CH // P
XS_BLOCKS = INNER // P
B_BLOCK = XS_BLOCKS
C_BLOCK = XS_BLOCKS + 1
IN_COLS = INNER + CONV_CH + HEADS + 3 * INNER
COL_Z = 0
COL_XBC = INNER
COL_Q = INNER + CONV_CH + HEADS
COL_K = COL_Q + INNER
COL_V = COL_K + INNER
XBC_COLS = CONV_CH + HEADS
BUCKETS = 32
MAX_DIST = 128
MOE_GROUPS = 4
PER_GROUP = 8
EXPERTS = MOE_GROUPS * PER_GROUP
ROUTES = MOE_GROUPS + EXPERTS
HID = 512
HC = HID // P
EPS = 1e-6
LOW = -1e30
CAP = 64
ROUNDS = SEQ // CAP
SLOTS = 3
UNITS = 2 * DC
BUFS = 4
GATE_DONE = DC + 2
BODY = 2 * SLOTS
PEELED = EXPERTS % BODY
assert 2 * CAP == P and PEELED == 2
PIECE = DC * HID
HALF = D // 2


def bucket_ranges():
    exact = BUCKETS // 2
    dist = np.arange(SEQ)
    far = exact + (np.log(np.maximum(dist, exact) / exact) / np.log(MAX_DIST / exact)
                   * (BUCKETS - exact)).astype(np.int64)
    bucket = np.where(dist < exact, dist, np.minimum(far, BUCKETS - 1))
    return [(b, int(np.flatnonzero(bucket == b)[0]), int(np.flatnonzero(bucket == b)[-1]))
            for b in range(BUCKETS) if (bucket == b).any()]


def hymba_layer(nc, x, rel_bias, norm1_g, w_in, conv_w, conv_b, dt_bias, a_log, d_skip, ssd_norm_g,
                q_norm_g, k_norm_g, w_out, norm2_g, w_r1, b_r1, w_r2, b_r2, w_gate, w_up, w_down,
                bias_rows, out):
    x_rows = x.rearrange("b (t p) d -> p (b t) d", p=P)
    out_rows = out.rearrange("b (t p) d -> p (b t) d", p=P)
    win_rows = w_in.rearrange("l (p c) n -> p (l c) n", c=DC)
    wout_rows = w_out.rearrange("l (c p) n -> p (l c) n", p=P)
    gate_rows = w_gate.rearrange("l e (p c) n -> (l e) p c n", c=DC)
    up_rows = w_up.rearrange("l e (p c) n -> (l e) p c n", c=DC)
    down_rows = w_down.rearrange("l e (c p) n -> (l e) p c n", p=P)

    ctx = ExitStack()
    with ctx:
        def sb(name, shape, dt=F32):
            return ctx.enter_context(nc.sbuf_tensor(name, shape, dt))

        def sem(name):
            return ctx.enter_context(nc.semaphore(name))

        ring = sb("ring", [P, SLOTS * 3 * PIECE])

        def piece(i, n=1):
            return ring[:, i * PIECE:(i + n) * PIECE]

        wg_sb = [piece(3 * s).rearrange("p (c n) -> p c n", c=DC) for s in range(SLOTS)]
        wu_sb = [piece(3 * s + 1).rearrange("p (c n) -> p c n", c=DC) for s in range(SLOTS)]
        wd_sb = [piece(3 * s + 2).rearrange("p (c n) -> p c n", c=HC) for s in range(SLOTS)]
        wxbc_sb = ring[:, 0:DC * XBC_COLS].rearrange("p (c n) -> p c n", c=DC)
        wq_sb, wk_sb, wv_sb, wz_sb = [piece(i).rearrange("p (c n) -> p c n", c=DC) for i in (2, 3, 4, 5)]
        wout_sb = piece(6, 2).rearrange("p (c n) -> p c n", c=DC)
        raw_at = DC * XBC_COLS
        RAWW = SEQ + TAPS - 1
        raw = ring[:, raw_at:raw_at + CONV_BLOCKS * RAWW].rearrange("p (b t) -> p b t", b=CONV_BLOCKS)
        assert raw_at + CONV_BLOCKS * RAWW <= 2 * PIECE
        last_piece = piece(8)
        bias_tab = last_piece[:, 0:HEADS * SEQ].rearrange("p (h j) -> p h j", h=HEADS)
        z_silu = last_piece[:, 0:TILES * INNER].rearrange("p (t n) -> p t n", t=TILES)
        xdt = last_piece[:, 2048:3072].rearrange("p (t n) -> p t n", t=TILES)
        y_ssd = last_piece[:, 3072:4096].rearrange("p (t n) -> p t n", t=TILES)

        work = sb("work", [P, 5504])
        xn = work[:, 0:2048].rearrange("p (t c q) -> p t c q", t=TILES, c=DC)
        xn_parts = [work[:, 2048 + 1024 * k:3072 + 1024 * k].bitcast(BF16).rearrange("p (t c q) -> p t c q", t=TILES, c=DC)
                    for k in range(3)]

        def xn_part(k, t):
            at = 2 * D + k * D + t * (D // 2)
            return work[:, at:at + D // 2].bitcast(BF16)

        low_sb = work[0:CAP, 0:512]
        silu_sb = work[0:CAP, 512:1024]
        hid_sb = work[0:CAP, 1024:1536]
        hidT_sb = work[:, 1536:1792].rearrange("p (m k) -> p m k", m=HC)
        gselT_sb = work[:, 1792:2048].rearrange("p (t k) -> p t k", t=TILES)
        turned_sb = work[:, 1536:2048]
        gsel = work[:, 5120:5376].rearrange("p (t w k) -> p t w k", t=TILES, w=2)
        sel = work[:, 5376:5440].bitcast(BF16).rearrange("p (t k) -> p t k", t=TILES)
        qk_tok = work[:, 0:2048].rearrange("p (w t n) -> p w t n", w=2, t=TILES)
        decay_mat = work[:, 0:2048].rearrange("p (t h l) -> p t h l", t=TILES, h=HEADS)
        prob = work[:, 2048:3584].rearrange("p (k n) -> p k n", k=4)
        a_bcast = work[:, 2048:3072].rearrange("p (h l) -> p h l", h=HEADS)
        probT = work[:, 3584:4352].rearrange("p (k n) -> p k n", k=2)
        v_tok = work[:, 4352:5376].rearrange("p (t n) -> p t n", t=TILES)

        with nc.sbuf_tensor("front", [P, 6144], F32) as front:
            pass
        xe_split = sb("xe_split", [P, 2, DC, P], F32R)
        w_split = sb("w_split", [P, BUFS, 2, HID], F32R)
        xT = front[:, 0:2048].rearrange("p (c t) -> p c t", c=DC)
        y_att = front[:, 0:1024].rearrange("p (t n) -> p t n", t=TILES)
        conv = front[:, 2048:3584].rearrange("p (b t) -> p b t", b=CONV_BLOCKS)
        qkT = front[:, 3584:5632].rearrange("p (w b t) -> p w b t", w=2, b=XS_BLOCKS)
        mixT = front[:, 3584:5632].rearrange("p (c t) -> p c t", c=DC)
        x_scaled = front[:, 3584:5632].rearrange("p (t q c) -> p t c q", t=TILES, c=DC)
        squares = front[:, 3584:5632].rearrange("p (w t n) -> p w t n", w=2, t=TILES)
        xnT = front[:, 0:2048].rearrange("p (c t) -> p c t", c=DC)
        y_off = work[:, 2048:2560]

        h_sb = sb("h", [P, TILES, D])
        ident = sb("ident", [P, P])
        upto = sb("upto", [P, P])
        before = sb("before", [P, P])
        ones = sb("ones", [P, P])
        zeros = sb("zeros", [P, P])
        before_bf = sb("before_bf", [P, P], BF16)
        ones_bf = sb("ones_bf", [P, P], BF16)
        rank_iota = sb("rank_iota", [P, 2 * CAP])
        expert_iota = sb("expert_iota", [P, EXPERTS])
        minus_half = sb("minus_half", [P, 16])
        g1_col = sb("g1_col", [P, DC])
        qg_col = sb("qg_col", [P, 1])
        kg_col = sb("kg_col", [P, 1])
        qkg_col = sb("qkg_col", [P, 1])
        conv_rows = last_piece[0:TAPS + 1, 3072:3072 + CONV_CH]
        conv_cols = sb("conv_cols", [P, CONV_BLOCKS, TAPS + 1])
        rel_rows = sb("rel_rows", [BUCKETS, HEADS])
        relT = sb("relT", [HEADS, BUCKETS])
        bias_line = last_piece[0:HEADS, 2048:2048 + SEQ + P]
        dtb_bc = sb("dtb_bc", [P, HEADS])
        alog_bc = sb("alog_bc", [P, HEADS])
        dskip_bc = sb("dskip_bc", [P, HEADS])
        ssdg_bc = sb("ssdg_bc", [P, INNER])
        g2_bc = sb("g2_bc", [P, D])
        y_sb = g2_bc
        br_bc = sb("br_bc", [P, ROUTES])
        wr1_sb = sb("wr1_sb", [P, DC, MOE_GROUPS])
        wr2_sb = sb("wr2_sb", [P, DC, EXPERTS])
        wr_sb = sb("wr_sb", [P, DC, ROUTES])
        ms1 = sb("ms1", [P, TILES])
        rs1 = sb("rs1", [P, TILES])
        msqk = sb("msqk", [P, 2, TILES * HEADS])
        rsqk = sb("rsqk", [P, 2, TILES * HEADS])
        dt_lin = sb("dt_lin", [P, TILES, HEADS])
        dt_abs = sb("dt_abs", [P, TILES, HEADS])
        dt_exp = sb("dt_exp", [P, TILES, HEADS])
        dt_log = sb("dt_log", [P, TILES, HEADS])
        dt_sb = sb("dt_sb", [P, TILES, HEADS])
        a_exp = sb("a_exp", [P, HEADS])
        a_dt = sb("a_dt", [P, TILES, HEADS])
        a_cs = sb("a_cs", [P, TILES, HEADS])
        decay_arg = sb("decay_arg", [P, HEADS])
        decay_end = sb("decay_end", [P, HEADS])
        decay_in = sb("decay_in", [P, HEADS])
        cb_sb = sb("cb_sb", [P, TILES, GROUPS, P])
        b_tok = sb("b_tok", [P, P])
        state_sb = sb("state_sb", [P, HPG * HD])
        row_max = sb("row_max", [P, HEADS, TILES])
        neg_max = sb("neg_max", [P, HEADS, TILES])
        row_sum = sb("row_sum", [P, HEADS, TILES])
        row_inv = sb("row_inv", [P, HEADS, TILES])
        ms3 = sb("ms3", [P, TILES])
        rs3 = sb("rs3", [P, TILES])
        ms2 = sb("ms2", [P, TILES])
        rs2 = sb("rs2", [P, TILES])
        logit = sb("logit", [P, TILES, ROUTES])
        top = sb("top", [P, 4, TILES])
        low_at = sb("low_at", [P, TILES])
        gexp = sb("gexp", [P, TILES, MOE_GROUPS])
        gsum = sb("gsum", [P, TILES])
        gval = sb("gval", [P, TILES])
        ghot = sb("ghot", [P, TILES, MOE_GROUPS])
        eq4 = sb("eq4", [P, TILES, MOE_GROUPS])
        eq32 = sb("eq32", [P, TILES, EXPERTS])
        masked = sb("masked", [P, TILES, EXPERTS])
        hot1 = sb("hot1", [P, TILES, EXPERTS])
        hot2 = sb("hot2", [P, TILES, EXPERTS])
        share = sb("share", [P, 4, TILES])
        gates = sb("gates", [P, TILES, EXPERTS])
        chosen = sb("chosen", [P, TILES, EXPERTS], BF16)
        rank = sb("rank", [P, TILES, EXPERTS + 2])
        most = sb("most", [1, 1])
        most_int = sb("most_int", [1, 1], I32)

        bank = [ctx.enter_context(nc.psum_tensor(f"bank{i}", [P, 512], F32)) for i in range(8)]

        x_in, small_in, late_in = sem("x_in"), sem("small_in"), sem("late_in")
        g1_in = sem("g1_in")
        wxbc_in, wq_in, wk_in, wv_in, wz_in = [sem(n) for n in ("wxbc_in", "wq_in", "wk_in", "wv_in", "wz_in")]
        wout_in, biasline_out, biastab_in, out_done = [sem(n) for n in ("wout_in", "biasline_out", "biastab_in", "out_done")]
        wg_in = [sem(f"wg_in{s}") for s in range(SLOTS)]
        wu_in = [sem(f"wu_in{s}") for s in range(SLOTS)]
        wd_in = [sem(f"wd_in{s}") for s in range(SLOTS)]
        names = """const_base const_ready zero_ready ms1_ready rs1_ready bf_ready xscaled xT_mm xT_ready small_mm
            small_ready relT_ready line_ready xbc_mm raw_ready dt_mm q_mm k_mm v_mm z_mm squares_ready
            msqk_ready rsqk_ready qk_ready v_ready conv_ready convsilu dtabs_ready dtlog_ready adt_ready acs_mm
            acs_ready ab_ready rowcs_mm decay_lin decay_exp dend_lin dend_exp xs_mm xdt_ready btok_ready cb_mm
            cb_ready mix_ready qkT_mm qT_ready kT_ready qkg_ready score_mm score_ready negmax_ready prob_ready
            probT_mm probT_ready pv_mm zsilu_ready yatt_ready ydiag_mm xdec_ready state_mm state_ready yoff_mm
            ms3_ready rs3_ready yssd_ready mixT_mm mixT_ready wout_mm h_ready ms2_ready ms2_act rs2_ready
            xn_ready xnT_mm xnT_ready wr_ready logit_mm gexp_in gexp_ready share_in share_ready chosen_ready
            rank_mm most_ready part0 part0_taken part1 part1_taken part2 sel_ready xe_mm xh_ready xe_ready
            whi_ready wlo_ready unit_mm glow_ready gsum_ready silu_ready ulow_ready hid_ready hidT_mm hidT_ready
            y0_mm y_mm y0_ready y1_ready scat_mm moe_done result_ready dve_step act_step o_rank
            o_turn o_w o_sel o_xe o_xh o_xs usum_ready o_scat""".split()
        S = {n: sem(n) for n in names}

        block = ctx.enter_context(nc.Block())

        def bc(ap, shape):
            return ap.to_broadcast(shape)

        @block.sync
        def _(sp):
            sp.dma_start(h_sb[:, :, :], x_rows).then_inc(x_in, 16)
            sp.dma_start(g1_col[:, :], norm1_g.rearrange("l (p c) -> p (l c)", c=DC)).then_inc(g1_in, 16)
            sp.dma_start(wxbc_sb, win_rows[:, :, COL_XBC:COL_XBC + XBC_COLS]).then_inc(wxbc_in, 16)
            sp.wait_ge(small_in, 16 * 10)
            sp.dma_start(wq_sb, win_rows[:, :, COL_Q:COL_Q + INNER]).then_inc(wq_in, 16)
            sp.dma_start(wk_sb, win_rows[:, :, COL_K:COL_K + INNER]).then_inc(wk_in, 16)
            sp.dma_start(wv_sb, win_rows[:, :, COL_V:COL_V + INNER]).then_inc(wv_in, 16)
            sp.dma_start(wz_sb, win_rows[:, :, COL_Z:COL_Z + INNER]).then_inc(wz_in, 16)
            sp.dma_start(wout_sb, wout_rows).then_inc(wout_in, 16)

            sp.wait_ge(S["line_ready"], len(bucket_ranges()))
            sp.dma_start(bias_rows.rearrange("p h i -> h p i"), bias_line.unsqueeze(1).to_broadcast([HEADS, P, SEQ + P])
                         ).then_inc(biasline_out, 16)
            sp.wait_ge(biasline_out, 16)
            sp.dma_start(bias_tab, bass.AP(bias_rows.tensor, P - 1,
                                           [[HEADS * (SEQ + P) - 1, P], [SEQ + P, HEADS], [1, SEQ]])
                         ).then_inc(biastab_in, 16)

            sp.wait_ge(S["dt_mm"], 1)
            sp.dma_start(wg_sb[0], gate_rows[0]).then_inc(wg_in[0], 16)
            sp.wait_ge(S["conv_ready"], CONV_BLOCKS)
            sp.dma_start(wu_sb[0], up_rows[0]).then_inc(wu_in[0], 16)
            sp.wait_ge(S["q_mm"], TILES)
            sp.dma_start(wd_sb[0], down_rows[0]).then_inc(wd_in[0], 16)
            sp.wait_ge(S["k_mm"], TILES)
            sp.dma_start(wg_sb[1], gate_rows[1]).then_inc(wg_in[1], 16)
            sp.wait_ge(S["v_mm"], TILES)
            sp.dma_start(wu_sb[1], up_rows[1]).then_inc(wu_in[1], 16)
            sp.wait_ge(S["z_mm"], 1)
            sp.dma_start(wd_sb[1], down_rows[1]).then_inc(wd_in[1], 16)
            sp.wait_ge(S["wout_mm"], TILES * 2)
            sp.dma_start(wg_sb[2], gate_rows[2]).then_inc(wg_in[2], 16)
            sp.dma_start(wu_sb[2], up_rows[2]).then_inc(wu_in[2], 16)
            sp.wait_ge(S["yssd_ready"], TILES)
            sp.dma_start(wd_sb[2], down_rows[2]).then_inc(wd_in[2], 16)

            def refill_gate(e, s):
                sp.wait_ge(S["wlo_ready"], e * UNITS + DC)
                sp.dma_start(wg_sb[s], gate_rows[e + SLOTS]).then_inc(wg_in[s], 16)

            def refill_up(e, s):
                sp.wait_ge(S["wlo_ready"], e * UNITS + UNITS)
                sp.dma_start(wu_sb[s], up_rows[e + SLOTS]).then_inc(wu_in[s], 16)

            def refill_down(e, s):
                sp.wait_ge(S["y_mm"], e + 1)
                sp.dma_start(wd_sb[s], down_rows[e + SLOTS]).then_inc(wd_in[s], 16)

            refill_gate(0, 0)
            refill_up(0, 0)
            full = (EXPERTS - SLOTS - 1) // SLOTS
            with sp.Fori(0, full) as i:
                for j in range(1, SLOTS + 1):
                    refill_gate(i * SLOTS + j, j % SLOTS)
                    refill_down(i * SLOTS + (j - 1), j - 1)
                    refill_up(i * SLOTS + j, j % SLOTS)
            for e in range(full * SLOTS + 1, EXPERTS - SLOTS):
                refill_gate(e, e % SLOTS)
                refill_down(e - 1, (e - 1) % SLOTS)
                refill_up(e, e % SLOTS)
            refill_down(EXPERTS - SLOTS - 1, (EXPERTS - SLOTS - 1) % SLOTS)

            sp.wait_ge(S["most_ready"], 1)
            most_tokens = sp.value_load(most_int[0:1, 0:1], min_val=0, max_val=SEQ)
            with sp.If(most_tokens > CAP):
                with sp.Fori(0, ROUNDS - 1) as r:
                    with sp.Fori(0, EXPERTS) as e:
                        sp.wait_ge(S["o_turn"], r * EXPERTS + e + 1)
                        sp.dma_start(wg_sb[0], gate_rows[e]).then_inc(S["o_w"], 16)
                        sp.dma_start(wu_sb[0], up_rows[e]).then_inc(S["o_w"], 16)
                        sp.dma_start(wd_sb[0], down_rows[e]).then_inc(S["o_w"], 16)
            sp.nop()

            for t in range(TILES):
                for n in range(2):
                    sp.wait_ge(S["result_ready"], t * 2 + n + 1)
                    sp.dma_start(out_rows[:, t, n * HALF:(n + 1) * HALF],
                                 h_sb[:, t, n * HALF:(n + 1) * HALF]).then_inc(out_done, 16)
            sp.wait_ge(out_done, 16 * TILES * 2)

        @block.gpsimd
        def _(pool):
            pool.memset(ident[:, :], 0.0).then_inc(S["const_base"], 1)
            pool.memset(ones[:, :], 1.0).then_inc(S["const_base"], 1)
            pool.memset(zeros[:, :], 0.0).then_inc(S["const_base"], 1)
            pool.memset(minus_half[:, :], -0.5).then_inc(S["const_base"], 1)
            pool.memset(bias_line[:, :], LOW).then_inc(S["const_base"], 1)
            pool.iota(rank_iota[:, :], [[0, 2], [1, CAP]], base=0, channel_multiplier=0,
                      allow_small_or_imprecise_dtypes=True).then_inc(S["const_base"], 1)
            pool.iota(expert_iota[:, :], [[1, EXPERTS]], base=0, channel_multiplier=0,
                      allow_small_or_imprecise_dtypes=True).then_inc(S["const_base"], 1)
            pool.wait_ge(S["const_base"], 7)
            pool.affine_select(out=ident[:, :], in_=ident[:, :], compare_op=ALU.not_equal, fill=1.0, base=0,
                               pattern=[[-1, P]], channel_multiplier=1).then_inc(S["const_ready"], 1)
            pool.affine_select(out=upto[:, :], in_=ones[:, :], compare_op=ALU.is_ge, fill=0.0, base=0,
                               pattern=[[1, P]], channel_multiplier=-1).then_inc(S["const_ready"], 1)
            pool.affine_select(out=before[:, :], in_=ones[:, :], compare_op=ALU.is_ge, fill=0.0, base=-1,
                               pattern=[[1, P]], channel_multiplier=-1).then_inc(S["const_ready"], 1)

            def rsqrt(dst, src, n, wait, count, done):
                pool.wait_ge(wait, count)
                pool.tensor_tensor(dst, src, minus_half[:, 0:n], ALU.pow).then_inc(done, 1)

            rsqrt(rs1[:, :], ms1[:, :], TILES, S["ms1_ready"], 1, S["rs1_ready"])
            pool.wait_ge(S["relT_ready"], 1)
            for b, near, far in bucket_ranges():
                last = pool.tensor_copy(bias_line[:, SEQ - 1 - far:SEQ - near],
                                        bc(relT[:, b:b + 1], [HEADS, far - near + 1]))
                last.then_inc(S["line_ready"], 1)
            rsqrt(rsqk[:, 0, :], msqk[:, 0, :], TILES * HEADS, S["msqk_ready"], 1, S["rsqk_ready"])
            rsqrt(rsqk[:, 1, :], msqk[:, 1, :], TILES * HEADS, S["msqk_ready"], 2, S["rsqk_ready"])
            for t in range(TILES):
                rsqrt(rs3[:, t:t + 1], ms3[:, t:t + 1], 1, S["ms3_ready"], t + 1, S["rs3_ready"])
            for t in range(TILES):
                rsqrt(rs2[:, t:t + 1], ms2[:, t:t + 1], 1, S["ms2_ready"], t + 1, S["rs2_ready"])
                pool.wait_ge(S["part1"], t + 1)
                pool.tensor_tensor(work[:, t * D:(t + 1) * D], work[:, t * D:(t + 1) * D], xn_part(1, t), ALU.subtract
                                   ).then_inc(S["part1_taken"], 1)

        @block.tensor
        def _(pe):
            conv_ps = bank[4][:, 0:CONV_BLOCKS * 8].rearrange("p (b k) -> p b k", b=CONV_BLOCKS)
            pe.wait_ge(S["const_ready"], 3)
            for t in range(TILES):
                pe.wait_ge(S["xscaled"], t + 1)
                for c in range(DC):
                    mm = pe.transpose(bank[c // 2][:, (c % 2) * SEQ + t * P:(c % 2) * SEQ + (t + 1) * P],
                                      x_scaled[:, t, c, :], ident[:, :])
            mm.then_inc(S["xT_mm"], 1)

            def turn_tables():
                pe.wait_ge(small_in, 16 * 10)
                for b in range(CONV_BLOCKS):
                    pe.transpose(conv_ps[:, b, 0:TAPS + 1], conv_rows[:, b * P:(b + 1) * P], ident[0:TAPS + 1, 0:TAPS + 1])
                pe.transpose(bank[4][0:HEADS, 64:64 + BUCKETS], rel_rows[:, :], ident[0:BUCKETS, 0:BUCKETS]
                             ).then_inc(S["small_mm"], 1)

            pe.wait_ge(wxbc_in, 16)
            for b in range(CONV_BLOCKS):
                for c in range(DC):
                    if b == 0 and c % 2 == 0:
                        pe.wait_ge(S["xT_ready"], c // 2 + 1)
                    mm = pe.matmul(bank[5 + b // 2][:, (b % 2) * SEQ:(b % 2 + 1) * SEQ],
                                   wxbc_sb[:, c, b * P:(b + 1) * P], xT[:, c, :], start=(c == 0), stop=(c == DC - 1))
                if b % 2:
                    mm.then_inc(S["xbc_mm"], 1)
                if b == 1:
                    turn_tables()
            pe.wait_ge(S["small_ready"], 1)
            for t in range(TILES):
                for c in range(DC):
                    mm = pe.matmul(bank[4][:, t * HEADS:(t + 1) * HEADS], xT[:, c, t * P:(t + 1) * P],
                                   wxbc_sb[:, c, CONV_CH:XBC_COLS], start=(c == 0), stop=(c == DC - 1))
            mm.then_inc(S["dt_mm"], 1)

            def project(dst, w, t, done):
                for c in range(DC):
                    mm = pe.matmul(dst[:, :], xT[:, c, t * P:(t + 1) * P], w[:, c, :], start=(c == 0), stop=(c == DC - 1))
                mm.then_inc(done, 1)

            pe.wait_ge(wq_in, 16)
            for t in range(TILES):
                project(bank[t], wq_sb, t, S["q_mm"])
            pe.wait_ge(wk_in, 16)
            for t in range(TILES):
                project(bank[2 + t], wk_sb, t, S["k_mm"])
            pe.wait_ge(S["adt_ready"], 1)
            pe.matmul(bank[4][:, 0:TILES * HEADS], upto[:, :], a_dt[:, :, :].rearrange("p t h -> p (t h)"),
                      start=True, stop=True).then_inc(S["acs_mm"], 1)
            pe.wait_ge(wv_in, 16)
            for t in range(TILES):
                pe.wait_ge(S["raw_ready"], t + 1)
                project(bank[5 + t], wv_sb, t, S["v_mm"])

            for t in range(TILES):
                if t == 0:
                    pe.wait_ge(S["raw_ready"], 3)
                    pe.wait_ge(S["convsilu"], 3)
                else:
                    pe.wait_ge(S["v_ready"], 1)
                for b in range(XS_BLOCKS):
                    mm = pe.transpose((bank[7] if t == 0 else bank[5])[:, b * P:(b + 1) * P],
                                      conv[:, b, t * P:(t + 1) * P], ident[:, :])
                mm.then_inc(S["xs_mm"], 1)
            pe.wait_ge(S["acs_ready"], 1)
            pe.transpose(bank[4][:, P:2 * P], conv[:, B_BLOCK, 0:P], ident[:, :])
            pe.wait_ge(S["v_ready"], 2)
            for t in range(TILES):
                for g in range(GROUPS):
                    rows = slice(g * STATE, (g + 1) * STATE)
                    mm = pe.matmul(bank[6 - 2 * g][:, (GROUPS + t) * P:(GROUPS + t + 1) * P],
                                   conv[rows, B_BLOCK, t * P:(t + 1) * P], conv[rows, C_BLOCK, t * P:(t + 1) * P],
                                   start=True, stop=True)
            mm.then_inc(S["cb_mm"], 1)
            pe.wait_ge(S["qk_ready"], 2 * TILES)
            for t in range(TILES):
                pe.wait_ge(S["ab_ready"], t + 1)
                for h in range(HEADS):
                    mm = pe.matmul(bank[2 * t + h // 4][:, (h % 4) * P:(h % 4 + 1) * P], a_bcast[:, h, :], upto[:, :],
                                   start=True, stop=True)
                mm.then_inc(S["rowcs_mm"], 1)
            for w in range(2):
                if w == 0:
                    pe.wait_ge(S["btok_ready"], 1)
                    pe.wait_ge(S["cb_ready"], GROUPS)
                    pe.wait_ge(S["xdt_ready"], TILES * 2)
                for b in range(XS_BLOCKS):
                    for t in range(TILES):
                        at = (b % 2) * SEQ + t * P
                        mm = pe.transpose(bank[4 + 2 * w + b // 2][:, at:at + P], qk_tok[:, w, t, b * P:(b + 1) * P],
                                          ident[:, :])
                mm.then_inc(S["qkT_mm"], 1)

            def scores(h):
                b, rows, dst = h // 2, slice((h % 2) * HD, (h % 2 + 1) * HD), bank[4 + h % 2]
                pe.wait_ge(S["qT_ready"], 2)
                pe.wait_ge(S["kT_ready"], 2)
                if h >= 2:
                    pe.wait_ge(S["score_ready"], h - 1)
                pe.matmul(dst[:, 0:SEQ], qkT[rows, 0, b, P:SEQ], qkT[rows, 1, b, :], start=True, stop=True)
                pe.matmul(dst[:, SEQ:SEQ + P], qkT[rows, 0, b, 0:P], qkT[rows, 1, b, 0:P],
                          start=True, stop=True).then_inc(S["score_mm"], 1)

            def turn_probs(h):
                pe.wait_ge(S["prob_ready"], h + 1)
                if h >= 2:
                    pe.wait_ge(S["probT_ready"], h - 1)
                for j in range(3):
                    mm = pe.transpose(bank[6 + h % 2][:, j * P:(j + 1) * P], prob[:, h % 4, j * P:(j + 1) * P], ident[:, :])
                mm.then_inc(S["probT_mm"], 1)

            def weigh_values(h):
                pe.wait_ge(S["probT_ready"], h + 1)
                cols = slice(h * HD, (h + 1) * HD)
                pT = probT[:, h % 2, :]
                pe.matmul(bank[2][:, cols], pT[:, 2 * P:3 * P], v_tok[:, 0, cols], start=True, stop=True)
                pe.matmul(bank[3][:, cols], pT[:, 0:P], v_tok[:, 0, cols], start=True, stop=False)
                pe.matmul(bank[3][:, cols], pT[:, P:2 * P], v_tok[:, 1, cols], start=False, stop=True
                          ).then_inc(S["pv_mm"], 1)

            scores(0)
            scores(1)
            pe.wait_ge(wz_in, 16)
            pe.wait_ge(S["decay_lin"], TILES * HEADS)
            pe.wait_ge(S["dend_lin"], 1)
            for h in range(HEADS):
                for k in (2 * h, 2 * h + 1):
                    t, c = k // DC, k % DC
                    mm = pe.matmul(bank[t][:, :], xT[:, c, t * P:(t + 1) * P], wz_sb[:, c, :],
                                   start=(c == 0), stop=(c == DC - 1))
                if h == HEADS - 1:
                    mm.then_inc(S["z_mm"], 1)
                if h + 2 < HEADS:
                    scores(h + 2)
                turn_probs(h)
                if h >= 1:
                    weigh_values(h - 1)
            weigh_values(HEADS - 1)

            pe.wait_ge(S["mix_ready"], 2 * TILES)
            pe.wait_ge(S["score_ready"], HEADS)
            for t in range(TILES):
                for h in range(HEADS):
                    cols = slice(h * HD, (h + 1) * HD)
                    mm = pe.matmul(bank[4 + t][:, cols], decay_mat[:, t, h, :], xdt[:, t, cols], start=True, stop=True)
                if t == 0:
                    mm.then_inc(S["ydiag_mm"], 1)
                    pe.wait_ge(S["xdec_ready"], 1)
                    pe.wait_ge(S["probT_ready"], HEADS)
                    pe.matmul(bank[6][:, :], b_tok[:, :], xdt[:, 0, :], start=True, stop=True).then_inc(S["state_mm"], 1)
                else:
                    mm.then_inc(S["ydiag_mm"], 1)
            pe.wait_ge(S["state_ready"], GROUPS)
            for g in range(GROUPS):
                rows = slice(g * STATE, (g + 1) * STATE)
                mm = pe.matmul(bank[7 - g][:, g * HPG * HD:(g + 1) * HPG * HD], conv[rows, C_BLOCK, P:SEQ],
                               state_sb[rows, :], start=True, stop=True)
            mm.then_inc(S["yoff_mm"], 1)

            def turn_outputs(src, dst, t):
                for b in range(XS_BLOCKS):
                    mm = pe.transpose(bank[dst + t][:, b * P:(b + 1) * P], src[:, t, b * P:(b + 1) * P], ident[:, :])
                mm.then_inc(S["mixT_mm"], 1)

            def project_out(t, c, first, last):
                for n in range(2):
                    mm = pe.matmul(bank[(0, 1, 4, 5)[2 * t + n]][:, :], mixT[:, c, t * P:(t + 1) * P],
                                   wout_sb[:, c, n * HALF:(n + 1) * HALF], start=first, stop=last)
                    if last:
                        mm.then_inc(S["wout_mm"], 1)

            def turn_normed(t):
                pe.wait_ge(S["xn_ready"], t + 1)
                for c in range(DC):
                    at = (c % 2) * SEQ + t * P
                    mm = pe.transpose(bank[(2, 3, 6, 7)[c // 2]][:, at:at + P], xn[:, t, c, :], ident[:, :])
                mm.then_inc(S["xnT_mm"], 1)

            def route(t):
                pe.wait_ge(S["xnT_ready"], (t + 1) * (DC // 2))
                for c in range(DC):
                    mm = pe.matmul(bank[0][:, t * ROUTES:(t + 1) * ROUTES], xnT[:, c, t * P:(t + 1) * P], wr_sb[:, c, :],
                                   start=(c == 0), stop=(c == DC - 1))
                return mm

            pe.wait_ge(S["yatt_ready"], TILES)
            for t in range(TILES):
                turn_outputs(y_att, 2, t)
            pe.wait_ge(wout_in, 16)
            pe.wait_ge(S["zsilu_ready"], TILES)
            pe.wait_ge(S["mixT_ready"], TILES)
            for c in range(XS_BLOCKS, DC):
                project_out(0, c, c == XS_BLOCKS, False)
            for t in range(TILES):
                pe.wait_ge(S["yssd_ready"], t + 1)
                if t == 0:
                    pe.wait_ge(S["state_ready"], GROUPS)
                turn_outputs(y_ssd, 6, t)
            pe.wait_ge(S["mixT_ready"], TILES + 1)
            for c in range(XS_BLOCKS):
                project_out(0, c, False, c == XS_BLOCKS - 1)
            for c in range(XS_BLOCKS, DC):
                project_out(1, c, c == XS_BLOCKS, False)
            pe.wait_ge(S["mixT_ready"], 2 * TILES)
            turn_normed(0)
            for c in range(XS_BLOCKS):
                project_out(1, c, False, c == XS_BLOCKS - 1)
            pe.wait_ge(S["wr_ready"], 2)
            pe.wait_ge(S["h_ready"], 2)
            route(0)
            turn_normed(1)
            route(1).then_inc(S["logit_mm"], 1)
            pe.wait_ge(S["h_ready"], 2 * TILES)
            total = [bank[4 + i] for i in range(4)]
            none = zeros[:, :].bitcast(BF16)
            for i in range(4):
                for j in range(2):
                    pe.matmul(total[i][:, j * 2 * P:(j + 1) * 2 * P], none[:, 0:P], none,
                              start=(j == 0), stop=False, skip_group_check=True)
            pe.wait_ge(S["bf_ready"], 2)
            pe.wait_ge(S["chosen_ready"], 1)
            pe.matmul(bank[1][:, 0:EXPERTS], before_bf[:, :], chosen[:, 0, :], start=True, stop=True)
            pe.matmul(bank[1][:, EXPERTS:2 * EXPERTS], ones_bf[:, :], chosen[:, 0, :], start=True, stop=False)
            pe.matmul(bank[1][:, EXPERTS:2 * EXPERTS], before_bf[:, :], chosen[:, 1, :], start=False, stop=True)
            pe.matmul(bank[1][:, 2 * EXPERTS:3 * EXPERTS], ones_bf[:, :], chosen[:, 0, :], start=True, stop=False)
            pe.matmul(bank[1][:, 2 * EXPERTS:3 * EXPERTS], ones_bf[:, :], chosen[:, 1, :], start=False, stop=True
                      ).then_inc(S["rank_mm"], 1)
            xe_ps = bank[0][:, :].rearrange("p (c k) -> p c k", c=DC)

            def gather():
                for c in range(DC):
                    for k in range(3):
                        for t in range(TILES):
                            mm = pe.matmul(xe_ps[:, c, :], xn_parts[k][:, t, c, :], sel[:, t, :],
                                           start=(k == 0 and t == 0), stop=(k == 2 and t == TILES - 1))
                return mm

            def unit(u, parity, before_last=None):
                c = u % DC
                for part in range(2):
                    if before_last is not None and part == 1:
                        pe.wait_ge(*before_last)
                    mm = pe.matmul(bank[u // DC][:, :], xe_split[:, parity, c, :], w_split[:, u % BUFS, part, :],
                                   start=(c == 0 and part == 0), stop=(c == DC - 1 and part == 1))
                return mm

            def turn_hidden():
                for m in range(HC):
                    mm = pe.transpose(bank[1][:, m * CAP:(m + 1) * CAP], hid_sb[:, m * P:(m + 1) * P], ident[0:CAP, 0:CAP])
                return mm

            def down(k, w, parity):
                n, c = k // HC, k % HC
                return pe.matmul(bank[2 + n][parity * CAP:(parity + 1) * CAP, :], hidT_sb[:, c, :],
                                 w[:, c, n * HALF:(n + 1) * HALF], start=(c == 0), stop=(c == HC - 1))

            def turn_selection():
                for t in range(TILES):
                    mm = pe.transpose(bank[1][:, (t + TILES) * P:(t + TILES + 1) * P],
                                      gsel[:, t, :, :].rearrange("p w k -> p (w k)"), ident[:, :])
                return mm

            def scatter():
                for t in range(TILES):
                    for n in range(2):
                        mm = pe.matmul(total[2 * t + n][:, :], gselT_sb[:, t, :], y_sb[:, n * HALF:(n + 1) * HALF],
                                       start=False, stop=False, skip_group_check=True)
                return mm

            def downs(e, s, turn, parity, ks, e_first=False):
                for k in ks:
                    if k == 0:
                        pe.wait_ge(wd_in[s], 16 * (turn + 1))
                        if not e_first:
                            pe.wait_ge(S["y0_ready"], e)
                        pe.wait_ge(S["hidT_ready"], e + 1)
                    if k == HC and not e_first:
                        pe.wait_ge(S["y1_ready"], e)
                    mm = down(k, wd_sb[s], parity)
                    if k == HC - 1:
                        mm.then_inc(S["y0_mm"], 1)
                mm.then_inc(S["y_mm"], 1) if ks[-1] == 2 * HC - 1 else None

            def expert(e, s, turn, parity, first, second):
                before_s = (s - 1) % SLOTS
                before_turn = turn if s else turn - 1
                for u in range(UNITS):
                    if u == 0:
                        pe.wait_ge(S["xe_ready"], e + 1)
                    if u == DC and not first:
                        pe.wait_ge(S["hidT_ready"], e)
                    pe.wait_ge(S["wlo_ready"], e * UNITS + (u + 1))
                    hidden = (S["hid_ready"], e) if u == 3 and not first else None
                    unit(u, parity, hidden).then_inc(S["unit_mm"], 1)
                    if u == 3 and not first:
                        mm = turn_hidden()
                        if parity and not second:
                            mm = turn_selection()
                        mm.then_inc(S["hidT_mm"], 1)
                    if u == GATE_DONE + 1:
                        pe.wait_ge(S["sel_ready"], e + 2)
                        pe.wait_ge(S["gsum_ready"], e + 1)
                        gather().then_inc(S["xe_mm"], 1)
                    if u >= 5 and u % 2 and not first:
                        downs(e - 1, before_s, before_turn, 1 - parity, [(u - 5) // 2], e_first=second)
                    if u == 7 and parity and not (first or second):
                        pe.wait_ge(S["y1_ready"], e - 1)
                        scatter().then_inc(S["scat_mm"], 1)
                if not first:
                    downs(e - 1, before_s, before_turn, 1 - parity, [2 * HC - 2, 2 * HC - 1])

            pe.wait_ge(S["part2"], TILES)
            pe.wait_ge(S["sel_ready"], 1)
            gather().then_inc(S["xe_mm"], 1)
            for e in range(PEELED):
                expert(e, e, 0, e, e == 0, e == 1)
            with pe.Fori(0, EXPERTS // BODY) as i:
                for j in range(BODY):
                    k = PEELED + j
                    expert(i * BODY + k, k % SLOTS, i * 2 + k // SLOTS, k % 2, False, False)
            last = EXPERTS - 1
            pe.wait_ge(S["hid_ready"], last + 1)
            turn_hidden()
            turn_selection().then_inc(S["hidT_mm"], 1)
            downs(last, last % SLOTS, last // SLOTS, 1, list(range(2 * HC)))
            pe.wait_ge(S["y0_ready"], EXPERTS)
            pe.wait_ge(S["y1_ready"], EXPERTS)
            scatter().then_inc(S["scat_mm"], 1)

            pe.wait_ge(S["most_ready"], 1)
            most_tokens = pe.value_load(most_int[0:1, 0:1], min_val=0, max_val=SEQ)
            with pe.If(most_tokens > CAP):
                with pe.Fori(0, ROUNDS - 1) as r:
                    with pe.Fori(0, EXPERTS) as e:
                        n = r * EXPERTS + e
                        m = n + EXPERTS
                        pe.wait_ge(S["o_sel"], n + 1)
                        gather().then_inc(S["o_xe"], 1)
                        pe.wait_ge(S["o_xs"], n + 1)
                        for u in range(UNITS):
                            pe.wait_ge(S["wlo_ready"], m * UNITS + (u + 1))
                            unit(u, 0).then_inc(S["unit_mm"], 1)
                        pe.wait_ge(S["hid_ready"], m + 1)
                        pe.matmul(bank[0][:, 0:P], zeros[0:32, :], zeros[0:32, :], start=True, stop=True)
                        turn_hidden()
                        turn_selection().then_inc(S["hidT_mm"], 1)
                        pe.wait_ge(S["hidT_ready"], m + 1)
                        for k in range(2 * HC):
                            mm = down(k, wd_sb[0], 0)
                        mm.then_inc(S["y_mm"], 1)
                        pe.wait_ge(S["y0_ready"], m + 1)
                        pe.wait_ge(S["y1_ready"], m + 1)
                        scatter().then_inc(S["o_scat"], 1)
            pe.matmul(bank[0][:, 0:P], zeros[0:32, :], zeros[0:32, :], start=True, stop=True).then_inc(S["moe_done"], 1)

        @block.scalar
        def _(act):
            steps = [0]

            def link(ins):
                steps[0] += 1
                ins.then_inc(S["act_step"], 1)
                act.wait_ge(S["act_step"], steps[0])

            def row(v):
                return v.rearrange("l n -> (l n)").partition_broadcast(P)

            for dst, src in ((conv_rows[0:TAPS, :], conv_w.rearrange("l k n -> (l k) n")),
                             (conv_rows[TAPS:TAPS + 1, :], conv_b), (rel_rows[:, :], rel_bias),
                             (qg_col[0:HD, :], q_norm_g.rearrange("l n -> n l")),
                             (qg_col[HD:P, :], q_norm_g.rearrange("l n -> n l")),
                             (kg_col[0:HD, :], k_norm_g.rearrange("l n -> n l")),
                             (kg_col[HD:P, :], k_norm_g.rearrange("l n -> n l")),
                             (dtb_bc[:, :], row(dt_bias)), (alog_bc[:, :], row(a_log)), (dskip_bc[:, :], row(d_skip))):
                act.dma_start(dst, src).then_inc(small_in, 16)
            for dst, src in ((ssdg_bc[:, :], row(ssd_norm_g)), (g2_bc[:, :], row(norm2_g)),
                             (br_bc[:, 0:MOE_GROUPS], row(b_r1)), (br_bc[:, MOE_GROUPS:ROUTES], row(b_r2)),
                             (wr1_sb[:, :, :], w_r1.rearrange("l (p c) n -> p (l c) n", c=DC)),
                             (wr2_sb[:, :, :], w_r2.rearrange("l (p c) n -> p (l c) n", c=DC))):
                act.dma_start(dst, src).then_inc(late_in, 16)

            act.wait_ge(S["const_ready"], 3)
            act.copy(before_bf[:, :], before[:, :]).then_inc(S["bf_ready"], 1)
            act.copy(ones_bf[:, :], ones[:, :]).then_inc(S["bf_ready"], 1)
            act.wait_ge(S["zero_ready"], 1)
            for i in range(3):
                act.wait_ge(S["xbc_mm"], i + 1)
                act.copy(raw[:, 2 * i:2 * i + 2, TAPS - 1:RAWW], bank[5 + i][:, :].rearrange("p (b t) -> p b t", b=2)
                         ).then_inc(S["raw_ready"], 1)
            act.wait_ge(S["dtabs_ready"], 1)
            act.activation(dt_exp[:, :, :], dt_abs[:, :, :], ACT.Exp, scale=-1.0)
            act.wait_ge(small_in, 16 * 10)
            link(act.activation(a_exp[:, :], alog_bc[:, :], ACT.Exp))
            act.activation(dt_log[:, :, :], dt_exp[:, :, :], ACT.Ln, bias=ones[:, 0:1]).then_inc(S["dtlog_ready"], 1)
            for w, done in ((0, S["q_mm"]), (1, S["k_mm"])):
                for t in range(TILES):
                    act.wait_ge(done, t + 1)
                    act.activation(squares[:, w, t, :], bank[2 * w + t][:, :], ACT.Square).then_inc(S["squares_ready"], 1)
            for i in range(3):
                act.wait_ge(S["conv_ready"], 2 * i + 2)
                act.activation(conv[:, 2 * i:2 * i + 2, :], conv[:, 2 * i:2 * i + 2, :], ACT.Silu).then_inc(S["convsilu"], 1)
            for t in range(TILES):
                act.wait_ge(S["v_mm"], t + 1)
                act.copy(v_tok[:, t, :], bank[5 + t][:, :]).then_inc(S["v_ready"], 1)
            for t in range(TILES):
                act.wait_ge(S["adt_ready"], 1)
                if t:
                    act.wait_ge(S["rowcs_mm"], t)
                act.copy(a_bcast, bc(a_dt[:, t, :].unsqueeze(2), [P, HEADS, P])).then_inc(S["ab_ready"], 1)
            act.wait_ge(S["acs_ready"], 1)
            act.activation(decay_in[:, :], a_cs[:, 1, :], ACT.Exp)
            act.wait_ge(S["dend_lin"], 1)
            act.activation(decay_end[:, :], decay_arg[:, :], ACT.Exp).then_inc(S["dend_exp"], 1)
            for t in range(TILES):
                for g in range(GROUPS):
                    act.wait_ge(S["decay_lin"], t * HEADS + (g + 1) * HPG)
                    block4 = decay_mat[:, t, g * HPG:(g + 1) * HPG, :]
                    act.activation(block4, block4, ACT.Exp).then_inc(S["decay_exp"], 1)
            def numerators(h):
                act.wait_ge(S["negmax_ready"], h + 1)
                act.activation(prob[:, h % 4, 0:SEQ], prob[:, h % 4, 0:SEQ], ACT.Exp, bias=neg_max[:, h, 1:2],
                               accum_out=row_sum[:, h, 1:2])
                act.activation(prob[:, h % 4, SEQ:SEQ + P], prob[:, h % 4, SEQ:SEQ + P], ACT.Exp, bias=neg_max[:, h, 0:1],
                               accum_out=row_sum[:, h, 0:1]).then_inc(S["prob_ready"], 1)

            def keep_turned(h):
                act.wait_ge(S["probT_mm"], h + 1)
                if h >= 2:
                    act.wait_ge(S["pv_mm"], h - 1)
                act.copy(probT[:, h % 2, :], bank[6 + h % 2][:, 0:3 * P]).then_inc(S["probT_ready"], 1)

            for h in range(HEADS + 1):
                if h < HEADS:
                    numerators(h)
                if h >= 1:
                    keep_turned(h - 1)
            act.wait_ge(S["z_mm"], 1)
            act.wait_ge(S["score_ready"], HEADS)
            for t in range(TILES):
                act.activation(z_silu[:, t, :], bank[t][:, :], ACT.Silu).then_inc(S["zsilu_ready"], 1)
            for i in range(2 * TILES):
                t = i % TILES
                act.wait_ge(S["mixT_mm"], i + 1)
                blocks = slice(XS_BLOCKS, DC) if i < TILES else slice(0, XS_BLOCKS)
                act.copy(mixT[:, blocks, t * P:(t + 1) * P],
                         bank[(2 if i < TILES else 6) + t][:, :].rearrange("p (b t) -> p b t", b=XS_BLOCKS)
                         ).then_inc(S["mixT_ready"], 1)
            def square_sum(t):
                act.wait_ge(S["h_ready"], 2 * t + 2)
                act.activation(conv[:, 0:4, :].rearrange("p b t -> p (b t)"), h_sb[:, t, :], ACT.Square,
                               accum_out=ms2[:, t:t + 1]).then_inc(S["ms2_act"], 1)

            def keep_normed(t):
                act.wait_ge(S["xnT_mm"], t + 1)
                for i in (0, 1):
                    act.copy(xnT[:, 2 * i:2 * i + 2, t * P:(t + 1) * P],
                             bank[(2, 3)[i]][:, :].rearrange("p (c t) -> p c t", c=2)[:, :, t * P:(t + 1) * P]
                             ).then_inc(S["xnT_ready"], 1)

            def bf16_part(k, t):
                if k:
                    act.wait_ge(S[("part0_taken", "part1_taken")[k - 1]], t + 1)
                act.copy(xn_part(k, t), work[:, t * D:(t + 1) * D]).then_inc(S[("part0", "part1", "part2")[k]], 1)

            square_sum(0)
            keep_normed(0)
            bf16_part(0, 0)
            bf16_part(1, 0)
            square_sum(1)
            bf16_part(2, 0)
            keep_normed(1)
            for k in range(3):
                bf16_part(k, 1)

            xe_ps = bank[0][:, :].rearrange("p (c k) -> p c k", c=DC)

            def high_part(u, s):
                return act.copy(w_split[:, u % BUFS, 0, :], (wg_sb, wu_sb)[u // DC][s][:, u % DC, :])

            def high_weights(e, s, turn, u, first=False):
                if u % DC == 0:
                    act.wait_ge((wg_in, wu_in)[u // DC][s], 16 * (turn + 1))
                if not (first and u < BUFS):
                    act.wait_ge(S["unit_mm"], e * UNITS + (u - BUFS + 1))
                high_part(u, s).then_inc(S["whi_ready"], 1)

            def high_tokens(e, parity):
                act.wait_ge(S["xe_mm"], e + 1)
                act.copy(xe_split[:, parity, :, 0:CAP], xe_ps).then_inc(S["xh_ready"], 1)

            def low_rows(src):
                return act.copy(low_sb, bank[src][CAP:P, :])

            def keep_hidden():
                return act.copy(work[:, 1536:1792], bank[1][:, 0:HC * CAP])

            def keep_hidden_selection():
                return act.copy(turned_sb, bank[1][:, :])

            def keep_y0(e, parity):
                act.wait_ge(S["y0_mm"], e + 1)
                rows = slice(parity * CAP, (parity + 1) * CAP)
                act.copy(y_sb[rows, 0:HALF], bank[2][rows, :]).then_inc(S["y0_ready"], 1)

            def up_low(e):
                act.wait_ge(S["unit_mm"], e * UNITS + UNITS)
                act.wait_ge(S["gsum_ready"], e + 1)
                low_rows(1).then_inc(S["ulow_ready"], 1)

            def turned(e, first, with_selection):
                act.wait_ge(S["hidT_mm"], e + 1)
                if not first:
                    act.wait_ge(S["y_mm"], e)
                (keep_hidden_selection if with_selection else keep_hidden)().then_inc(S["hidT_ready"], 1)

            def expert(e, s, turn, parity, first, second):
                for u in range(UNITS):
                    if not (first and u < BUFS):
                        high_weights(e, s, turn, u, first)
                    if u == 2 and not first:
                        up_low(e - 1)
                    if u == 6 and not first:
                        turned(e - 1, second, parity and not second)
                    if u == GATE_DONE:
                        act.wait_ge(S["unit_mm"], e * UNITS + DC)
                        if not first:
                            act.wait_ge(S["hid_ready"], e)
                        low_rows(0).then_inc(S["glow_ready"], 1)
                    if u == GATE_DONE + 2:
                        act.wait_ge(S["gsum_ready"], e + 1)
                        act.activation(silu_sb, silu_sb, ACT.Silu).then_inc(S["silu_ready"], 1)
                high_tokens(e + 1, 1 - parity)
                if not first:
                    keep_y0(e - 1, 1 - parity)

            act.wait_ge(S["logit_mm"], 1)
            for u in range(BUFS):
                high_weights(0, 0, 0, u, True)
            act.wait_ge(S["gexp_in"], 1)
            act.activation(gexp[:, :, :], gexp[:, :, :], ACT.Exp).then_inc(S["gexp_ready"], 1)
            act.wait_ge(S["share_in"], 1)
            act.activation(share[:, 0, :], share[:, 0, :], ACT.Exp).then_inc(S["share_ready"], 1)
            high_tokens(0, 0)
            expert(0, 0, 0, 0, True, False)
            expert(1, 1, 0, 1, False, True)
            with act.Fori(0, EXPERTS // BODY) as i:
                for j in range(BODY):
                    k = PEELED + j
                    expert(i * BODY + k, k % SLOTS, i * 2 + k // SLOTS, k % 2, False, False)
            up_low(EXPERTS - 1)
            turned(EXPERTS - 1, False, True)
            keep_y0(EXPERTS - 1, 1)

            act.wait_ge(S["most_ready"], 1)
            most_tokens = act.value_load(most_int[0:1, 0:1], min_val=0, max_val=SEQ)
            with act.If(most_tokens > CAP):
                with act.Fori(0, (ROUNDS - 1) * EXPERTS) as n:
                    m = n + EXPERTS
                    act.wait_ge(S["o_xe"], n + 1)
                    act.copy(xe_split[:, 0, :, 0:CAP], xe_ps).then_inc(S["o_xh"], 1)
                    act.wait_ge(S["o_w"], (n + 1) * 48)
                    for u in range(UNITS):
                        if u >= BUFS:
                            act.wait_ge(S["unit_mm"], m * UNITS + (u - BUFS + 1))
                        high_part(u, 0).then_inc(S["whi_ready"], 1)
                        if u == GATE_DONE:
                            act.wait_ge(S["unit_mm"], m * UNITS + DC)
                            low_rows(0).then_inc(S["glow_ready"], 1)
                            act.wait_ge(S["gsum_ready"], m + 1)
                            act.activation(silu_sb, silu_sb, ACT.Silu).then_inc(S["silu_ready"], 1)
                    act.wait_ge(S["unit_mm"], m * UNITS + UNITS)
                    low_rows(1).then_inc(S["ulow_ready"], 1)
                    act.wait_ge(S["hidT_mm"], m + 1)
                    keep_hidden_selection().then_inc(S["hidT_ready"], 1)
                    act.wait_ge(S["y_mm"], m + 1)
                    act.copy(y_sb[0:CAP, 0:HALF], bank[2][0:CAP, :]).then_inc(S["y0_ready"], 1)
            act.nop()

        @block.vector
        def _(dve):
            steps = [0]

            def link(ins):
                steps[0] += 1
                ins.then_inc(S["dve_step"], 1)
                dve.wait_ge(S["dve_step"], steps[0])

            def mean(ap, n):
                return dve.tensor_scalar(ap, ap, 1.0 / n, EPS, ALU.mult, ALU.add)

            dve.memset(raw[:, :, 0:TAPS - 1], 0.0).then_inc(S["zero_ready"], 1)
            dve.wait_ge(x_in, 16)
            for t in range(TILES):
                link(dve.tensor_tensor_reduce(xT[:, 4 * t:4 * t + 4, :].rearrange("p c t -> p (c t)"), h_sb[:, t, :],
                                              h_sb[:, t, :], 1.0, 0.0, ALU.mult, ALU.add, ms1[:, t:t + 1]))
            mean(ms1[:, :], D).then_inc(S["ms1_ready"], 1)
            dve.wait_ge(S["rs1_ready"], 1)
            for t in range(TILES):
                dve.tensor_scalar(front[:, 3584 + t * D:3584 + (t + 1) * D], h_sb[:, t, :], rs1[:, t:t + 1], None, ALU.mult
                                  ).then_inc(S["xscaled"], 1)
            dve.wait_ge(g1_in, 16)
            dve.wait_ge(S["xT_mm"], 1)
            for i in range(DC // 2):
                dve.tensor_tensor(xT[:, 2 * i:2 * i + 2, :], bank[i][:, :].rearrange("p (c t) -> p c t", c=2),
                                  bc(g1_col[:, 2 * i:2 * i + 2].unsqueeze(2), [P, 2, SEQ]), ALU.mult
                                  ).then_inc(S["xT_ready"], 1)
            dve.wait_ge(S["small_mm"], 1)
            dve.tensor_copy(relT[:, :], bank[4][0:HEADS, 64:64 + BUCKETS]).then_inc(S["relT_ready"], 1)
            dve.tensor_copy(conv_cols[:, :, :], bank[4][:, 0:CONV_BLOCKS * 8].rearrange("p (b k) -> p b k", b=CONV_BLOCKS)
                            [:, :, 0:TAPS + 1]).then_inc(S["small_ready"], 1)
            dve.tensor_tensor(qkg_col[:, :], qg_col[:, :], kg_col[:, :], ALU.mult).then_inc(S["qkg_ready"], 1)
            dve.wait_ge(S["small_ready"], 1)
            def convolve(b):
                if b % 2 == 0:
                    dve.wait_ge(S["raw_ready"], b // 2 + 1)
                link(dve.tensor_scalar(conv[:, b, :], raw[:, b, 0:SEQ], conv_cols[:, b, 0:1], conv_cols[:, b, TAPS:TAPS + 1],
                                       ALU.mult, ALU.add))
                for k in range(1, TAPS):
                    ins = dve.scalar_tensor_tensor(conv[:, b, :], raw[:, b, k:k + SEQ], conv_cols[:, b, k:k + 1], conv[:, b, :],
                                                   ALU.mult, ALU.add)
                    if k < TAPS - 1:
                        link(ins)
                    else:
                        ins.then_inc(S["conv_ready"], 1)

            for b in range(CONV_BLOCKS):
                convolve(b)
            dve.wait_ge(S["dt_mm"], 1)
            link(dve.tensor_tensor(dt_lin[:, :, :], bank[4][:, 0:TILES * HEADS].rearrange("p (t h) -> p t h", t=TILES),
                                   bc(dtb_bc[:, :].unsqueeze(1), [P, TILES, HEADS]), ALU.add))
            dve.scalar_tensor_tensor(dt_abs[:, :, :], dt_lin[:, :, :], -1.0, dt_lin[:, :, :], ALU.mult, ALU.max
                                     ).then_inc(S["dtabs_ready"], 1)
            dve.wait_ge(S["dtlog_ready"], 1)
            link(dve.scalar_tensor_tensor(dt_sb[:, :, :], dt_lin[:, :, :], 0.0, dt_log[:, :, :], ALU.max, ALU.add))
            dve.scalar_tensor_tensor(a_dt[:, :, :], dt_sb[:, :, :], -1.0, bc(a_exp[:, :].unsqueeze(1), [P, TILES, HEADS]),
                                     ALU.mult, ALU.mult).then_inc(S["adt_ready"], 1)
            for w in range(2):
                for t in range(TILES):
                    dve.wait_ge(S["squares_ready"], 2 * w + t + 1)
                    ins = dve.tensor_reduce(msqk[:, w, t * HEADS:(t + 1) * HEADS],
                                            squares[:, w, t, :].rearrange("p (h d) -> p h d", h=HEADS), AX.X, ALU.add)
                    link(ins)
                mean(msqk[:, w, :], HD).then_inc(S["msqk_ready"], 1)
                if w == 0:
                    dve.wait_ge(S["acs_mm"], 1)
                    dve.tensor_copy(a_cs[:, :, :], bank[4][:, 0:TILES * HEADS].rearrange("p (t h) -> p t h", t=TILES)
                                    ).then_inc(S["acs_ready"], 1)
            for w in range(2):
                dve.wait_ge(S["rsqk_ready"], w + 1)
                for t in range(TILES):
                    dve.tensor_tensor(qk_tok[:, w, t, :].rearrange("p (h d) -> p h d", h=HEADS),
                                      bank[2 * w + t][:, :].rearrange("p (h d) -> p h d", h=HEADS),
                                      bc(rsqk[:, w, t * HEADS:(t + 1) * HEADS].unsqueeze(2), [P, HEADS, HD]), ALU.mult
                                      ).then_inc(S["qk_ready"], 1)
            dve.wait_ge(biasline_out, 16)
            for t in range(TILES):
                dve.wait_ge(S["xs_mm"], t + 1)
                xs_ps = (bank[7] if t == 0 else bank[5])[:, :].rearrange("p (h d) -> p h d", h=HEADS)
                for dst, by in ((xdt, dt_sb[:, t, :]), (y_ssd, dskip_bc[:, :])):
                    dve.tensor_tensor(dst[:, t, :].rearrange("p (h d) -> p h d", h=HEADS), xs_ps,
                                      bc(by.unsqueeze(2), [P, HEADS, HD]), ALU.mult).then_inc(S["xdt_ready"], 1)
            dve.wait_ge(S["cb_mm"], 1)
            dve.tensor_copy(b_tok[:, :], bank[4][:, P:2 * P]).then_inc(S["btok_ready"], 1)
            for g in range(GROUPS):
                dve.tensor_tensor(cb_sb[:, :, g, :], bank[6 - 2 * g][:, 2 * P:].rearrange("p (t l) -> p t l", t=TILES),
                                  bc(upto[:, :].unsqueeze(1), [P, TILES, P]), ALU.mult).then_inc(S["cb_ready"], 1)
            dve.wait_ge(S["qkg_ready"], 1)
            dve.wait_ge(S["qkT_mm"], 1)
            for i in range(2):
                dve.tensor_scalar(qkT[:, 0, 2 * i:2 * i + 2, :], bank[4 + i][:, :].rearrange("p (b t) -> p b t", b=2),
                                  qkg_col[:, 0:1], HD ** -0.5, ALU.mult, ALU.mult).then_inc(S["qT_ready"], 1)
            dve.wait_ge(S["qkT_mm"], 2)
            for i in range(2):
                dve.tensor_copy(qkT[:, 1, 2 * i:2 * i + 2, :], bank[6 + i][:, :].rearrange("p (b t) -> p b t", b=2)
                                ).then_inc(S["kT_ready"], 1)
            for t in range(TILES):
                dve.wait_ge(S["rowcs_mm"], t + 1)
                for h in range(HEADS):
                    dve.tensor_scalar(decay_mat[:, t, h, :], bank[2 * t + h // 4][:, (h % 4) * P:(h % 4 + 1) * P],
                                      a_cs[:, t, h:h + 1], 0.0, ALU.subtract, ALU.min).then_inc(S["decay_lin"], 1)
                if t == 0:
                    for g in range(GROUPS):
                        ins = dve.tensor_tensor(decay_arg[:, g * HPG:(g + 1) * HPG],
                                                bank[g][:, :].rearrange("p (h l) -> p h l", h=HPG)[:, :, P - 1],
                                                a_cs[:, 0, g * HPG:(g + 1) * HPG], ALU.subtract)
                        if g:
                            ins.then_inc(S["dend_lin"], 1)

            def bias_and_max(h):
                dve.wait_ge(S["score_mm"], h + 1)
                if h == 0:
                    dve.wait_ge(biastab_in, 16)
                if h >= 4:
                    dve.wait_ge(S["probT_mm"], h - 3)
                dve.tensor_tensor_reduce(prob[:, h % 4, 0:SEQ], bank[4 + h % 2][:, 0:SEQ], bias_tab[:, h, :], 1.0, LOW,
                                         ALU.add, ALU.max, row_max[:, h, 1:2])
                link(dve.tensor_tensor_reduce(prob[:, h % 4, SEQ:SEQ + P], bank[4 + h % 2][:, SEQ:SEQ + P],
                                              bias_tab[:, h, P:SEQ], 1.0, LOW, ALU.add, ALU.max, row_max[:, h, 0:1]))
                dve.tensor_scalar(neg_max[:, h, :], row_max[:, h, :], -1.0, None, ALU.mult).then_inc(S["negmax_ready"], 1)
                dve.nop().then_inc(S["score_ready"], 1)

            def mix(t, g):
                dve.wait_ge(S["decay_exp"], t * GROUPS + g + 1)
                block4 = decay_mat[:, t, g * HPG:(g + 1) * HPG, :]
                dve.tensor_tensor(block4, block4, bc(cb_sb[:, t, g, :].unsqueeze(1), [P, HPG, P]), ALU.mult
                                  ).then_inc(S["mix_ready"], 1)

            for h in range(HEADS):
                bias_and_max(h)
                if h % 2 == 1:
                    mix((h // 2) // GROUPS, (h // 2) % GROUPS)
            dve.wait_ge(S["prob_ready"], HEADS)
            link(dve.reciprocal(row_inv[:, :, :], row_sum[:, :, :]))
            dve.wait_ge(S["pv_mm"], HEADS)
            dve.wait_ge(S["z_mm"], 1)
            for t in range(TILES):
                dve.tensor_tensor(y_att[:, t, :].rearrange("p (h d) -> p h d", h=HEADS),
                                  bank[2 + t][:, :].rearrange("p (h d) -> p h d", h=HEADS),
                                  bc(row_inv[:, :, t].unsqueeze(2), [P, HEADS, HD]), ALU.mult).then_inc(S["yatt_ready"], 1)
            dve.wait_ge(S["ydiag_mm"], 1)
            link(dve.tensor_tensor(y_ssd[:, 0, :], bank[4][:, :], y_ssd[:, 0, :], ALU.add))
            dve.wait_ge(S["dend_exp"], 1)
            dve.tensor_tensor(xdt[:, 0, :].rearrange("p (h d) -> p h d", h=HEADS),
                              xdt[:, 0, :].rearrange("p (h d) -> p h d", h=HEADS),
                              bc(decay_end[:, :].unsqueeze(2), [P, HEADS, HD]), ALU.mult).then_inc(S["xdec_ready"], 1)

            def gated(t):
                dve.wait_ge(S["zsilu_ready"], t + 1)
                link(dve.tensor_tensor(y_ssd[:, t, :], y_ssd[:, t, :], z_silu[:, t, :], ALU.mult))
                link(dve.tensor_tensor_reduce(work[:, 2560:3072], y_ssd[:, t, :], y_ssd[:, t, :], 1.0, 0.0, ALU.mult, ALU.add,
                                              ms3[:, t:t + 1]))
                mean(ms3[:, t:t + 1], INNER).then_inc(S["ms3_ready"], 1)

            def normed(t):
                dve.wait_ge(late_in, 16 * 6)
                dve.wait_ge(S["rs3_ready"], t + 1)
                dve.scalar_tensor_tensor(y_ssd[:, t, :], y_ssd[:, t, :], rs3[:, t:t + 1], ssdg_bc[:, :], ALU.mult, ALU.mult
                                         ).then_inc(S["yssd_ready"], 1)

            dve.wait_ge(S["state_mm"], 1)
            for g in range(GROUPS):
                rows = slice(g * STATE, (g + 1) * STATE)
                dve.tensor_copy(state_sb[rows, :], bank[6][rows, g * HPG * HD:(g + 1) * HPG * HD]
                                ).then_inc(S["state_ready"], 1)
            gated(0)
            dve.wait_ge(S["ydiag_mm"], 2)
            dve.tensor_tensor(y_ssd[:, 1, :], bank[5][:, :], y_ssd[:, 1, :], ALU.add)
            dve.wait_ge(S["yoff_mm"], 1)
            for g in range(GROUPS):
                cols, hs = slice(g * HPG * HD, (g + 1) * HPG * HD), slice(g * HPG, (g + 1) * HPG)
                link(dve.tensor_tensor(y_off[:, cols].rearrange("p (h d) -> p h d", h=HPG),
                                       bank[7 - g][:, cols].rearrange("p (h d) -> p h d", h=HPG),
                                       bc(decay_in[:, hs].unsqueeze(2), [P, HPG, HD]), ALU.mult))
            link(dve.tensor_tensor(y_ssd[:, 1, :], y_ssd[:, 1, :], y_off, ALU.add))
            normed(0)
            gated(1)
            normed(1)
            dve.tensor_copy(wr_sb[:, :, 0:MOE_GROUPS], wr1_sb[:, :, :]).then_inc(S["wr_ready"], 1)
            dve.tensor_copy(wr_sb[:, :, MOE_GROUPS:ROUTES], wr2_sb[:, :, :]).then_inc(S["wr_ready"], 1)
            for t in range(TILES):
                for n in range(2):
                    dve.wait_ge(S["wout_mm"], 2 * t + n + 1)
                    cols = slice(n * HALF, (n + 1) * HALF)
                    dve.tensor_tensor(h_sb[:, t, cols], bank[(0, 1, 4, 5)[2 * t + n]][:, :], h_sb[:, t, cols], ALU.add
                                      ).then_inc(S["h_ready"], 1)
                dve.wait_ge(S["ms2_act"], t + 1)
                mean(ms2[:, t:t + 1], D).then_inc(S["ms2_ready"], 1)
                dve.wait_ge(S["rs2_ready"], t + 1)
                dve.scalar_tensor_tensor(xn[:, t, :, :].rearrange("p c q -> p q c"),
                                         h_sb[:, t, :].rearrange("p (q c) -> p q c", c=DC), rs2[:, t:t + 1],
                                         g2_bc[:, :].rearrange("p (q c) -> p q c", c=DC), ALU.mult, ALU.mult
                                         ).then_inc(S["xn_ready"], 1)
                dve.wait_ge(S["xnT_mm"], t + 1)
                for i in (2, 3):
                    dve.tensor_copy(xnT[:, 2 * i:2 * i + 2, t * P:(t + 1) * P],
                                    bank[(2, 3, 6, 7)[i]][:, :].rearrange("p (c t) -> p c t", c=2)[:, :, t * P:(t + 1) * P]
                                    ).then_inc(S["xnT_ready"], 1)
                dve.wait_ge(S["part0"], t + 1)
                dve.tensor_tensor(work[:, t * D:(t + 1) * D], work[:, t * D:(t + 1) * D], xn_part(0, t), ALU.subtract
                                  ).then_inc(S["part0_taken"], 1)
            link(dve.memset(rank[:, :, :], 0.0))

            dve.wait_ge(S["logit_mm"], 1)
            link(dve.tensor_tensor(logit[:, :, :], bank[0][:, 0:TILES * ROUTES].rearrange("p (t n) -> p t n", t=TILES),
                                   bc(br_bc[:, :].unsqueeze(1), [P, TILES, ROUTES]), ALU.add))
            l1, l2 = logit[:, :, 0:MOE_GROUPS], logit[:, :, MOE_GROUPS:ROUTES]

            def first_highest(hot, eq, values, high, n):
                link(dve.tensor_reduce(high, values, AX.X, ALU.max))
                link(dve.tensor_tensor(eq, values, bc(high.unsqueeze(2), [P, TILES, n]), ALU.is_equal))
                link(dve.scalar_tensor_tensor(eq, eq, -float(P), bc(expert_iota[:, 0:n].unsqueeze(1), [P, TILES, n]),
                                              ALU.mult, ALU.add))
                link(dve.tensor_reduce(low_at[:, :], eq, AX.X, ALU.min))
                link(dve.tensor_tensor(hot, eq, bc(low_at[:, :].unsqueeze(2), [P, TILES, n]), ALU.is_equal))

            first_highest(ghot[:, :, :], eq4[:, :, :], l1, top[:, 0, :], MOE_GROUPS)
            dve.tensor_tensor(gexp[:, :, :], l1, bc(top[:, 0, :].unsqueeze(2), [P, TILES, MOE_GROUPS]), ALU.subtract
                              ).then_inc(S["gexp_in"], 1)
            link(dve.tensor_scalar(ghot[:, :, :], ghot[:, :, :], -LOW, LOW, ALU.mult, ALU.add))
            link(dve.tensor_tensor(masked[:, :, :].rearrange("p t (g k) -> p t g k", g=MOE_GROUPS),
                                   l2.rearrange("p t (g k) -> p t g k", g=MOE_GROUPS),
                                   bc(ghot[:, :, :].unsqueeze(3), [P, TILES, MOE_GROUPS, PER_GROUP]), ALU.add))
            first_highest(hot1[:, :, :], eq32[:, :, :], masked[:, :, :], top[:, 1, :], EXPERTS)
            link(dve.scalar_tensor_tensor(masked[:, :, :], hot1[:, :, :], 2 * LOW, masked[:, :, :], ALU.mult, ALU.add))
            first_highest(hot2[:, :, :], eq32[:, :, :], masked[:, :, :], top[:, 2, :], EXPERTS)
            dve.tensor_tensor(share[:, 0, :], top[:, 2, :], top[:, 1, :], ALU.subtract).then_inc(S["share_in"], 1)
            dve.tensor_tensor(chosen[:, :, :], hot1[:, :, :], hot2[:, :, :], ALU.add).then_inc(S["chosen_ready"], 1)
            dve.wait_ge(S["rank_mm"], 1)
            rank_ps = bank[1][:, 0:TILES * EXPERTS].rearrange("p (t n) -> p t n", t=TILES)
            link(dve.scalar_tensor_tensor(rank[:, :, 0:EXPERTS], rank_ps, 1.0, chosen[:, :, :], ALU.add, ALU.mult))
            link(dve.tensor_scalar(rank[:, :, :], rank[:, :, :], 1.0, None, ALU.subtract))

            def select(e, done):
                for t in range(TILES):
                    ins = dve.tensor_scalar(sel[:, t, :], rank_iota[:, 0:CAP], rank[:, t, bass.ds(e, 1)], None, ALU.is_equal)
                ins.then_inc(done, 1)

            def select_gated(e, parity):
                for t in range(TILES):
                    ins = dve.tensor_scalar(gsel[:, t, parity, :], rank_iota[:, 0:CAP], rank[:, t, bass.ds(e, 1)],
                                            gates[:, t, bass.ds(e, 1)], ALU.is_equal, ALU.mult)
                return ins

            def low_part(u, s):
                return dve.tensor_tensor(w_split[:, u % BUFS, 1, :], (wg_sb, wu_sb)[u // DC][s][:, u % DC, :],
                                         w_split[:, u % BUFS, 0, :].bitcast(F32), ALU.subtract)

            xe_ps = bank[0][:, :].rearrange("p (c k) -> p c k", c=DC)

            def low_tokens(parity):
                return dve.tensor_tensor(xe_split[:, parity, :, CAP:P], xe_ps,
                                         xe_split[:, parity, :, 0:CAP].bitcast(F32), ALU.subtract)

            def gate_sum():
                return dve.tensor_tensor(silu_sb, bank[0][0:CAP, :], low_sb, ALU.add)

            def up_sum(steps_sem, done):
                dve.tensor_tensor(hid_sb, bank[1][0:CAP, :], low_sb, ALU.add).then_inc(steps_sem[0], 1)
                dve.wait_ge(*steps_sem)
                dve.tensor_tensor(hid_sb, hid_sb, silu_sb, ALU.mult).then_inc(done, 1)

            def keep_y1(e, parity):
                dve.wait_ge(S["y_mm"], e + 1)
                rows = slice(parity * CAP, (parity + 1) * CAP)
                dve.tensor_copy(y_sb[rows, HALF:D], bank[3][rows, :]).then_inc(S["y1_ready"], 1)

            def low_weights(e, s, u):
                dve.wait_ge(S["whi_ready"], e * UNITS + (u + 1))
                low_part(u, s).then_inc(S["wlo_ready"], 1)

            def hidden(e, first):
                dve.wait_ge(S["ulow_ready"], e + 1)
                dve.wait_ge(S["silu_ready"], e + 1)
                if not first:
                    dve.wait_ge(S["hidT_mm"], e)
                up_sum((S["usum_ready"], e + 1), S["hid_ready"])

            def expert(e, s, parity, first, second):
                for u in range(UNITS):
                    if not (first and u < BUFS):
                        low_weights(e, s, u)
                    if u == 2 and not first:
                        hidden(e - 1, second)
                    if u == 5 and not (first or second):
                        keep_y1(e - 2, parity)
                    if u == 9:
                        if second:
                            work_out_gates()
                        if parity:
                            if not second:
                                dve.wait_ge(S["hidT_mm"], e)
                            select_gated(e - 1, 0)
                            select_gated(e, 1)
                    if u == GATE_DONE:
                        dve.wait_ge(S["glow_ready"], e + 1)
                        gate_sum().then_inc(S["gsum_ready"], 1)
                dve.wait_ge(S["xh_ready"], e + 2)
                low_tokens(1 - parity).then_inc(S["xe_ready"], 1)
                select(e + 2, S["sel_ready"])

            def work_out_gates():
                dve.wait_ge(S["gexp_ready"], 1)
                link(dve.tensor_reduce(gsum[:, :], gexp[:, :, :], AX.X, ALU.add))
                dve.wait_ge(S["share_ready"], 1)
                link(dve.scalar_tensor_tensor(share[:, 1, :], share[:, 0, :], 1.0, gsum[:, :], ALU.add, ALU.mult))
                link(dve.reciprocal(share[:, 2, :], share[:, 1, :]))
                link(dve.tensor_tensor(share[:, 3, :], share[:, 2, :], share[:, 0, :], ALU.mult))
                link(dve.tensor_tensor(hot1[:, :, :], hot1[:, :, :], bc(share[:, 2, :].unsqueeze(2), [P, TILES, EXPERTS]), ALU.mult))
                link(dve.tensor_tensor(hot2[:, :, :], hot2[:, :, :], bc(share[:, 3, :].unsqueeze(2), [P, TILES, EXPERTS]), ALU.mult))
                link(dve.tensor_tensor(gates[:, :, :], hot1[:, :, :], hot2[:, :, :], ALU.add))

            select(0, S["sel_ready"])
            link(dve.tensor_reduce(most[0:1, :], bank[1][0:1, 2 * EXPERTS:3 * EXPERTS], AX.X, ALU.max))
            dve.tensor_copy(most_int[0:1, :], most[0:1, :]).then_inc(S["most_ready"], 1)
            for u in range(BUFS):
                low_weights(0, 0, u)
            dve.wait_ge(S["xh_ready"], 1)
            low_tokens(0).then_inc(S["xe_ready"], 1)
            select(1, S["sel_ready"])
            expert(0, 0, 0, True, False)
            expert(1, 1, 1, False, True)
            with dve.Fori(0, EXPERTS // BODY) as i:
                for j in range(BODY):
                    k = PEELED + j
                    expert(i * BODY + k, k % SLOTS, k % 2, False, False)
            hidden(EXPERTS - 1, False)
            keep_y1(EXPERTS - 2, 0)
            keep_y1(EXPERTS - 1, 1)

            dve.wait_ge(S["most_ready"], 1)
            most_tokens = dve.value_load(most_int[0:1, 0:1], min_val=0, max_val=SEQ)
            with dve.If(most_tokens > CAP):
                dve.wait_ge(S["scat_mm"], EXPERTS // 2)
                dve.memset(y_sb[CAP:P, :], 0.0)
                for t in range(TILES):
                    dve.memset(gsel[:, t, 1, :], 0.0)
                dve.nop().then_inc(S["o_turn"], 1)
                with dve.Fori(0, ROUNDS - 1) as r:
                    dve.tensor_scalar(rank[:, :, :], rank[:, :, :], float(CAP), None, ALU.subtract).then_inc(S["o_rank"], 1)
                    with dve.Fori(0, EXPERTS) as e:
                        n = r * EXPERTS + e
                        m = n + EXPERTS
                        dve.wait_ge(S["o_rank"], r + 1)
                        select_gated(e, 0)
                        select(e, S["o_sel"])
                        dve.wait_ge(S["o_xh"], n + 1)
                        low_tokens(0).then_inc(S["o_xs"], 1)
                        for u in range(UNITS):
                            dve.wait_ge(S["whi_ready"], m * UNITS + (u + 1))
                            low_part(u, 0).then_inc(S["wlo_ready"], 1)
                            if u == GATE_DONE:
                                dve.wait_ge(S["glow_ready"], m + 1)
                                gate_sum().then_inc(S["gsum_ready"], 1)
                        dve.wait_ge(S["ulow_ready"], m + 1)
                        dve.wait_ge(S["silu_ready"], m + 1)
                        up_sum((S["usum_ready"], m + 1), S["hid_ready"])
                        dve.wait_ge(S["y_mm"], m + 1)
                        dve.tensor_copy(y_sb[0:CAP, HALF:D], bank[3][0:CAP, :]).then_inc(S["y1_ready"], 1)
                        dve.wait_ge(S["o_scat"], n + 1)
                        dve.nop().then_inc(S["o_turn"], 1)
            dve.nop()

            dve.wait_ge(S["moe_done"], 1)
            for t in range(TILES):
                for n in range(2):
                    cols = slice(n * HALF, (n + 1) * HALF)
                    dve.tensor_tensor(h_sb[:, t, cols], bank[4 + 2 * t + n][:, :], h_sb[:, t, cols], ALU.add
                                      ).then_inc(S["result_ready"], 1)


_INS = ["x", "rel_bias", "norm1_g", "w_in", "conv_w", "conv_b", "dt_bias", "a_log", "d_skip", "ssd_norm_g",
        "q_norm_g", "k_norm_g", "w_out", "norm2_g", "w_r1", "b_r1", "w_r2", "b_r2", "w_gate", "w_up", "w_down"]


def kernel(**inputs):
    import numpy as _np
    import concourse.bacc as _bacc
    from concourse import mybir as _mybir
    from concourse.bass_utils import run_bass_kernel_spmd as _run

    nc = _bacc.Bacc("TRN2", target_bir_lowering=False, num_devices=1, dynamic_dma_scratch_size=1024)
    arrays, args = {}, []
    for name in _INS:
        a = _np.ascontiguousarray(inputs[name])
        arrays[f"in_{name}_dram"] = a
        args.append(nc.dram_tensor(f"in_{name}_dram", a.shape, _mybir.dt.from_np(a.dtype), kind="ExternalInput").ap())
    args.append(nc.dram_tensor("bias_rows", (P, HEADS, SEQ + P), F32, kind="Internal").ap())
    args.append(nc.dram_tensor("out_0_dram", (1, SEQ, D), F32, kind="ExternalOutput").ap())
    hymba_layer(nc, *args)
    r = _run(nc, [arrays], core_ids=[0])
    return r.results[0]["out_0_dram"]
```
